# Optimizing a Trainium2 kernel written in Bass

```python
import math
import jax, jax.numpy as jnp
from jax import lax
import numpy as np

D_MODEL = 1024
BATCH = 1
SEQ = 256
DEPTH = 1

HEAD_DIM = 64
BLK = 128
A_GROUPS = ((128, 1), (512, 4), (2048, 16))
A_HEADS = 4
B_Q_HEADS = 8
B_KV_HEADS = 2
B_WINDOW = 128
C_HEADS = 4
N_BRANCH = 3
NUM_BUCKETS = 32
MAX_DISTANCE = max(w for w, _ in A_GROUPS)
D_FF = 4 * D_MODEL
CONV_WIDTH = 3
EPS = 1e-6

A_WIDTH = A_HEADS * HEAD_DIM
B_WIDTH = B_Q_HEADS * HEAD_DIM
C_WIDTH = C_HEADS * HEAD_DIM
B_GROUP = B_Q_HEADS // B_KV_HEADS
N_A_GROUP_HEADS = len(A_GROUPS) * A_HEADS
N_BIAS_HEADS = N_A_GROUP_HEADS + B_Q_HEADS
A_QKV_COLS = 3 * N_A_GROUP_HEADS * HEAD_DIM
B_Q_COLS = B_WIDTH
B_KV_COLS = 2 * B_KV_HEADS * HEAD_DIM
C_QKV_COLS = 3 * C_WIDTH
GATE_COLS = N_BRANCH * D_MODEL
OFF_B_Q = A_QKV_COLS
OFF_B_KV = OFF_B_Q + B_Q_COLS
OFF_C = OFF_B_KV + B_KV_COLS
OFF_GATE = OFF_C + C_QKV_COLS
IN_COLS = OFF_GATE + GATE_COLS
SCALE = HEAD_DIM ** -0.5


def rms_norm(x, g):
    xf = x.astype(jnp.float32)
    y = xf * lax.rsqrt(jnp.mean(xf * xf, axis=-1, keepdims=True) + EPS)
    return (y * g.astype(jnp.float32)).astype(x.dtype)

def t5_bucket(dist):
    max_exact = NUM_BUCKETS // 2
    nf = jnp.maximum(dist, 1).astype(jnp.float32)
    large = max_exact + (jnp.log(nf / max_exact) / math.log(MAX_DISTANCE / max_exact)
                         * (NUM_BUCKETS - max_exact)).astype(jnp.int32)
    large = jnp.minimum(large, NUM_BUCKETS - 1)
    return jnp.where(dist < max_exact, dist, large)

def band_layout(n_blocks, max_dist):
    a = jnp.arange(BLK)[:, None]
    b = jnp.arange(2 * BLK)[None, :]
    dist = a + BLK - b
    in_band = (dist >= 0) & (dist <= max_dist)
    key_exists = (jnp.arange(n_blocks)[:, None] > 0) | (jnp.arange(2 * BLK)[None, :] >= BLK)
    mask = in_band[None] & key_exists[:, None, :]
    return jnp.maximum(dist, 0), mask

def band_bias(table, dist):
    return jnp.transpose(table[t5_bucket(dist)], (2, 0, 1)).astype(jnp.float32)

def banded_attention(q, k, v, bias, mask):
    n, hkv, g, L, dh = q.shape
    nb = L // BLK
    qb = q.reshape(n, hkv, g, nb, BLK, dh)

    def two_blocks(t):
        tb = t.reshape(n, hkv, nb, BLK, dh)
        prev = jnp.pad(tb, ((0, 0), (0, 0), (1, 0), (0, 0), (0, 0)))[:, :, :nb]
        return jnp.concatenate([prev, tb], axis=3)

    kw, vw = two_blocks(k), two_blocks(v)
    logits = jnp.einsum('nkgbqd,nkbsd->nkgbqs', qb, kw, preferred_element_type=jnp.float32) * SCALE
    logits = jnp.where(mask, logits + bias[:, :, None], -jnp.inf)
    m = jnp.max(logits, axis=-1)
    p = jnp.exp(logits - m[..., None])
    l = jnp.sum(p, axis=-1)
    num = jnp.einsum('nkgbqs,nkbsd->nkgbqd', p, vw.astype(jnp.float32))
    return num.reshape(n, hkv, g, L, dh), m.reshape(n, hkv, g, L), l.reshape(n, hkv, g, L)

def to_sub(t, d, lp):
    b, s, h, dh = t.shape
    L = s // d
    t = t.reshape(b, L, d, h, dh).transpose(0, 2, 3, 1, 4).reshape(b * d, h, L, dh)
    return jnp.pad(t, ((0, 0), (0, 0), (0, lp - L), (0, 0)))

def dilated_attention(q, k, v, table_a):
    b, s = q.shape[:2]
    nums, ms, ls = [], [], []
    for gi, (window, d) in enumerate(A_GROUPS):
        L = s // d
        lp = -(-L // BLK) * BLK
        dist, mask = band_layout(lp // BLK, window // d)
        bias = band_bias(table_a[:, gi], dist * d)[:, None]
        num, m, l = banded_attention(to_sub(q[:, :, gi], d, lp)[:, :, None],
                                     to_sub(k[:, :, gi], d, lp), to_sub(v[:, :, gi], d, lp), bias, mask)
        num = num[:, :, 0, :L].reshape(b, d, A_HEADS, L, HEAD_DIM).transpose(0, 3, 1, 2, 4)
        nums.append(num.reshape(b, s, A_HEADS, HEAD_DIM))
        ms.append(m[:, :, 0, :L].reshape(b, d, A_HEADS, L).transpose(0, 3, 1, 2).reshape(b, s, A_HEADS))
        ls.append(l[:, :, 0, :L].reshape(b, d, A_HEADS, L).transpose(0, 3, 1, 2).reshape(b, s, A_HEADS))
    nums = jnp.stack(nums, axis=2)
    ms = jnp.stack(ms, axis=2)
    ls = jnp.stack(ls, axis=2)
    c = jnp.exp(ms - jnp.max(ms, axis=2, keepdims=True))
    out = jnp.sum(c[..., None] * nums, axis=2) / jnp.sum(c * ls, axis=2)[..., None]
    return out.reshape(b, s, A_WIDTH).astype(q.dtype)

def sliding_window_gqa(q, k, v, sinks, table_b):
    b, s = q.shape[:2]
    dist, mask = band_layout(s // BLK, B_WINDOW - 1)
    bias = band_bias(table_b, dist).reshape(B_KV_HEADS, B_GROUP, BLK, 2 * BLK)
    qh = q.reshape(b, s, B_KV_HEADS, B_GROUP, HEAD_DIM).transpose(0, 2, 3, 1, 4)
    num, m, l = banded_attention(qh, k.transpose(0, 2, 1, 3), v.transpose(0, 2, 1, 3), bias, mask)
    sink = sinks.reshape(B_KV_HEADS, B_GROUP)[None, :, :, None].astype(jnp.float32)
    mx = jnp.maximum(m, sink)
    c = jnp.exp(m - mx)
    out = num * (c / (l * c + jnp.exp(sink - mx)))[..., None]
    return out.transpose(0, 3, 1, 2, 4).reshape(b, s, B_WIDTH).astype(q.dtype)

def stick_breaking_attention(q, k, v):
    b, s = q.shape[:2]
    qh, kh, vh = (t.transpose(0, 2, 1, 3) for t in (q, k, v))
    outs = []
    for i in range(s // BLK):
        lo, hi = i * BLK, (i + 1) * BLK
        z = jnp.einsum('bhqd,bhsd->bhqs', qh[:, :, lo:hi], kh[:, :, :hi],
                       preferred_element_type=jnp.float32) * SCALE
        before = jnp.arange(hi)[None, :] < jnp.arange(lo, hi)[:, None]
        log_keep = jnp.where(before, jax.nn.log_sigmoid(-z), 0.0)
        log_rest = lax.cumsum(log_keep, axis=3, reverse=True) - log_keep
        wts = jnp.where(before, jnp.exp(jax.nn.log_sigmoid(z) + log_rest), 0.0)
        outs.append(jnp.einsum('bhqs,bhsd->bhqd', wts, vh[:, :, :hi].astype(jnp.float32)))
    out = jnp.concatenate(outs, axis=2).transpose(0, 2, 1, 3)
    return out.reshape(b, s, C_WIDTH).astype(q.dtype)

def hybrid_mixer(h, rel_bias, w_in, b_gate, sinks, w_br_a, w_br_b, w_br_c, w_out):
    b, s, _ = h.shape
    proj = h @ w_in
    a_qkv, b_q, b_kv, c_qkv, gates = jnp.split(proj, [OFF_B_Q, OFF_B_KV, OFF_C, OFF_GATE], axis=-1)
    a_qkv = a_qkv.reshape(b, s, 3, len(A_GROUPS), A_HEADS, HEAD_DIM)
    table_a = rel_bias[:, :N_A_GROUP_HEADS].reshape(NUM_BUCKETS, len(A_GROUPS), A_HEADS)
    o_a = dilated_attention(a_qkv[:, :, 0], a_qkv[:, :, 1], a_qkv[:, :, 2], table_a)
    b_kv = b_kv.reshape(b, s, 2, B_KV_HEADS, HEAD_DIM)
    o_b = sliding_window_gqa(b_q.reshape(b, s, B_Q_HEADS, HEAD_DIM), b_kv[:, :, 0], b_kv[:, :, 1],
                             sinks, rel_bias[:, N_A_GROUP_HEADS:])
    c_qkv = c_qkv.reshape(b, s, 3, C_HEADS, HEAD_DIM)
    o_c = stick_breaking_attention(c_qkv[:, :, 0], c_qkv[:, :, 1], c_qkv[:, :, 2])
    g = jax.nn.sigmoid(gates.reshape(b, s, N_BRANCH, D_MODEL) + b_gate)
    merged = g[:, :, 0] * (o_a @ w_br_a) + g[:, :, 1] * (o_b @ w_br_b) + g[:, :, 2] * (o_c @ w_br_c)
    return merged @ w_out

def conv_ffn(h, w_up, conv_w, conv_b, w_down):
    u = h @ w_up
    u = lax.conv_general_dilated(u, conv_w[:, None, :], window_strides=(1,),
                                 padding=[(CONV_WIDTH - 1, 0)],
                                 dimension_numbers=('NWC', 'WIO', 'NWC'),
                                 feature_group_count=u.shape[-1]) + conv_b
    gate, val = jnp.split(u, 2, axis=-1)
    return (jax.nn.gelu(gate, approximate=True) * val) @ w_down

def first_inputs(seed: int = 0) -> dict:
    key = jax.random.key(seed)
    ks = jax.random.split(key, 17)

    def nrm(k, shape, scale):
        return jax.random.normal(k, shape, jnp.float32) * scale

    def gain(k):
        return 1.0 + nrm(k, (DEPTH, D_MODEL), 0.1)

    return {
        'x': nrm(ks[0], (BATCH, SEQ, D_MODEL), 1.0),
        'rel_bias': nrm(ks[1], (NUM_BUCKETS, N_BIAS_HEADS), 0.5),
        'attn_pre_norm': gain(ks[2]),
        'w_in': nrm(ks[3], (DEPTH, D_MODEL, IN_COLS), D_MODEL ** -0.5),
        'b_gate': nrm(ks[4], (DEPTH, N_BRANCH, D_MODEL), 0.1),
        'sinks': nrm(ks[5], (DEPTH, B_Q_HEADS), 0.5),
        'w_br_a': nrm(ks[6], (DEPTH, A_WIDTH, D_MODEL), A_WIDTH ** -0.5),
        'w_br_b': nrm(ks[7], (DEPTH, B_WIDTH, D_MODEL), B_WIDTH ** -0.5),
        'w_br_c': nrm(ks[8], (DEPTH, C_WIDTH, D_MODEL), C_WIDTH ** -0.5),
        'w_out': nrm(ks[9], (DEPTH, D_MODEL, D_MODEL), D_MODEL ** -0.5),
        'attn_post_norm': gain(ks[10]),
        'ffn_pre_norm': gain(ks[11]),
        'w_up': nrm(ks[12], (DEPTH, D_MODEL, 2 * D_FF), D_MODEL ** -0.5),
        'conv_w': nrm(ks[13], (DEPTH, CONV_WIDTH, 2 * D_FF), CONV_WIDTH ** -0.5),
        'conv_b': nrm(ks[14], (DEPTH, 2 * D_FF), 0.02),
        'w_down': nrm(ks[15], (DEPTH, D_FF, D_MODEL), D_FF ** -0.5),
        'ffn_post_norm': gain(ks[16]),
    }

def first_block(x, rel_bias, attn_pre_norm, w_in, b_gate, sinks, w_br_a, w_br_b, w_br_c, w_out,
              attn_post_norm, ffn_pre_norm, w_up, conv_w, conv_b, w_down, ffn_post_norm):
    for layer in range(DEPTH):
        h = rms_norm(x, attn_pre_norm[layer])
        h = hybrid_mixer(h, rel_bias, w_in[layer], b_gate[layer], sinks[layer],
                         w_br_a[layer], w_br_b[layer], w_br_c[layer], w_out[layer])
        x = x + rms_norm(h, attn_post_norm[layer])
        h = rms_norm(x, ffn_pre_norm[layer])
        h = conv_ffn(h, w_up[layer], conv_w[layer], conv_b[layer], w_down[layer])
        x = x + rms_norm(h, ffn_post_norm[layer])
    return x


DEPTH_2 = 2

NA_HEADS = 8
GQA_Q_HEADS = 8
GQA_KV_HEADS = 2
GRID_W = 64
NA_WIN_ROWS = 8
NA_WIN_COLS = 16
SWA_WINDOW = 128
SWA_BLOCK = 128
ROPE_THETA = 10000.0
PEER_HEADS = 8
PEER_N_KEYS = 128
PEER_N_EXPERTS = PEER_N_KEYS * PEER_N_KEYS
PEER_TOPK = 16
PEER_KEY_DIM = 256
PEER_CHUNK = 128
N_BRANCH_2 = 2

NA_WIDTH = NA_HEADS * HEAD_DIM
GQA_Q_WIDTH = GQA_Q_HEADS * HEAD_DIM
GQA_KV_WIDTH = GQA_KV_HEADS * HEAD_DIM
IN_SPLITS = (NA_WIDTH, 2 * NA_WIDTH, 3 * NA_WIDTH,
             3 * NA_WIDTH + GQA_Q_WIDTH,
             3 * NA_WIDTH + GQA_Q_WIDTH + GQA_KV_WIDTH,
             3 * NA_WIDTH + GQA_Q_WIDTH + 2 * GQA_KV_WIDTH)
IN_COLS_2 = IN_SPLITS[-1] + N_BRANCH_2 * D_MODEL


def rms_norm_2(x, g):
    xf = x.astype(jnp.float32)
    y = xf * lax.rsqrt(jnp.mean(xf * xf, axis=-1, keepdims=True) + EPS)
    return (y * g.astype(jnp.float32)).astype(x.dtype)

def rotary(x, pos):
    half = x.shape[-1] // 2
    inv = ROPE_THETA ** (-jnp.arange(half, dtype=jnp.float32) / half)
    ang = pos.astype(jnp.float32)[:, None] * inv[None, :]
    cos = jnp.cos(ang)[None, :, None, :]
    sin = jnp.sin(ang)[None, :, None, :]
    xf = x.astype(jnp.float32)
    x1, x2 = xf[..., :half], xf[..., half:]
    out = jnp.concatenate([x1 * cos - x2 * sin, x1 * sin + x2 * cos], axis=-1)
    return out.astype(x.dtype)

def neighbourhood_attention(q, k, v, rpb):
    B, S, H, dh = q.shape
    rows = S // GRID_W
    kr = min(NA_WIN_ROWS, rows)
    r = jnp.arange(rows)
    rs = jnp.clip(r - kr // 2, 0, rows - kr)
    key_rows = rs[:, None] + jnp.arange(kr)[None, :]
    c = jnp.arange(GRID_W)
    cs = jnp.clip(c - NA_WIN_COLS // 2, 0, GRID_W - NA_WIN_COLS)
    qg = q.reshape(B, rows, GRID_W, H, dh)
    kg = k.reshape(B, rows, GRID_W, H, dh)[:, key_rows]
    vg = v.reshape(B, rows, GRID_W, H, dh)[:, key_rows]
    s = jnp.einsum('brqhd,brakhd->brhqak', qg, kg).astype(jnp.float32) * (dh ** -0.5)
    dr_idx = key_rows - r[:, None] + (NA_WIN_ROWS - 1)
    dc = c[None, :] - c[:, None]
    dc_idx = jnp.clip(dc + NA_WIN_COLS - 1, 0, 2 * NA_WIN_COLS - 2)
    in_win = (c[None, :] >= cs[:, None]) & (c[None, :] < cs[:, None] + NA_WIN_COLS)
    bias = rpb.astype(jnp.float32)[:, dr_idx[:, None, :, None], dc_idx[None, :, None, :]]
    bias = jnp.where(in_win[:, None, :], jnp.transpose(bias, (1, 0, 2, 3, 4)), -jnp.inf)
    p = jax.nn.softmax(s + bias[None], axis=(-2, -1))
    o = jnp.einsum('brhqak,brakhd->brqhd', p.astype(v.dtype), vg)
    return o.reshape(B, S, H * dh)

def sliding_window_gqa_2(q, k, v, sink):
    B, S, Hq, dh = q.shape
    Hkv = k.shape[2]
    G = Hq // Hkv
    nb = S // SWA_BLOCK
    pad = ((0, 0), (SWA_BLOCK, SWA_BLOCK), (0, 0), (0, 0))
    kp = jnp.pad(k, pad).reshape(B, nb + 2, SWA_BLOCK, Hkv, dh)
    vp = jnp.pad(v, pad).reshape(B, nb + 2, SWA_BLOCK, Hkv, dh)
    kw = jnp.concatenate([kp[:, :-2], kp[:, 1:-1], kp[:, 2:]], axis=2)
    vw = jnp.concatenate([vp[:, :-2], vp[:, 1:-1], vp[:, 2:]], axis=2)
    qb = q.reshape(B, nb, SWA_BLOCK, Hkv, G, dh)
    s = jnp.einsum('bnqkgd,bnckd->bnkgqc', qb, kw).astype(jnp.float32) * (dh ** -0.5)
    blk = jnp.arange(nb)[:, None]
    qpos = blk * SWA_BLOCK + jnp.arange(SWA_BLOCK)[None, :]
    kpos = (blk - 1) * SWA_BLOCK + jnp.arange(3 * SWA_BLOCK)[None, :]
    valid = ((kpos >= 0) & (kpos < S))[:, None, :] & \
        (jnp.abs(qpos[:, :, None] - kpos[:, None, :]) <= SWA_WINDOW)
    s = jnp.where(valid[None, :, None, None], s, -jnp.inf)
    sink_l = jnp.broadcast_to(sink.astype(jnp.float32).reshape(Hkv, G)[None, None, :, :, None, None],
                              s.shape[:-1] + (1,))
    p = jax.nn.softmax(jnp.concatenate([s, sink_l], axis=-1), axis=-1)[..., :-1]
    o = jnp.einsum('bnkgqc,bnckd->bnqkgd', p.astype(v.dtype), vw)
    return o.reshape(B, S, Hq * dh)

def token_mixer(h, w_in, gate_bias, qk_norm, na_rpb, swa_sink, w_branch_na, w_branch_swa, w_out, pos):
    B, S, _ = h.shape
    proj = h @ w_in
    qa, ka, va, qb, kb, vb, gl = jnp.split(proj, IN_SPLITS, axis=-1)
    heads = lambda t, n: t.reshape(B, S, n, HEAD_DIM)
    qa = rms_norm_2(heads(qa, NA_HEADS), qk_norm[0])
    ka = rms_norm_2(heads(ka, NA_HEADS), qk_norm[1])
    va = heads(va, NA_HEADS)
    qb = rotary(rms_norm_2(heads(qb, GQA_Q_HEADS), qk_norm[2]), pos)
    kb = rotary(rms_norm_2(heads(kb, GQA_KV_HEADS), qk_norm[3]), pos)
    vb = heads(vb, GQA_KV_HEADS)
    oa = neighbourhood_attention(qa, ka, va, na_rpb)
    ob = sliding_window_gqa_2(qb, kb, vb, swa_sink)
    gates = jax.nn.sigmoid((gl.reshape(B, S, N_BRANCH_2, D_MODEL) + gate_bias).astype(jnp.float32)).astype(h.dtype)
    merged = gates[:, :, 0] * (oa @ w_branch_na) + gates[:, :, 1] * (ob @ w_branch_swa)
    return merged @ w_out

def peer_ffn(x, w_query, sub_keys, expert_down, expert_up):
    B, S, D = x.shape
    T = B * S
    half = PEER_KEY_DIM // 2

    def chunk(xc):
        q = (xc @ w_query).reshape(PEER_CHUNK, PEER_HEADS, 2, half)
        s = jnp.einsum('thpk,pnk->thpn', q, sub_keys).astype(jnp.float32)
        sv, si = lax.top_k(s, PEER_TOPK)
        cand = (sv[:, :, 0, :, None] + sv[:, :, 1, None, :]).reshape(PEER_CHUNK, PEER_HEADS, PEER_TOPK * PEER_TOPK)
        cidx = (si[:, :, 0, :, None] * PEER_N_KEYS + si[:, :, 1, None, :]).reshape(PEER_CHUNK, PEER_HEADS, PEER_TOPK * PEER_TOPK)
        top_s, sel = lax.top_k(cand, PEER_TOPK)
        eidx = jnp.take_along_axis(cidx, sel, axis=-1)
        g = jax.nn.softmax(top_s, axis=-1)
        u = expert_down[eidx]
        vv = expert_up[eidx]
        act = jax.nn.gelu(jnp.einsum('td,thkd->thk', xc, u).astype(jnp.float32), approximate=False)
        return jnp.einsum('thk,thkd->td', (g * act).astype(x.dtype), vv)

    out = lax.map(chunk, x.reshape(T // PEER_CHUNK, PEER_CHUNK, D))
    return out.reshape(B, S, D)

def second_inputs(seed: int = 0) -> dict:
    key = jax.random.key(seed)
    ks = jax.random.split(key, 16)
    f32 = jnp.float32

    def nrm(k, shape, scale):
        return jax.random.normal(k, shape, f32) * scale

    return {
        "x": nrm(ks[0], (BATCH, SEQ, D_MODEL), 1.0),
        "norm_mix": 1.0 + nrm(ks[1], (DEPTH_2, D_MODEL), 0.02),
        "w_in": nrm(ks[2], (DEPTH_2, D_MODEL, IN_COLS_2), D_MODEL ** -0.5),
        "gate_bias": nrm(ks[3], (DEPTH_2, N_BRANCH_2, D_MODEL), 0.02),
        "qk_norm": 1.0 + nrm(ks[4], (DEPTH_2, 4, HEAD_DIM), 0.02),
        "na_rpb": nrm(ks[5], (DEPTH_2, NA_HEADS, 2 * NA_WIN_ROWS - 1, 2 * NA_WIN_COLS - 1), 0.1),
        "swa_sink": nrm(ks[6], (DEPTH_2, GQA_Q_HEADS), 0.5),
        "w_branch_na": nrm(ks[7], (DEPTH_2, NA_WIDTH, D_MODEL), NA_WIDTH ** -0.5),
        "w_branch_swa": nrm(ks[8], (DEPTH_2, GQA_Q_WIDTH, D_MODEL), GQA_Q_WIDTH ** -0.5),
        "w_out": nrm(ks[9], (DEPTH_2, D_MODEL, D_MODEL), D_MODEL ** -0.5),
        "norm_ffn": 1.0 + nrm(ks[10], (DEPTH_2, D_MODEL), 0.02),
        "peer_query": nrm(ks[11], (DEPTH_2, D_MODEL, PEER_HEADS * PEER_KEY_DIM), D_MODEL ** -0.5),
        "peer_sub_keys": nrm(ks[12], (DEPTH_2, 2, PEER_N_KEYS, PEER_KEY_DIM // 2), (PEER_KEY_DIM // 2) ** -0.5),
        "peer_down": nrm(ks[13], (DEPTH_2, PEER_N_EXPERTS, D_MODEL), D_MODEL ** -0.5),
        "peer_up": nrm(ks[14], (DEPTH_2, PEER_N_EXPERTS, D_MODEL), (PEER_HEADS * PEER_TOPK) ** -0.5),
    }

def second_block(x, norm_mix, w_in, gate_bias, qk_norm, na_rpb, swa_sink, w_branch_na, w_branch_swa,
              w_out, norm_ffn, peer_query, peer_sub_keys, peer_down, peer_up):
    S = x.shape[1]
    pos = jnp.arange(S, dtype=jnp.int32)
    for l in range(DEPTH_2):
        x = x + token_mixer(rms_norm_2(x, norm_mix[l]), w_in[l], gate_bias[l], qk_norm[l], na_rpb[l],
                            swa_sink[l], w_branch_na[l], w_branch_swa[l], w_out[l], pos)
        x = x + peer_ffn(rms_norm_2(x, norm_ffn[l]), peer_query[l], peer_sub_keys[l], peer_down[l], peer_up[l])
    return x


def setup_inputs(seed=0):
    out = dict(first_inputs(seed))
    for name, value in second_inputs(seed + 1).items():
        if name != "x":
            out[name + "_2"] = value
    return out


def reference(
    x, rel_bias, attn_pre_norm, w_in, b_gate, sinks, w_br_a, w_br_b, w_br_c, w_out,
    attn_post_norm, ffn_pre_norm, w_up, conv_w, conv_b, w_down, ffn_post_norm, norm_mix_2,
    w_in_2, gate_bias_2, qk_norm_2, na_rpb_2, swa_sink_2, w_branch_na_2, w_branch_swa_2,
    w_out_2, norm_ffn_2, peer_query_2, peer_sub_keys_2, peer_down_2, peer_up_2,
):
    x = first_block(
        x, rel_bias, attn_pre_norm, w_in, b_gate, sinks, w_br_a, w_br_b, w_br_c, w_out,
        attn_post_norm, ffn_pre_norm, w_up, conv_w, conv_b, w_down, ffn_post_norm,
    )
    return second_block(
        x, norm_mix_2, w_in_2, gate_bias_2, qk_norm_2, na_rpb_2, swa_sink_2, w_branch_na_2,
        w_branch_swa_2, w_out_2, norm_ffn_2, peer_query_2, peer_sub_keys_2, peer_down_2,
        peer_up_2,
    )


_drawn_inputs = setup_inputs


def setup_inputs(seed=0):
    import zlib

    import numpy as np

    out = dict(_drawn_inputs(seed))
    spreads = {}
    factors = {'sinks': 4.972,
     'conv_b': 3.249,
     'norm_mix_2': 8.0,
     'gate_bias_2': 8.0,
     'qk_norm_2': 8.0,
     'na_rpb_2': 6.713,
     'swa_sink_2': 8.0,
     'norm_ffn_2': 8.0}
    for name, (base, spread) in spreads.items():
        noise = np.random.default_rng([zlib.crc32(name.encode()), seed]).standard_normal(out[name].shape)
        drawn = base * np.exp(spread * noise) if base else spread * noise
        out[name] = __import__('jax').numpy.asarray(drawn.astype(out[name].dtype))
    for name, factor in factors.items():
        out[name] = (out[name] * factor).astype(out[name].dtype)
    return out
```

```python
from contextlib import ExitStack, contextmanager

import numpy as np

import concourse.bass as bass
from concourse import mybir

F32 = mybir.dt.float32
BF16 = mybir.dt.bfloat16
U32 = mybir.dt.uint32
ACT = mybir.ActivationFunctionType
ALU = mybir.AluOpType
AX = mybir.AxisListType

P = 128
D = 1024
S = 256
TT = S // P
KC = D // P
HD = 64
SCALE = HD ** -0.5
EPS = 1e-6
NEG = -1e30
LOWEST = -3.0e38

GC = 256
GW = KC * GC
SLOTS = 3
IN_QKV, IN_GATE, BR, WO = 15, 12, 4, 4
FF_BLOCKS = 32
G_GATE = IN_QKV
G_BR = IN_QKV + IN_GATE
G_WO = G_BR + BR
G_FF = G_WO + WO
G_LAYER = G_FF + FF_BLOCKS + FF_BLOCKS // 2
L_PROJ, L_GATE, L_PQ = 9, 8, 8
LG_GATE = L_PROJ
LG_BR = LG_GATE + L_GATE
LG_WO = LG_BR + BR
LG_PQ = LG_WO + WO
L_GROUPS = LG_PQ + L_PQ
LAYERS = 2
GROUPS = G_LAYER + LAYERS * L_GROUPS
assert L_GROUPS % SLOTS == 0 and (G_LAYER - 1 - G_FF - 2) % SLOTS == 0

A_H, A_G, B_H, C_H = 4, 3, 8, 4
VAR = 4
EW = 384
NB_BUCKETS = 32

NQ = 8
QK_HEADS = 3 * NQ + 2
QKW = QK_HEADS * HD
ROWS = 4
GRID_W = 64
RPB_R, RPB_C = 15, 31
RPB_PAD = 2 * GRID_W - 1
NA_KK = 6
PH = 8
NKEY = 128
TOPK = 16
EXPERTS = NKEY * NKEY
PICKS = PH * TOPK
SETS, SET = 4, 2
RING = SETS * SET
GITER = PICKS // RING

C_ID, C_TURN, C_BM, C_NB, C_NA, C_SW, C_COS, C_SIN, C_IOTA, C_END = np.cumsum(
    [0, P, P, S, S, GRID_W, TT * S, TT * 32, TT * 32, TOPK]).tolist()
P_G1, P_G2, P_BG, P_CV, P_SK, P_POST, P_FPOST, P_END = np.cumsum(
    [0, KC, KC, 24, FF_BLOCKS * 8, B_H, D, D]).tolist()
Q_G, Q_BG, Q_SK, Q_QKN, Q_GF, Q_KEYS, Q_END = np.cumsum(
    [0, KC, 16, NQ, QKW, D, 2 * NKEY]).tolist()


def wait_alone(eng, sem, value, passed):
    eng.wait_ge(sem, value)
    eng.sem_inc(passed, 1)


class Chain:

    def __init__(self, eng, sem):
        self.eng, self.sem, self.base, self.n = eng, sem, 0, 0

    def step(self, ins):
        self.n += 1
        return ins.then_inc(self.sem, 1)

    def sync(self):
        self.eng.wait_ge(self.sem, self.base + self.n)

    def link(self, ins):
        self.step(ins)
        self.sync()

    def restart(self):
        self.sync()
        self.eng.drain()
        self.eng.sem_clear(self.sem)
        self.base = self.n = 0

    @contextmanager
    def loop(self, count, per):
        before = self.base + self.n
        with self.eng.Fori(0, count) as i:
            self.base, self.n = i * per + before, 0
            yield i
            assert self.n == per, f"{self.n} steps in a loop's body, {per} stated"
        self.base, self.n = before + count * per, 0


def view(ap, *dims):
    return bass.AP(tensor=ap.tensor, offset=ap.offset, ap=[list(ap.ap[0])] + [list(d) for d in dims])




def build(nc, x_in, wstream, consts, onehot, relb, par1, par2, rpb, experts, out):
    ctx = ExitStack()
    with ctx:
        def sb(name, shape, dt=F32):
            return ctx.enter_context(nc.sbuf_tensor(name, shape, dt))

        def sem(name):
            return ctx.enter_context(nc.semaphore(name))

        X = sb("x", [P, TT, D])
        HN = sb("h_norm", [P, TT, D])
        HT = sb("h_T", [P, KC, S])
        W = sb("weights", [P, SLOTS, GW])
        CONST = sb("consts", [P, C_END])
        PAR = sb("params", [P, max(P_END, Q_END)])
        SMALL = sb("small", [P, 512])
        DIAG = sb("diag", [P, RING, P])
        ZERO = sb("zero", [P, 512], BF16)
        IDXS = sb("idx_stage", [P, RING], U32)
        EIDX = sb("expert_idx", [P, TT, PICKS], U32)
        GWT = sb("expert_gate", [P, TT, PICKS])
        work = sb("work", [P, 20496])
        arena = sb("arena", [P, 12800])
        ps = ctx.enter_context(nc.psum_tensor("ps", [P, 8 * 512], F32))
        na_rows = nc.dram_tensor("na_rows", [LAYERS, P, NQ, NA_KK * GRID_W], F32).ap()
        scratch = nc.dram_tensor("bias_rows", [20, VAR * EW], F32).ap()

        def carve(region, at, *shape):
            n = int(np.prod(shape))
            v = region[:, at:at + n]
            if len(shape) > 1:
                names = "abcd"[:len(shape)]
                v = v.rearrange(f"p ({' '.join(names)}) -> p {' '.join(names)}",
                                **dict(zip(names, shape)))
            return v, at + n

        ident = CONST[:, C_ID:C_ID + P]
        turn = CONST[:, C_TURN:C_TURN + P]
        before = CONST[:, C_BM:C_BM + S]
        not_before = CONST[:, C_NB:C_NB + S]
        iota16 = CONST[:, C_IOTA:C_IOTA + TOPK]

        LG, w0 = carve(work, 0, 2056)
        PT, w0 = carve(work, w0, 16, P)
        O, w0 = carve(work, w0, TT, D)
        OT, w0 = carve(work, w0, KC, S)
        MT, w0 = carve(work, w0, KC, S)
        C2, w0 = carve(work, w0, 2056)
        Y, w0 = carve(work, w0, TT, D)
        GT, w0 = carve(work, w0, 24, S)
        ring = work[:, 0:RING * 2 * D].rearrange("p (r n) -> p r n", r=RING)
        ffacc = work[:, 0:1024].rearrange("p (j g n) -> p j g n", j=2, g=2)
        ffg = work[:, 1024:1536].rearrange("p (j n) -> p j n", j=2)
        aqT, a0 = carve(arena, 0, 6, S)
        akT, a0 = carve(arena, a0, 6, S)
        av, a0 = carve(arena, a0, TT, 768)
        bqT, a0 = carve(arena, a0, 4, S)
        bkT, a0 = carve(arena, a0, S)
        bv, a0 = carve(arena, a0, TT, P)
        cqT, a0 = carve(arena, a0, 2, S)
        ckT, a0 = carve(arena, a0, 2, S)
        cv, a0 = carve(arena, a0, TT, S)
        bias_all = arena[:, a0:a0 + (A_H * A_G + B_H) * S]
        biasA, a0 = carve(arena, a0, A_H, A_G, S)
        biasB, a0 = carve(arena, a0, B_H, S)
        hankA, h0 = carve(work, 8200, A_H, A_G, S)
        hankB, h0 = carve(work, h0, B_H, S)
        hank = work[:, 8200:h0]
        BIAS_FILLS = (h0 - 8200) // 512
        erow, _ = carve(work, 0, VAR * EW)
        ohot, _ = carve(work, 2056, VAR * EW)
        relb_sb, _ = carve(work, 2056 + VAR * EW, 20)
        naB, b0 = carve(arena, 0, NQ, NA_KK * GRID_W)
        QK, b0 = carve(arena, b0, TT, QKW)
        qkT, b0 = carve(arena, b0, QK_HEADS // 2, S)
        va, b0 = carve(arena, b0, TT, NQ * HD)
        vb, b0 = carve(arena, b0, TT, P)
        rot, _ = carve(work, 0, 4, TT * 10 * 32)
        qksq, _ = carve(work, 2560, TT * QKW)
        pqT, c0 = carve(arena, 0, 16, S)
        SC, c0 = carve(arena, c0, TT, 16, NKEY)
        cand, c0 = carve(arena, c0, PH, TOPK * TOPK)
        eqA, e0 = carve(work, RING * 2 * D, PH * TOPK * TOPK)
        eqB, e0 = carve(work, e0, PH * TOPK * TOPK)
        cand2 = eqA[:, 0:TOPK * TOPK]
        s2 = eqB[:, 0:NKEY]
        sv, d0 = carve(DIAG[:, :, :].rearrange("p r n -> p (r n)"), 0, 16, TOPK)
        siF, d0 = carve(DIAG[:, :, :].rearrange("p r n -> p (r n)"), d0, 16, TOPK)
        topv, d0 = carve(DIAG[:, :, :].rearrange("p r n -> p (r n)"), d0, PH, TOPK)
        abF, c0 = carve(arena, c0, 2, PICKS)
        eF, c0 = carve(arena, c0, 2, PICKS)
        si = arena[:, c0:c0 + 16 * TOPK].bitcast(U32).rearrange("p (a k) -> p a k", k=TOPK)
        SEL = arena[:, c0 + 16 * TOPK:c0 + 16 * TOPK + 3 * PICKS].bitcast(U32).rearrange("p (a k) -> p a k", k=PICKS)
        ssq, std, rstd = SMALL[:, 0:2], SMALL[:, 2:4], SMALL[:, 4:6]
        negm, sums, rsum = SMALL[:, 8:16], SMALL[:, 16:24], SMALL[:, 24:32]
        hssq, hrstd = SMALL[:, 32:32 + 52], SMALL[:, 96:96 + 52]
        hd = SMALL[:, 160:160 + RING]
        ga = SMALL[:, 176:176 + RING]
        gw8 = SMALL[:, 192:192 + RING]
        lbase = SMALL[:, 208:209]
        esum, ersum = SMALL[:, 216:224], SMALL[:, 224:232]
        junk = OT.rearrange("p (t a) b -> p t (a b)", t=TT)

        def bank(b, n=1):
            return ps[:, b * 512:(b + n) * 512]

        x_loaded, const_loaded, par1_loaded, bias_in = sem("x_loaded"), sem("const_loaded"), sem("par1_loaded"), sem("bias_in")
        w_landed = [sem(f"w_landed{i}") for i in range(SLOTS)]
        group_done = sem("group_done")
        proj_taken = sem("proj_taken")
        lproj_taken = sem("layer_proj_taken")
        merged = sem("merged")
        ff_taken = sem("ff_taken")
        wo_taken = sem("wo_taken")
        br_taken = sem("branch_taken")
        zeroed = sem("zeroed")
        erow_ready, erow_copied, erow_stored = sem("erow_ready"), sem("erow_copied"), sem("erow_stored")
        bias_loaded = sem("bias_loaded")
        bias_turned, bias_taken = sem("bias_turned"), sem("bias_taken")
        dve_step = sem("dve_step")
        x_ready = sem("x_ready")
        low_scores, llow_scores = sem("low_scores"), sem("layer_low_scores")
        scores_ready, logits_ready, probs_ready = sem("scores_ready"), sem("logits_ready"), sem("probs_ready")
        pT_ready, pT_taken, pv_ready, heads_out = sem("pT_ready"), sem("pT_taken"), sem("pv_ready"), sem("heads_out")
        lscores_ready, llogits_ready, lprobs_ready = sem("layer_scores_ready"), sem("layer_logits_ready"), sem("layer_probs_ready")
        lpT_ready, lpT_taken, lpv_ready, lheads_out = sem("layer_pT_ready"), sem("layer_pT_taken"), sem("layer_pv_ready"), sem("layer_heads_out")
        ff_init, ff_conv, ff_gelu, ff_gated = sem("ff_init"), sem("ff_conv"), sem("ff_gelu"), sem("ff_gated")
        out_stored = sem("out_stored")
        par2_loaded, na_loaded, na_stored = sem("par2_loaded"), sem("na_loaded"), sem("na_stored")
        qksq_ready, qkvar_ready, qkstd_ready, qk_ready = sem("qksq_ready"), sem("qkvar_ready"), sem("qkstd_ready"), sem("qk_ready")
        sc_done, sc_ready = sem("sc_done"), sem("sc_ready")
        topd_ready, texp_ready, routed = sem("topd_ready"), sem("texp_ready"), sem("routed")
        idx_staged = sem("idx_staged")
        g_landed = [sem(f"g_landed{i}") for i in range(RING)]
        set_used = [sem(f"set_used{i}") for i in range(SETS)]
        dots_ready, gelu_ready, w_ready, diag_ready = sem("dots_ready"), sem("gelu_ready"), sem("w_ready"), sem("diag_ready")
        acc_ready = sem("acc_ready")
        pool_passed, dve_passed = sem("pool_waits_passed"), sem("dve_waits_passed")

        class Norm:

            def __init__(self, name):
                self.sq = sem(name + "_squares")
                self.var = sem(name + "_var")
                self.std = sem(name + "_std")
                self.hn = sem(name + "_normed")
                self.xp = sem(name + "_transposed")
                self.hT = sem(name + "_hT")

        n_attn, n_post, n_ffn, n_fpost = Norm("n_attn"), Norm("n_post"), Norm("n_ffn"), Norm("n_fpost")
        n_mix, n_peer = Norm("n_mix"), Norm("n_peer")


        def norm_act(act, nm, src, l):
            for t in range(TT):
                ins = nc.scalar.activation(junk[:, t, :], src[:, t, :], ACT.Square, accum_out=ssq[:, t:t + 1])
            ins.then_inc(nm.sq, 1)
            act.wait_ge(nm.var, l + 1)
            nc.scalar.activation(std, ssq, ACT.Sqrt).then_inc(nm.std, 1)

        def norm_dve_rstd(dve, ch, nm, l):
            dve.wait_ge(nm.sq, l + 1)
            nc.vector.tensor_scalar(ssq, ssq, 1.0 / D, EPS, ALU.mult, ALU.add).then_inc(nm.var, 1)
            dve.wait_ge(nm.std, l + 1)
            ch.link(nc.vector.reciprocal(rstd, std))

        def norm_dve_pre(dve, ch, nm, l, gain_fm, gain_tok):
            norm_dve_rstd(dve, ch, nm, l)
            for t in range(TT):
                if gain_tok is None:
                    ins = nc.vector.tensor_scalar(HN[:, t, :], X[:, t, :], rstd[:, t:t + 1], None, ALU.mult)
                else:
                    ins = nc.vector.scalar_tensor_tensor(out=HN[:, t, :], in0=X[:, t, :], scalar=rstd[:, t:t + 1],
                                                         in1=gain_tok, op0=ALU.mult, op1=ALU.mult)
            ins.then_inc(nm.hn, 1)
            for b in range(4):
                dve.wait_ge(nm.xp, 4 * l + b + 1)
                for c in (2 * b, 2 * b + 1):
                    src = ps[:, c * S:(c + 1) * S]
                    if gain_fm is None:
                        ins = nc.vector.tensor_copy(HT[:, c, :], src)
                    else:
                        ins = nc.vector.tensor_scalar(HT[:, c, :], src, gain_fm[:, c:c + 1], None, ALU.mult)
            ins.then_inc(nm.hT, 1)

        def norm_pe(pe, nm, l):
            pe.wait_ge(nm.hn, l + 1)
            for b in range(4):
                for c in (2 * b, 2 * b + 1):
                    for t in range(TT):
                        ins = nc.tensor.transpose(ps[:, c * S + t * P:c * S + (t + 1) * P],
                                                  HN[:, t, c * P:(c + 1) * P], ident)
                ins.then_inc(nm.xp, 1)

        def norm_dve_post(dve, ch, nm, gain):
            norm_dve_rstd(dve, ch, nm, 0)
            for t in range(TT):
                ch.step(nc.vector.scalar_tensor_tensor(out=Y[:, t, :], in0=Y[:, t, :], scalar=rstd[:, t:t + 1],
                                                       in1=gain, op0=ALU.mult, op1=ALU.mult))
            ch.sync()
            nc.vector.tensor_tensor(X[:, :, :], X[:, :, :], Y, ALU.add).then_inc(x_ready, 1)

        def landed(pe, g, l=0):
            per = 16 * L_GROUPS // SLOTS
            pe.wait_ge(w_landed[g % SLOTS], l * per + 16 * (g // SLOTS + 1))
            return W[:, g % SLOTS, :].rearrange("p (c n) -> p c n", c=KC)

        def group_fm(pe, g, b, l=0, src=HT, chunks=range(KC), done=True, base=0):
            w = landed(pe, g, l)
            for blk in range(2):
                for c in chunks:
                    ins = nc.tensor.matmul(ps[:, b * 512 + blk * S:b * 512 + (blk + 1) * S],
                                           w[:, c, blk * P:(blk + 1) * P], src[:, c, :],
                                           start=c == chunks[0], stop=c == chunks[-1])
            if done:
                ins.then_inc(group_done, 1)

        def group_tok(pe, g, b, l=0, src=HT):
            w = landed(pe, g, l)
            for t in range(TT):
                for c in range(KC):
                    ins = nc.tensor.matmul(ps[:, b * 512 + t * GC:b * 512 + (t + 1) * GC],
                                           src[:, c, t * P:(t + 1) * P], w[:, c, :],
                                           start=c == 0, stop=c == KC - 1)
            ins.then_inc(group_done, 1)

        class Attn:

            def __init__(self, low, scores, logits, probs, pTr, pTt, pv, heads, batches, fills):
                self.low, self.scores, self.logits, self.probs = low, scores, logits, probs
                self.pTr, self.pTt, self.pv, self.heads = pTr, pTt, pv, heads
                self.batches, self.fills = batches, fills

        class Batch:

            def __init__(self, at, fill, rows, width, q, col, kind, bias=None, sink=None):
                self.at, self.fill, self.rows, self.width, self.q, self.col = at, fill, rows, width, q, col
                self.kind, self.bias, self.sink = kind, bias, sink
                self.n = len(rows)
                self.wide = width + (sink is not None)
                self.blocks = self.n * width // P
                self.fills = -(-self.blocks // 4)
                self.L = LG[:, 0:self.n * self.wide].rearrange("p (n w) -> p n w", n=self.n)
                self.ps = ps[:, 0:self.n * width].rearrange("p (n w) -> p n w", n=self.n)

        def scores_pe(pe, A, b, l=0):
            if b.at:
                pe.wait_ge(A.heads, l * A.batches + b.at)
            places = []
            for r, (pieces, _) in enumerate(b.rows):
                at = r * b.width
                for q, k in pieces:
                    places.append((q.base_partition(), at, q, k))
                    at += k.shape[-1]
            for part in (0, HD):
                for p, at, q, k in places:
                    if p == part:
                        ins = nc.tensor.matmul(ps[:, at:at + k.shape[-1]], q, k, start=True, stop=True)
                if part == 0:
                    ins.then_inc(A.low, 1)
                    pe.wait_ge(A.low, l * A.batches + b.at + 1)
            ins.then_inc(A.scores, 1)

        def transposes_pe(pe, A, fill, sources, l):
            for f in range(0, len(sources), 4):
                n = fill + f // 4
                if n >= 2:
                    pe.wait_ge(A.pTt, l * A.fills + n - 1)
                for j, src in enumerate(sources[f:f + 4]):
                    ins = nc.tensor.transpose(ps[:, (4 + n % 2) * 512 + j * P:(4 + n % 2) * 512 + (j + 1) * P], src, ident)
                ins.then_inc(A.pTr, 1)

        def transposed_dve(dve, A, fill, count, dst, l):
            for f in range(0, count, 4):
                n, m = fill + f // 4, min(4, count - f)
                dve.wait_ge(A.pTr, l * A.fills + n + 1)
                nc.vector.tensor_copy(dst[:, f * P:(f + m) * P], ps[:, (4 + n % 2) * 512:(4 + n % 2) * 512 + m * P]).then_inc(A.pTt, 1)

        def values_pe(pe, A, b, l=0):
            pe.wait_ge(A.probs, l * A.batches + b.at + 1)
            per = b.width // P
            transposes_pe(pe, A, b.fill, [b.L[:, r, k * P:(k + 1) * P] for r in range(b.n) for k in range(per)], l)
            pe.wait_ge(A.pTt, l * A.fills + b.fill + b.fills)
            for r, (_, vals) in enumerate(b.rows):
                for k, v in enumerate(vals):
                    ins = nc.tensor.matmul(ps[:, r * HD:(r + 1) * HD], PT[:, r * per + k, :], v,
                                           start=k == 0, stop=k == per - 1)
            ins.then_inc(A.pv, 1)

        def logits_dve(dve, ch, A, b, l=0):
            if b.sink is not None:
                ch.step(nc.vector.tensor_copy(b.L[:, :, b.width:], b.sink.unsqueeze(2)))
            dve.wait_ge(A.scores, l * A.batches + b.at + 1)
            src, dst, bias = b.ps, b.L[:, :, 0:b.width], b.bias
            if len(bias.shape) == 3 and bias.shape[1] != b.n:
                src = ps[:, 0:b.n * b.width].rearrange("p (n w) -> p n w", n=bias.shape[1])
                dst = LG[:, 0:b.n * b.width].rearrange("p (n w) -> p n w", n=bias.shape[1])
            ch.link(nc.vector.scalar_tensor_tensor(out=dst, in0=src, scalar=SCALE, in1=bias,
                                                   op0=ALU.mult, op1=ALU.add))
            nc.vector.tensor_reduce(negm[:, 0:b.n], b.L, AX.X, ALU.max, negate=True).then_inc(A.logits, 1)

        def probs_act(act, A, b, l=0):
            act.wait_ge(A.logits, l * A.batches + b.at + 1)
            for r in range(b.n):
                ins = nc.scalar.activation(b.L[:, r, :], b.L[:, r, :], ACT.Exp, bias=negm[:, r:r + 1],
                                           accum_out=sums[:, r:r + 1])
            ins.then_inc(A.probs, 1)

        def heads_dve(dve, ch, A, b, l=0):
            transposed_dve(dve, A, b.fill, b.blocks, PT.rearrange("p k n -> p (k n)"), l)
            if b.kind == "softmax":
                ch.link(nc.vector.reciprocal(rsum[:, 0:b.n], sums[:, 0:b.n]))
            dve.wait_ge(A.pv, l * A.batches + b.at + 1)
            dst = O[:, b.q, b.col:b.col + b.n * HD]
            if b.kind == "softmax":
                nc.vector.tensor_tensor(dst.rearrange("p (n d) -> p n d", n=b.n),
                                        ps[:, 0:b.n * HD].rearrange("p (n d) -> p n d", n=b.n),
                                        view(rsum, [1, b.n], [0, HD]), ALU.mult).then_inc(A.heads, 1)
            else:
                nc.vector.tensor_copy(dst, ps[:, 0:b.n * HD]).then_inc(A.heads, 1)

        beta = LG
        keep = C2

        def stick_act(act, A, b):
            act.wait_ge(A.scores, b.at + 1)
            n = b.n * b.width
            nc.scalar.activation(beta[:, 0:n], ps[:, 0:n], ACT.Sigmoid, scale=SCALE)
            nc.scalar.activation(keep[:, 0:n], ps[:, 0:n], ACT.Sigmoid, scale=-SCALE).then_inc(A.logits, 1)

        def stick_dve(dve, ch, A, b):
            n, w = b.n * b.width, b.width
            prod = Y.rearrange("p t d -> p (t d)")[:, 0:b.n * (w + 1)].rearrange("p (n w) -> p n w", n=b.n)
            zeros = Y.rearrange("p t d -> p (t d)")[:, 1100:1100 + w]
            ch.step(nc.vector.memset(prod[:, :, w:], 1.0))
            ch.step(nc.vector.memset(zeros, 0.0))
            dve.wait_ge(A.logits, b.at + 1)
            k3 = keep[:, 0:n].rearrange("p (n w) -> p n w", n=b.n)
            mask = not_before[:, S - w:S]
            ch.link(nc.vector.tensor_tensor(k3, k3, view(mask, [0, b.n], [1, w]), ALU.max))
            for r in range(b.n):
                ch.step(nc.vector.tensor_tensor_scan(prod[:, r, 0:w][:, ::-1], k3[:, r, ::-1], zeros, 1.0,
                                                     ALU.mult, ALU.add))
            ch.sync()
            b3 = beta[:, 0:n].rearrange("p (n w) -> p n w", n=b.n)
            ch.link(nc.vector.tensor_tensor(b3, b3, prod[:, :, 1:], ALU.mult))
            mask = before[:, S - w:S]
            nc.vector.tensor_tensor(b3, b3, view(mask, [0, b.n], [1, w]), ALU.mult).then_inc(A.probs, 1)

        def branches_pe(pe, A, fill, g0, parts, l=0):
            transposes_pe(pe, A, fill, [O[:, t, c * P:(c + 1) * P] for c in range(KC) for t in range(TT)], l)
            pe.wait_ge(A.pTt, l * A.fills + fill + 4)
            for g in range(BR):
                at = 3 * (g % 2)
                if g >= 2:
                    pe.wait_ge(br_taken, g - 1 if isinstance(l, int) else l * BR + BR + g - 1)
                for j, chunks in enumerate(parts):
                    group_fm(pe, g0 + g, at + j, l, src=OT, chunks=chunks, done=j == len(parts) - 1)

        def merge_dve(dve, ch, A, fill, g0, n_br, l=0):
            transposed_dve(dve, A, fill, 16, OT.rearrange("p c n -> p (c n)"), l)
            for g in range(BR):
                dve.wait_ge(group_done, l * L_GROUPS + g0 + g + 1)
                at = 3 * (g % 2)
                dst = MT[:, 2 * g:2 * g + 2, :].rearrange("p a b -> p (a b)")
                tmp = PT.rearrange("p k n -> p (k n)")[:, (g % 2) * 1024:(g % 2) * 1024 + (n_br - 1) * 512]
                for j in range(n_br):
                    ins = nc.vector.tensor_tensor(dst if j == 0 else tmp[:, (j - 1) * 512:j * 512], bank(at + j),
                                                  GT[:, KC * j + 2 * g:KC * j + 2 * g + 2, :].rearrange("p a b -> p (a b)"), ALU.mult)
                    if j < n_br - 1:
                        ch.step(ins)
                ins.then_inc(br_taken, 1)
                dve.wait_ge(br_taken, g + 1 if isinstance(l, int) else l * BR + BR + g + 1)
                ch.sync()
                for j in range(1, n_br):
                    ins = nc.vector.tensor_tensor(dst, dst, tmp[:, (j - 1) * 512:j * 512], ALU.add)
                    if j < n_br - 1:
                        ch.link(ins)
                ins.then_inc(merged, 1)

        def wo_pe(pe, ch_wait, g0, taken, l=0):
            for g in range(WO):
                if g >= 2:
                    pe.wait_ge(wo_taken, g - 1 if isinstance(l, int) else l * (WO - 1) + WO + g - 1)
                else:
                    pe.wait_ge(ch_wait[0], ch_wait[1])
                if g == 0:
                    pe.wait_ge(taken[0], taken[1])
                group_tok(pe, g0 + g, 6 + g % 2, l, src=MT)

        AT1 = Attn(low_scores, scores_ready, logits_ready, probs_ready, pT_ready, pT_taken, pv_ready, heads_out, 7, 0)
        batches1 = []

        def add1(**kw):
            batches1.append(Batch(len(batches1), sum(b.fills for b in batches1), **kw))

        def half(tile3, c, h, sl):
            return tile3[HD * h:HD * (h + 1), c, sl]

        def rows_a(heads, q):
            rows = []
            for h in heads:
                hs = [(g * A_H + h) for g in range(A_G)]
                rows.append(([(half(aqT, j // 2, j % 2, slice(q * P, (q + 1) * P)),
                               half(akT, j // 2, j % 2, slice(0, (q + 1) * P))) for j in hs],
                             [av[:, k, j * HD:(j + 1) * HD] for j in hs for k in range(q + 1)]))
            return rows

        a_blocks = biasA.rearrange("p h g w -> p (h g) w")
        add1(rows=rows_a(range(4), 0), width=3 * P, q=0, col=0, kind="softmax", bias=a_blocks[:, :, P:S])
        for h in (0, 2):
            add1(rows=rows_a((h, h + 1), 1), width=3 * S, q=1, col=h * HD, kind="softmax",
                 bias=a_blocks[:, 3 * h:3 * h + 6, :])
        for q in range(TT):
            rows = [([(half(bqT, h % 4, h // 4, slice(q * P, (q + 1) * P)),
                       bkT[HD * (h // 4):HD * (h // 4 + 1), 0:(q + 1) * P])],
                     [bv[:, k, HD * (h // 4):HD * (h // 4 + 1)] for k in range(q + 1)]) for h in range(B_H)]
            add1(rows=rows, width=(q + 1) * P, q=q, col=A_H * HD, kind="softmax",
                 bias=biasB[:, :, (1 - q) * P:S], sink=PAR[:, P_SK:P_SK + B_H])
        for q in range(TT):
            rows = [([(half(cqT, h // 2, h % 2, slice(q * P, (q + 1) * P)),
                       half(ckT, h // 2, h % 2, slice(0, (q + 1) * P)))],
                     [cv[:, k, h * HD:(h + 1) * HD] for k in range(q + 1)]) for h in range(C_H)]
            add1(rows=rows, width=(q + 1) * P, q=q, col=(A_H + B_H) * HD, kind="stick")
        fill_o1 = sum(b.fills for b in batches1)

        order1 = ["G"] * 9 + ["B"]
        for b in batches1:
            order1 += [("S", b), "G", "G", ("V", b)]
        order1 += ["G"] * (IN_QKV + IN_GATE - order1.count("G"))

        FILL_QKT = 7
        batches2 = []
        for kind in range(2):
            for q in range(TT):
                rows = []
                for h in range(NQ):
                    if kind == 0:
                        c, k, part = h // 2, 4 + h // 2, h % 2
                        vals = [va[:, t, h * HD:(h + 1) * HD] for t in range(TT)]
                    else:
                        c, k, part = 8 + h % 4, 12, h // 4
                        vals = [vb[:, t, HD * part:HD * (part + 1)] for t in range(TT)]
                    rows.append(([(half(qkT, c, part, slice(q * P, (q + 1) * P)), half(qkT, k, part, slice(0, S)))], vals))
                if kind == 0:
                    bias, sink = naB[:, :, (2 - 2 * q) * GRID_W:(2 - 2 * q) * GRID_W + S], None
                else:
                    bias = view(CONST[:, C_SW + q * S:C_SW + q * S + S], [0, NQ], [1, S])
                    sink = PAR[:, Q_SK:Q_SK + NQ]
                batches2.append(Batch(len(batches2), FILL_QKT + sum(b.fills for b in batches2), rows=rows, width=S, q=q,
                                      col=kind * NQ * HD, kind="softmax", bias=bias, sink=sink))
        fill_o2 = FILL_QKT + sum(b.fills for b in batches2)
        L_FILLS = fill_o2 + 4
        AT2 = Attn(llow_scores, lscores_ready, llogits_ready, lprobs_ready, lpT_ready, lpT_taken, lpv_ready, lheads_out, 4, L_FILLS)
        order2 = ["G"] * L_PROJ + ["Q"]
        for b in batches2:
            order2 += [("S", b), "G", "G", ("V", b)]
        N2 = L_PROJ + L_GATE + L_PQ

        block = ctx.enter_context(nc.Block())

        @block.sync
        def _(sp):
            sp.dma_start(X[:, :, :], x_in.rearrange("(t p) d -> p t d", p=P)).then_inc(x_loaded, 16)
            sp.dma_start(CONST[:, :], consts).then_inc(const_loaded, 16)
            for g in range(SLOTS):
                sp.dma_start(W[:, g, :], wstream[g]).then_inc(w_landed[g], 16)
            whole = (GROUPS - SLOTS) // SLOTS
            with sp.Fori(0, whole) as k:
                for s in range(SLOTS):
                    sp.wait_ge(group_done, k * SLOTS + s + 1)
                    sp.dma_start(W[:, s, :], wstream[k * SLOTS + SLOTS + s]).then_inc(w_landed[s], 16)
            for g in range(SLOTS + whole * SLOTS, GROUPS):
                sp.wait_ge(group_done, g - SLOTS + 1)
                sp.dma_start(W[:, g % SLOTS, :], wstream[g]).then_inc(w_landed[g % SLOTS], 16)
            sp.wait_ge(x_ready, 2 + 3 * LAYERS)
            sp.dma_start(out.rearrange("(t p) d -> p t d", p=P), X[:, :, :]).then_inc(out_stored, 16)
            sp.wait_ge(out_stored, 16)

        @block.gpsimd
        def _(pool):
            nc.gpsimd.memset(ZERO[:, :], 0.0)
            nc.gpsimd.memset(lbase, 0.0).then_inc(zeroed, 1)
            for l in range(LAYERS):
                for r in range(2):
                    for h in range(NQ):
                        at = ((l * NQ + h) * RPB_R + 5 - r) * GRID_W * RPB_PAD + GRID_W - 1
                        pool.dma_start(na_rows[l, r * GRID_W:(r + 1) * GRID_W, h, :].rearrange("p (k n) -> p k n", k=NA_KK),
                                       bass.AP(tensor=rpb.tensor, offset=at, ap=[[RPB_PAD - 1, GRID_W], [GRID_W * RPB_PAD, NA_KK], [1, GRID_W]])).then_inc(na_stored, 16)
            with pool.Fori(0, LAYERS) as l:
                for t in range(TT):
                    wait_alone(pool, routed, l * TT + t + 1, pool_passed)
                    with pool.Fori(0, GITER) as i:
                        use = l * (TT * GITER) + i + t * GITER
                        for q in range(SETS):
                            wait_alone(pool, set_used[q], use + 1, pool_passed)
                            nc.gpsimd.tensor_copy(IDXS[:, q * SET:(q + 1) * SET],
                                                  EIDX[:, t, bass.ds(i * RING + q * SET, SET)]).then_inc(idx_staged, 1)
                            wait_alone(pool, idx_staged, use * SETS + q + 1, pool_passed)
                            for r in range(q * SET, (q + 1) * SET):
                                nc.gpsimd.indirect_dma_start(
                                    ring[:, r, :], None, experts,
                                    bass.IndirectOffsetOnAxis(ap=IDXS[:, r:r + 1], axis=0)).then_inc(g_landed[r], 16)

        @block.tensor
        def _(pe):
            for q in range(SETS):
                pe.sem_inc(set_used[q], 1)
            pe.wait_ge(bias_in, 32)
            for v in range(VAR):
                ins = nc.tensor.matmul(ps[0:20, v * 512:v * 512 + EW], relb_sb[0:NB_BUCKETS + 1, :],
                                       ohot[0:NB_BUCKETS + 1, v * EW:(v + 1) * EW], start=True, stop=True)
            ins.then_inc(erow_ready, 1)
            pe.wait_ge(const_loaded, 16)
            pe.wait_ge(erow_copied, 1)
            norm_pe(pe, n_attn, 0)
            pe.wait_ge(n_attn.hT, 1)
            g = 0
            for what in order1:
                if what == "G":
                    if g >= 2:
                        pe.wait_ge(proj_taken, g - 1)
                    token_major = g in (6, 7, 8, 14)
                    if g == 11:
                        w = landed(pe, g)
                        for c in range(KC):
                            nc.tensor.matmul(ps[:, (6 + g % 2) * 512:(6 + g % 2) * 512 + S], w[:, c, 0:P], HT[:, c, :],
                                             start=c == 0, stop=c == KC - 1)
                        for t in range(TT):
                            for c in range(KC):
                                ins = nc.tensor.matmul(ps[:, (6 + g % 2) * 512 + S + t * P:(6 + g % 2) * 512 + S + (t + 1) * P],
                                                       HT[:, c, t * P:(t + 1) * P], w[:, c, P:2 * P],
                                                       start=c == 0, stop=c == KC - 1)
                        ins.then_inc(group_done, 1)
                    elif token_major:
                        group_tok(pe, g, 6 + g % 2)
                    else:
                        group_fm(pe, g, 6 + g % 2)
                    g += 1
                elif what == "B":
                    pe.wait_ge(bias_loaded, 64)
                    for n in range(BIAS_FILLS):
                        if n >= 4:
                            pe.wait_ge(bias_taken, n - 3)
                        nc.tensor.matmul(bank(n % 4), turn, hank[:, n * 512:(n + 1) * 512], start=True, stop=True).then_inc(bias_turned, 1)
                    pe.wait_ge(bias_taken, BIAS_FILLS)
                elif what[0] == "S":
                    b = what[1]
                    pe.wait_ge(proj_taken, 9 if b.at < 3 else 12 if b.at < 5 else 15)
                    scores_pe(pe, AT1, b)
                else:
                    values_pe(pe, AT1, what[1])
            pe.wait_ge(heads_out, 7)
            branches_pe(pe, AT1, fill_o1, G_BR, (range(0, 2), range(2, 6), range(6, 8)))
            wo_pe(pe, (proj_taken, IN_QKV + IN_GATE), G_WO, (merged, BR))
            norm_pe(pe, n_ffn, 0)
            pe.wait_ge(n_ffn.hT, 1)
            pe.wait_ge(zeroed, 1)
            for b in range(4):
                nc.tensor.matmul(bank(b), ZERO[:, 0:P], ZERO[:, :], start=True, stop=False)

            def up(w, b):
                for half_ in range(2):
                    for c in range(KC):
                        ins = nc.tensor.matmul(ps[:, b * 512 + half_ * S:b * 512 + (half_ + 1) * S],
                                               w[:, c, half_ * P:(half_ + 1) * P], HT[:, c, :], start=c == 0, stop=c == KC - 1)
                ins.then_inc(group_done, 1)

            def down(slot, last):
                for j in range(2):
                    for t in range(TT):
                        for h in range(2):
                            ins = nc.tensor.matmul(bank(2 * t + h), ffg[:, j, t * P:(t + 1) * P],
                                                   W[:, slot, j * D + h * 512:j * D + (h + 1) * 512],
                                                   start=False, stop=last and j == 1)
                ins.then_inc(group_done, 1)

            for j in range(2):
                up(landed(pe, G_FF + j), 6 + j)
            first = G_FF + 2
            with pe.Fori(0, FF_BLOCKS // 2 - 1) as i:
                for j in range(2):
                    s = (first + j) % SLOTS
                    pe.wait_ge(w_landed[s], i * 16 + 16 * ((first + j) // SLOTS + 1))
                    pe.wait_ge(ff_conv, i * 2 + j + 1)
                    up(W[:, s, :].rearrange("p (c n) -> p c n", c=KC), 6 + j)
                s = (first + 2) % SLOTS
                pe.wait_ge(w_landed[s], i * 16 + 16 * ((first + 2) // SLOTS + 1))
                pe.wait_ge(ff_gated, i * 2 + 2)
                down(s, False)
            g = G_LAYER - 1
            landed(pe, g)
            pe.wait_ge(ff_gated, FF_BLOCKS)
            down(g % SLOTS, True)

            with pe.Fori(0, LAYERS) as l:
                norm_pe(pe, n_mix, l)
                pe.wait_ge(n_mix.hT, l + 1)
                g = 0
                for what in order2:
                    if what == "G":
                        if g >= 2:
                            pe.wait_ge(lproj_taken, l * N2 + g - 1)
                        (group_tok if g < L_PROJ else group_fm)(pe, G_LAYER + g, 6 + g % 2, l)
                        g += 1
                    elif what == "Q":
                        pe.wait_ge(qk_ready, l + 1)
                        transposes_pe(pe, AT2, 0, [QK[:, t, c * P:(c + 1) * P] for c in range(QK_HEADS // 2) for t in range(TT)], l)
                        pe.wait_ge(lpT_taken, l * L_FILLS + FILL_QKT)
                        pe.wait_ge(lproj_taken, l * N2 + L_PROJ)
                    elif what[0] == "S":
                        scores_pe(pe, AT2, what[1], l)
                    else:
                        values_pe(pe, AT2, what[1], l)
                pe.wait_ge(lheads_out, l * 4 + 4)
                branches_pe(pe, AT2, fill_o2, G_LAYER + LG_BR, (range(0, 4), range(4, 8)), l)
                wo_pe(pe, (lproj_taken, l * N2 + L_PROJ + L_GATE), G_LAYER + LG_WO, (merged, l * BR + 2 * BR), l)
                norm_pe(pe, n_peer, l)
                pe.wait_ge(n_peer.hT, l + 1)
                for j in range(L_PQ):
                    if j >= 2:
                        pe.wait_ge(lproj_taken, l * N2 + L_PROJ + L_GATE + j - 1)
                    group_fm(pe, G_LAYER + LG_PQ + j, 6 + j % 2, l)
                pe.wait_ge(lproj_taken, (l + 1) * N2)
                for t in range(TT):
                    for hp in range(16):
                        ins = nc.tensor.matmul(ps[:, t * 2048 + hp * NKEY:t * 2048 + (hp + 1) * NKEY], pqT[:, hp, t * P:(t + 1) * P],
                                               PAR[:, Q_KEYS + (hp % 2) * NKEY:Q_KEYS + (hp % 2 + 1) * NKEY], start=True, stop=True)
                    ins.then_inc(sc_done, 1)
                pe.wait_ge(sc_ready, l * TT + TT)
                for t in range(TT):
                    for h in range(2):
                        nc.tensor.matmul(bank(2 * t + h), ZERO[:, 0:P], ZERO[:, :], start=True, stop=False)
                    with pe.Fori(0, GITER) as i:
                        use = l * (TT * GITER) + i + t * GITER
                        for q in range(SETS):
                            pe.wait_ge(diag_ready, use * SETS + q + 1)
                            for r in range(q * SET, (q + 1) * SET):
                                for h in range(2):
                                    ins = nc.tensor.matmul(bank(2 * t + h), DIAG[:, r, :], ring[:, r, D + h * 512:D + (h + 1) * 512],
                                                           start=False, stop=False)
                            ins.then_inc(set_used[q], 1)
                    for h in range(2):
                        ins = nc.tensor.matmul(bank(2 * t + h), ZERO[:, 0:P], ZERO[:, :], start=False, stop=True)
                    ins.then_inc(acc_ready, 1)

        @block.scalar
        def _(act):
            act.dma_start(relb_sb[0:NB_BUCKETS + 1, :], relb).then_inc(bias_in, 16)
            act.dma_start(ohot[0:NB_BUCKETS + 1, :], onehot).then_inc(bias_in, 16)
            act.dma_start(PAR[:, 0:P_END], par1).then_inc(par1_loaded, 16)
            act.wait_ge(erow_ready, 1)
            for v in range(VAR):
                ins = nc.scalar.activation(erow[0:20, v * EW:(v + 1) * EW], ps[0:20, v * 512:v * 512 + EW], ACT.Copy)
            ins.then_inc(erow_copied, 1)
            act.wait_ge(erow_copied, 1)
            act.dma_start(scratch, erow[0:20, :]).then_inc(erow_stored, 16)
            act.wait_ge(x_loaded, 16)
            norm_act(act, n_attn, X, 0)
            act.wait_ge(erow_stored, 16)
            for gi in range(A_G):
                act.dma_start(hankA[:, :, gi, :], bass.AP(tensor=scratch.tensor, offset=gi * A_H * VAR * EW + gi * EW,
                                                          ap=[[1, P], [VAR * EW, A_H], [1, S]])).then_inc(bias_loaded, 16)
            act.dma_start(hankB, bass.AP(tensor=scratch.tensor, offset=A_G * A_H * VAR * EW + 3 * EW,
                                         ap=[[1, P], [VAR * EW, B_H], [1, S]])).then_inc(bias_loaded, 16)
            act.wait_ge(par1_loaded, 16)

            def take1(g):
                act.wait_ge(group_done, g + 1)
                src = bank(6 + g % 2)
                t2 = src.rearrange("p (t n) -> p t n", t=TT)
                if g < 3:
                    ins = nc.scalar.activation(aqT[:, 2 * g:2 * g + 2, :], t2, ACT.Copy)
                elif g < 6:
                    ins = nc.scalar.activation(akT[:, 2 * g - 6:2 * g - 4, :], t2, ACT.Copy)
                elif g < 9:
                    ins = nc.scalar.activation(av[:, :, (g - 6) * GC:(g - 5) * GC], t2, ACT.Copy)
                elif g < 11:
                    ins = nc.scalar.activation(bqT[:, 2 * (g - 9):2 * (g - 8), :], t2, ACT.Copy)
                elif g == 11:
                    nc.scalar.activation(bkT, src[:, 0:S], ACT.Copy)
                    ins = nc.scalar.activation(bv, src[:, S:2 * S].rearrange("p (t n) -> p t n", t=TT), ACT.Copy)
                elif g < 15:
                    ins = nc.scalar.activation((cqT, ckT, cv)[g - 12], t2, ACT.Copy)
                else:
                    for j in range(2):
                        f = 2 * (g - G_GATE) + j
                        ins = nc.scalar.activation(GT[:, f, :], t2[:, j, :], ACT.Sigmoid, bias=PAR[:, P_BG + f:P_BG + f + 1])
                ins.then_inc(proj_taken, 1)

            g = 0
            for at, what in enumerate(order1):
                if what == "G":
                    take1(g)
                    g += 1
                    if at and order1[at - 1][0] == "S":
                        b = order1[at - 1][1]
                        if b.kind == "softmax":
                            probs_act(act, AT1, b)
                        else:
                            stick_act(act, AT1, b)
            act.wait_ge(wo_taken, WO)
            norm_act(act, n_post, Y, 0)
            act.wait_ge(x_ready, 1)
            norm_act(act, n_ffn, X, 0)

            def ff_act(blk, j, cvw, done):
                act.wait_ge(group_done, done)
                for gv in range(2):
                    ins = nc.scalar.activation(ffacc[:, j, gv, :], bank(6 + j)[:, gv * S:(gv + 1) * S], ACT.Identity,
                                               scale=cvw(gv, 2), bias=cvw(gv, 3))
                ins.then_inc(ff_init, 1)
                act.wait_ge(ff_conv, blk + 1)
                nc.scalar.activation(ffacc[:, j, 0, :], ffacc[:, j, 0, :], ACT.Gelu_apprx_tanh).then_inc(ff_gelu, 1)

            def static_taps(n):
                return lambda gv, k: PAR[:, P_CV + n * 8 + gv * 4 + k:P_CV + n * 8 + gv * 4 + k + 1]

            for j in range(2):
                ff_act(j, j, static_taps(j), G_FF + j + 1)
            with act.Fori(0, FF_BLOCKS // 2 - 1) as i:
                for j in range(2):
                    def taps(gv, k):
                        return PAR[:, bass.ds(i * 16 + (P_CV + 16 + j * 8 + gv * 4 + k), 1)]
                    act.wait_ge(ff_gated, i * 2 + j + 1)
                    ff_act(i * 2 + 2 + j, j, taps, i * 3 + G_FF + 2 + j + 1)
            act.wait_ge(ff_taken, 1)
            norm_act(act, n_fpost, Y, 0)

            act.wait_ge(na_stored, LAYERS * 2 * NQ * 16)
            with act.Fori(0, LAYERS) as l:
                act.wait_ge(x_ready, l * 3 + 2)
                act.dma_start(PAR[:, 0:Q_END], par2[l]).then_inc(par2_loaded, 16)
                act.dma_start(naB, na_rows[l]).then_inc(na_loaded, 16)
                norm_act(act, n_mix, X, l)
                act.wait_ge(par2_loaded, l * 16 + 16)

                def take2(g):
                    act.wait_ge(group_done, l * L_GROUPS + G_LAYER + g + 1)
                    t2 = bank(6 + g % 2).rearrange("p (t n) -> p t n", t=TT)
                    if g < 6:
                        ins = nc.scalar.activation(QK[:, :, g * GC:(g + 1) * GC], t2, ACT.Copy)
                    elif g == 6:
                        nc.scalar.activation(QK[:, :, 6 * GC:6 * GC + P], t2[:, :, 0:P], ACT.Copy)
                        ins = nc.scalar.activation(vb, t2[:, :, P:2 * P], ACT.Copy)
                    elif g < 9:
                        ins = nc.scalar.activation(va[:, :, (g - 7) * GC:(g - 6) * GC], t2, ACT.Copy)
                    else:
                        for j in range(2):
                            f = 2 * (g - L_PROJ) + j
                            ins = nc.scalar.activation(GT[:, f, :], t2[:, j, :], ACT.Sigmoid, bias=PAR[:, Q_BG + f:Q_BG + f + 1])
                    ins.then_inc(lproj_taken, 1)
                    if g == 6:
                        act.wait_ge(lproj_taken, l * N2 + 7)
                        nc.scalar.activation(qksq, QK.rearrange("p t n -> p (t n)"), ACT.Square).then_inc(qksq_ready, 1)
                        act.wait_ge(qkvar_ready, l + 1)
                        nc.scalar.activation(hrstd, hssq, ACT.Sqrt).then_inc(qkstd_ready, 1)

                g = 0
                for at, what in enumerate(order2):
                    if what == "G":
                        take2(g)
                        g += 1
                        if at and order2[at - 1][0] == "S":
                            probs_act(act, AT2, order2[at - 1][1], l)
                act.wait_ge(x_ready, l * 3 + 3)
                norm_act(act, n_peer, X, l)
                for j in range(L_PQ):
                    act.wait_ge(group_done, l * L_GROUPS + G_LAYER + LG_PQ + j + 1)
                    nc.scalar.activation(pqT[:, 2 * j:2 * j + 2, :], bank(6 + j % 2).rearrange("p (t n) -> p t n", t=TT),
                                         ACT.Copy).then_inc(lproj_taken, 1)
                for t in range(TT):
                    act.wait_ge(sc_done, l * TT + t + 1)
                    for j in range(4):
                        ins = nc.scalar.activation(SC[:, t, 4 * j:4 * j + 4, :], bank(4 * t + j).rearrange("p (a n) -> p a n", a=4), ACT.Copy)
                    ins.then_inc(sc_ready, 1)
                for t in range(TT):
                    act.wait_ge(topd_ready, l * TT + t + 1)
                    nc.scalar.activation(GWT[:, t, :], GWT[:, t, :], ACT.Exp).then_inc(texp_ready, 1)
                for t in range(TT):
                    with act.Fori(0, GITER) as i:
                        use = l * (TT * GITER) + i + t * GITER

                        def gelu(q):
                            act.wait_ge(dots_ready, use * SETS + q + 1)
                            nc.scalar.activation(ga[:, q * SET:(q + 1) * SET], hd[:, q * SET:(q + 1) * SET], ACT.Gelu).then_inc(gelu_ready, 1)

                        def diagonals(q):
                            act.wait_ge(w_ready, use * SETS + q + 1)
                            for r in range(q * SET, (q + 1) * SET):
                                ins = nc.scalar.activation(DIAG[:, r, :], ident, ACT.Copy, scale=gw8[:, r:r + 1])
                            ins.then_inc(diag_ready, 1)

                        gelu(0)
                        for q in range(1, SETS):
                            gelu(q)
                            diagonals(q - 1)
                        diagonals(SETS - 1)

        @block.vector
        def _(dve):
            ch = Chain(dve, dve_step)
            dve.wait_ge(x_loaded, 16)
            dve.wait_ge(par1_loaded, 16)
            dve.wait_ge(const_loaded, 16)
            norm_dve_pre(dve, ch, n_attn, 0, PAR[:, P_G1:P_G1 + KC], None)
            for n in range(BIAS_FILLS):
                dve.wait_ge(bias_turned, n + 1)
                nc.vector.tensor_copy(bias_all[:, n * 512:(n + 1) * 512], bank(n % 4)).then_inc(bias_taken, 1)
            dve.wait_ge(bias_taken, BIAS_FILLS)
            for b in batches1:
                if b.kind == "softmax":
                    logits_dve(dve, ch, AT1, b)
                else:
                    stick_dve(dve, ch, AT1, b)
                heads_dve(dve, ch, AT1, b)
            dve.wait_ge(proj_taken, IN_QKV + IN_GATE)
            merge_dve(dve, ch, AT1, fill_o1, G_BR, 3)
            for g in range(WO):
                dve.wait_ge(group_done, G_WO + g + 1)
                nc.vector.tensor_copy(Y[:, :, g * GC:(g + 1) * GC], bank(6 + g % 2).rearrange("p (t n) -> p t n", t=TT)).then_inc(wo_taken, 1)
            dve.wait_ge(wo_taken, WO)
            norm_dve_post(dve, ch, n_post, PAR[:, P_POST:P_POST + D])
            dve.wait_ge(x_ready, 1)
            norm_dve_pre(dve, ch, n_ffn, 0, PAR[:, P_G2:P_G2 + KC], None)

            def ff_conv_dve(blk, j, taps):
                dve.wait_ge(ff_init, blk + 1)
                for back, k in ((1, 1), (2, 0)):
                    for gv in range(2):
                        acc = ffacc[:, j, gv, back:S]
                        ins = nc.vector.scalar_tensor_tensor(out=acc, in0=bank(6 + j)[:, gv * S:(gv + 1) * S - back], scalar=taps(gv, k),
                                                             in1=acc, op0=ALU.mult, op1=ALU.add)
                        if back == 1:
                            ch.step(ins)
                    if back == 1:
                        ch.sync()
                ins.then_inc(ff_conv, 1)

            def ff_gate_dve(blk, j):
                dve.wait_ge(ff_gelu, blk + 1)
                nc.vector.tensor_tensor(ffg[:, j, :], ffacc[:, j, 0, :], ffacc[:, j, 1, :], ALU.mult).then_inc(ff_gated, 1)

            def static_taps(n):
                return lambda gv, k: PAR[:, P_CV + n * 8 + gv * 4 + k:P_CV + n * 8 + gv * 4 + k + 1]

            for j in range(2):
                ff_conv_dve(j, j, static_taps(j))
            for j in range(2):
                ff_gate_dve(j, j)
            with ch.loop(FF_BLOCKS // 2 - 1, 4) as i:
                for j in range(2):
                    def taps(gv, k):
                        return PAR[:, bass.ds(i * 16 + (P_CV + 16 + j * 8 + gv * 4 + k), 1)]
                    ff_conv_dve(i * 2 + 2 + j, j, taps)
                dve.wait_ge(group_done, i * 3 + G_FF + 5)
                for j in range(2):
                    ff_gate_dve(i * 2 + 2 + j, j)
            dve.wait_ge(group_done, G_LAYER)
            nc.vector.tensor_copy(Y, ps[:, 0:2048].rearrange("p (t n) -> p t n", t=TT)).then_inc(ff_taken, 1)
            dve.wait_ge(ff_taken, 1)
            norm_dve_post(dve, ch, n_fpost, PAR[:, P_FPOST:P_FPOST + D])

            dve.wait_ge(zeroed, 1)
            ch.restart()
            with dve.Fori(0, LAYERS) as l:
                dve.wait_ge(x_ready, l * 3 + 2)
                dve.wait_ge(par2_loaded, l * 16 + 16)
                norm_dve_pre(dve, ch, n_mix, l, PAR[:, Q_G:Q_G + KC], None)
                dve.wait_ge(na_loaded, l * 16 + 16)
                na4 = naB.rearrange("p h (k n) -> p (h k) n", k=NA_KK)
                ch.step(nc.vector.tensor_tensor(na4, na4, view(CONST[:, C_NA:C_NA + GRID_W], [0, NQ * NA_KK], [1, GRID_W]), ALU.add))
                dve.wait_ge(qksq_ready, l + 1)
                ch.link(nc.vector.tensor_reduce(hssq, qksq.rearrange("p (h d) -> p h d", d=HD), AX.X, ALU.add))
                nc.vector.tensor_scalar(hssq, hssq, 1.0 / HD, EPS, ALU.mult, ALU.add).then_inc(qkvar_ready, 1)
                dve.wait_ge(qkstd_ready, l + 1)
                ch.link(nc.vector.reciprocal(hrstd, hrstd))
                qk3 = QK.rearrange("p t (h d) -> p (t h) d", d=HD)
                ch.link(nc.vector.tensor_tensor(qk3, qk3, view(hrstd, [1, TT * QK_HEADS], [0, HD]), ALU.mult))
                ch.link(nc.vector.tensor_tensor(QK, QK, view(PAR[:, Q_QKN:Q_QKN + QKW], [0, TT], [1, QKW]), ALU.mult))
                q4 = QK[:, :, 2 * NQ * HD:].rearrange("p t (h s d) -> p t h s d", s=2, d=32)
                x1, x2 = q4[:, :, :, 0, :], q4[:, :, :, 1, :]
                cos = view(CONST[:, C_COS:C_COS + 1], [32, TT], [0, 10], [1, 32])
                sin = view(CONST[:, C_SIN:C_SIN + 1], [32, TT], [0, 10], [1, 32])
                r4 = [rot[:, j, :].rearrange("p (t h d) -> p t h d", t=TT, h=10) for j in range(4)]
                for j, (a, c) in enumerate(((x1, cos), (x2, sin), (x1, sin), (x2, cos))):
                    ch.step(nc.vector.tensor_tensor(r4[j], a, c, ALU.mult))
                ch.sync()
                ch.step(nc.vector.tensor_tensor(x1, r4[0], r4[1], ALU.subtract))
                nc.vector.tensor_tensor(x2, r4[2], r4[3], ALU.add).then_inc(qk_ready, 1)
                transposed_dve(dve, AT2, 0, QK_HEADS, qkT.rearrange("p c n -> p (c n)"), l)
                for b in batches2:
                    logits_dve(dve, ch, AT2, b, l)
                    heads_dve(dve, ch, AT2, b, l)
                dve.wait_ge(lproj_taken, l * N2 + L_PROJ + L_GATE)
                merge_dve(dve, ch, AT2, fill_o2, G_LAYER + LG_BR, 2, l)
                for g in range(WO):
                    dve.wait_ge(group_done, l * L_GROUPS + G_LAYER + LG_WO + g + 1)
                    dst = X[:, :, g * GC:(g + 1) * GC]
                    ins = nc.vector.tensor_tensor(dst, dst, bank(6 + g % 2).rearrange("p (t n) -> p t n", t=TT), ALU.add)
                    ins.then_inc(wo_taken if g < WO - 1 else x_ready, 1)
                dve.wait_ge(x_ready, l * 3 + 3)
                norm_dve_pre(dve, ch, n_peer, l, None, PAR[:, Q_GF:Q_GF + D])

                def route(t):
                    wait_alone(dve, sc_ready, l * TT + t + 1, dve_passed)
                    for hp in range(16):
                        s = SC[:, t, hp, :]
                        ch.link(nc.vector.max(sv[:, hp, 0:8], s))
                        ch.step(nc.vector.max_index(si[:, hp, 0:8], sv[:, hp, 0:8], s))
                        ch.link(nc.vector.match_replace(s2, sv[:, hp, 0:8], s, LOWEST))
                        ch.link(nc.vector.max(sv[:, hp, 8:16], s2))
                        ch.link(nc.vector.max_index(si[:, hp, 8:16], sv[:, hp, 8:16], s2))
                    ch.step(nc.vector.tensor_copy(siF, si[:, :, :]))
                    sv4 = sv.rearrange("p (h s) k -> p h s k", s=2)
                    a4, b4 = sv4[:, :, 0, :], sv4[:, :, 1, :]
                    ch.link(nc.vector.tensor_tensor(cand.rearrange("p h (a b) -> p h a b", a=TOPK),
                                                    view(a4, [2 * TOPK, PH], [1, TOPK], [0, TOPK]),
                                                    view(b4, [2 * TOPK, PH], [0, TOPK], [1, TOPK]), ALU.add))
                    sel = SEL[:, 0, :].rearrange("p (h k) -> p h k", h=PH)
                    for h in range(PH):
                        s = cand[:, h, :]
                        ch.link(nc.vector.max(topv[:, h, 0:8], s))
                        ch.step(nc.vector.max_index(sel[:, h, 0:8], topv[:, h, 0:8], s))
                        ch.link(nc.vector.match_replace(cand2, topv[:, h, 0:8], s, LOWEST))
                        ch.link(nc.vector.max(topv[:, h, 8:16], cand2))
                        ch.link(nc.vector.max_index(sel[:, h, 8:16], topv[:, h, 8:16], cand2))
                    g3 = GWT[:, t, :].rearrange("p (h k) -> p h k", h=PH)
                    nc.vector.tensor_tensor(g3, topv, view(topv, [TOPK, PH], [0, TOPK]), ALU.subtract).then_inc(topd_ready, 1)
                    ch.step(nc.vector.tensor_scalar(SEL[:, 1, :], SEL[:, 0, :], 4, None, ALU.logical_shift_right))
                    ch.link(nc.vector.tensor_scalar(SEL[:, 2, :], SEL[:, 0, :], TOPK - 1, None, ALU.bitwise_and))
                    ch.link(nc.vector.tensor_copy(abF[:, :, :], SEL[:, 1:3, :]))
                    si4 = siF.rearrange("p (h s) k -> p h s k", s=2)
                    for j, eq in enumerate((eqA, eqB)):
                        ch.step(nc.vector.tensor_tensor(eq.rearrange("p (n a) -> p n a", a=TOPK), view(abF[:, j, :], [1, PICKS], [0, TOPK]),
                                                        view(iota16, [0, PICKS], [1, TOPK]), ALU.is_equal))
                    ch.sync()
                    for j, eq in enumerate((eqA, eqB)):
                        eq4 = eq.rearrange("p (h k a) -> p h k a", h=PH, a=TOPK)
                        ch.step(nc.vector.tensor_tensor(eq4, eq4, view(si4[:, :, j, :], [2 * TOPK, PH], [0, TOPK], [1, TOPK]), ALU.mult))
                    ch.sync()
                    for j, eq in enumerate((eqA, eqB)):
                        ch.step(nc.vector.tensor_reduce(eF[:, j, :], eq.rearrange("p (n a) -> p n a", a=TOPK), AX.X, ALU.add))
                    ch.sync()
                    ch.link(nc.vector.scalar_tensor_tensor(out=eF[:, 0, :], in0=eF[:, 0, :], scalar=float(NKEY), in1=eF[:, 1, :],
                                                           op0=ALU.mult, op1=ALU.add))
                    ch.step(nc.vector.tensor_scalar(EIDX[:, t, :], eF[:, 0, :], lbase, None, ALU.add))
                    dve.wait_ge(texp_ready, l * TT + t + 1)
                    ch.link(nc.vector.tensor_reduce(esum, g3, AX.X, ALU.add))
                    ch.link(nc.vector.reciprocal(ersum, esum))
                    nc.vector.tensor_tensor(g3, g3, view(ersum, [1, PH], [0, TOPK]), ALU.mult).then_inc(routed, 1)

                for t in range(TT):
                    route(t)
                ch.step(nc.vector.tensor_scalar(lbase, lbase, float(EXPERTS), None, ALU.add))
                wait_alone(dve, routed, l * TT + TT, dve_passed)
                for t in range(TT):
                    with dve.Fori(0, GITER) as i:
                        use = l * (TT * GITER) + i + t * GITER

                        def dots(q):
                            for r in range(q * SET, (q + 1) * SET):
                                dve.wait_ge(g_landed[r], use * 16 + 16)
                                ins = nc.vector.tensor_tensor_reduce(ring[:, r, 0:D], HN[:, t, :], ring[:, r, 0:D], 1.0, 0.0,
                                                                     ALU.mult, ALU.add, hd[:, r:r + 1])
                            ins.then_inc(dots_ready, 1)

                        def weights(q):
                            wait_alone(dve, gelu_ready, use * SETS + q + 1, dve_passed)
                            nc.vector.tensor_tensor(gw8[:, q * SET:(q + 1) * SET], ga[:, q * SET:(q + 1) * SET],
                                                    GWT[:, t, bass.ds(i * RING + q * SET, SET)], ALU.mult).then_inc(w_ready, 1)

                        dots(0)
                        for q in range(1, SETS):
                            dots(q)
                            weights(q - 1)
                        weights(SETS - 1)
                    dve.wait_ge(acc_ready, l * TT + t + 1)
                    nc.vector.tensor_tensor(X[:, t, :], X[:, t, :], ps[:, 2 * t * 512:(2 * t + 2) * 512], ALU.add).then_inc(x_ready, 1)
                ch.restart()


def t5_bucket(dist):
    exact = NB_BUCKETS // 2
    nf = np.maximum(dist, 1).astype(np.float32)
    large = exact + (np.log(nf / np.float32(exact)) / np.float32(np.log(2048 / exact)) * np.float32(NB_BUCKETS - exact)).astype(np.int32)
    return np.where(dist < exact, dist, np.minimum(large, NB_BUCKETS - 1))


def shape_constants():
    f = np.float32
    c = np.zeros((P, C_END), f)
    c[:, C_ID:C_ID + P] = np.eye(P, dtype=f)
    c[:, C_TURN:C_TURN + P] = np.eye(P, dtype=f)[::-1]
    q = np.arange(P)
    b = np.ones((P, S), f)
    b[:, P:] = q[None, :] < q[:, None]
    c[:, C_BM:C_BM + S] = b
    c[:, C_NB:C_NB + S] = 1 - b
    col = q % GRID_W
    cs = np.clip(col - 8, 0, GRID_W - 16)
    kc = np.arange(GRID_W)
    c[:, C_NA:C_NA + GRID_W] = np.where((kc[None] >= cs[:, None]) & (kc[None] < cs[:, None] + 16), 0, NEG)
    inv = f(10000.0) ** (-np.arange(32, dtype=f) / f(32))
    for t in range(TT):
        pos = q + t * P
        c[:, C_SW + t * S:C_SW + (t + 1) * S] = np.where(np.abs(pos[:, None] - np.arange(S)[None]) <= 128, 0, NEG)
        ang = pos.astype(f)[:, None] * inv[None]
        c[:, C_COS + t * 32:C_COS + (t + 1) * 32] = np.cos(ang)
        c[:, C_SIN + t * 32:C_SIN + (t + 1) * 32] = np.sin(ang)
    c[:, C_IOTA:C_IOTA + TOPK] = np.arange(TOPK, dtype=f)
    oh = np.zeros((NB_BUCKETS + 1, VAR, EW), f)
    for v, (step, limit) in enumerate(((1, 128), (4, 512), (16, 2048), (1, 127))):
        for x in range(EW):
            dist = S - 1 - x
            ok = 0 <= dist <= limit and dist % step == 0
            oh[int(t5_bucket(np.array(dist))) if ok else NB_BUCKETS, v, x] = 1
    return c, oh.reshape(NB_BUCKETS + 1, VAR * EW)


def pack(w):
    n = w.shape[1] // GC
    return w.reshape(KC, P, n, GC).transpose(2, 1, 0, 3).reshape(n, P, GW)


def by_feature(v):
    return v.reshape(-1, P).T


def rows_on_all(v):
    return np.broadcast_to(v.reshape(1, -1), (P, v.size))


def lay_out(i):
    cat = np.concatenate
    pairs = [0, 4, 1, 5, 2, 6, 3, 7]
    w = i["w_in"][0]
    bq = w[:, 2304:2816].reshape(D, 8, HD)[:, pairs].reshape(D, 512)
    w = cat([w[:, :2304], bq, w[:, 2816:]], 1)
    groups = [pack(w), pack(cat([i["w_br_a"][0], i["w_br_b"][0], i["w_br_c"][0]], 0)), pack(i["w_out"][0])]
    up = pack(i["w_up"][0].reshape(D, 2, FF_BLOCKS, P).transpose(0, 2, 1, 3).reshape(D, 2 * FF_BLOCKS * P))
    dn = i["w_down"][0].reshape(FF_BLOCKS // 2, 2, P, D).transpose(0, 2, 1, 3).reshape(FF_BLOCKS // 2, P, GW)
    ff = [up[0:2]]
    for k in range(1, FF_BLOCKS // 2):
        ff += [up[2 * k:2 * k + 2], dn[k - 1:k]]
    groups += ff + [dn[-1:]]
    par2, rpb = [], []
    for l in range(LAYERS):
        w = i["w_in_2"][l]
        qb = w[:, 1536:2048].reshape(D, 8, HD)[:, pairs].reshape(D, 512)
        w = cat([w[:, 0:1024], qb, w[:, 2048:2304], w[:, 1024:1536], w[:, 2304:]], 1)
        groups += [pack(w), pack(cat([i["w_branch_na_2"][l], i["w_branch_swa_2"][l]], 0)), pack(i["w_out_2"][l]), pack(i["peer_query_2"][l])]
        n = i["qk_norm_2"][l]
        qkn = cat([np.broadcast_to(n[j], (c, HD)).reshape(-1) for j, c in ((0, 8), (1, 8), (2, 8), (3, 2))])
        par2.append(cat([by_feature(i["norm_mix_2"][l]), by_feature(i["gate_bias_2"][l].reshape(-1)), rows_on_all(i["swa_sink_2"][l]),
                         rows_on_all(qkn), rows_on_all(i["norm_ffn_2"][l]),
                         i["peer_sub_keys_2"][l].transpose(2, 0, 1).reshape(P, 2 * NKEY)], 1))
        padded = np.pad(i["na_rpb_2"][l], ((0, 0), (0, 0), (GRID_W - 16, GRID_W - 16)))
        rpb.append(np.broadcast_to(padded[:, :, None, :], (NQ, RPB_R, GRID_W, RPB_PAD)))
    cw = i["conv_w"][0].reshape(3, 2, FF_BLOCKS, P)
    cb = i["conv_b"][0].reshape(1, 2, FF_BLOCKS, P)
    taps = cat([cw, cb], 0).transpose(3, 2, 1, 0).reshape(P, FF_BLOCKS * 8)
    par1 = cat([by_feature(i["attn_pre_norm"][0]), by_feature(i["ffn_pre_norm"][0]), by_feature(i["b_gate"][0].reshape(-1)), taps,
                rows_on_all(i["sinks"][0]), rows_on_all(i["attn_post_norm"][0]), rows_on_all(i["ffn_post_norm"][0])], 1)
    consts, onehot = shape_constants()
    return {
        "x": i["x"][0], "wstream": cat(groups, 0), "consts": consts, "onehot": onehot,
        "relb": np.pad(i["rel_bias"], ((0, 1), (0, 0)), constant_values=NEG),
        "par1": par1, "par2": np.stack(par2), "rpb": np.stack(rpb),
        "experts": cat([i["peer_down_2"].reshape(-1, D), i["peer_up_2"].reshape(-1, D)], 1),
    }


def kernel(**inputs):
    import concourse.bacc as bacc
    from concourse.bass_utils import run_bass_kernel_spmd as run

    nc = bacc.Bacc("TRN2", target_bir_lowering=False, num_devices=1)
    laid = lay_out({k: np.asarray(v) for k, v in inputs.items()})
    arrays, args = {}, []
    for name, a in laid.items():
        arrays["in_" + name] = np.ascontiguousarray(a, dtype=np.float32)
        args.append(nc.dram_tensor("in_" + name, a.shape, F32, kind="ExternalInput").ap())
    result = nc.dram_tensor("result", (S, D), F32, kind="ExternalOutput").ap()
    build(nc, *args, result)
    return run(nc, [arrays], core_ids=[0]).results[0]["result"].reshape(1, S, D)
```

```python
from contextlib import ExitStack, contextmanager

import numpy as np

import concourse.bass as bass
from concourse import mybir

F32 = mybir.dt.float32
F32R = mybir.dt.float32r
BF16 = mybir.dt.bfloat16
U32 = mybir.dt.uint32
ACT = mybir.ActivationFunctionType
ALU = mybir.AluOpType
AX = mybir.AxisListType

P = 128
D = 1024
S = 256
TT = S // P
KC = D // P
HD = 64
SCALE = HD ** -0.5
EPS = 1e-6
NEG = -1e30
LOWEST = -3.0e38

GC = 256
GW = KC * GC
HW = GW // 2
HC = KC // 2
SLOTS = 3
IN_QKV, IN_GATE, BR, WO = 15, 12, 4, 4
FF_BLOCKS = 32
TOK_1 = (6, 7, 8, 14)
G_GATE = IN_QKV
G_BR = IN_QKV + IN_GATE
G_WO = G_BR + BR
G_FF = G_WO + WO
G_LAYER = G_FF + FF_BLOCKS + FF_BLOCKS // 2
L_PROJ, L_GATE, L_PQ = 9, 8, 8
LG_GATE = L_PROJ
LG_BR = LG_GATE + L_GATE
LG_WO = LG_BR + BR
LG_PQ = LG_WO + WO
L_GROUPS = LG_PQ + L_PQ
LAYERS = 2
GROUPS = G_LAYER + LAYERS * L_GROUPS
HALVES, L_HALVES = 2 * GROUPS, 2 * L_GROUPS
F_HALF, L_HALF = 2 * G_FF, 2 * G_LAYER
F_BODY = 6
assert L_HALVES % SLOTS == 0 and F_BODY % SLOTS == 0

A_H, A_G, B_H, C_H = 4, 3, 8, 4
VAR = 4
EW = 384
NB_BUCKETS = 32

NQ = 8
QK_HEADS = 3 * NQ + 2
QKW = QK_HEADS * HD
ROWS = 4
GRID_W = 64
RPB_R, RPB_C = 15, 31
RPB_PAD = 2 * GRID_W - 1
NA_KK = 6
PH = 8
NKEY = 128
TOPK = 16
EXPERTS = NKEY * NKEY
PICKS = PH * TOPK
SETS, SET = 4, 2
RING = SETS * SET
PASSES = TOPK // RING
STEPS = TT * PH
USES = STEPS * PASSES
ROUTES = STEPS + 1

C_ID, C_TURN, C_BM, C_NB, C_NA, C_SW, C_COS, C_SIN, C_IOTA, C_END = np.cumsum(
    [0, P, P, S, S, GRID_W, TT * S, TT * 32, TT * 32, TOPK]).tolist()
P_G1, P_G2, P_BG, P_CV, P_SK, P_POST, P_FPOST, P_END = np.cumsum(
    [0, KC, KC, 24, FF_BLOCKS * 8, B_H, D, D]).tolist()
Q_G, Q_BG, Q_SK, Q_QKN, Q_GF, Q_KEYS, Q_END = np.cumsum(
    [0, KC, 16, NQ, QKW, D, 2 * NKEY]).tolist()


def wait_alone(eng, sem, value, passed):
    eng.wait_ge(sem, value)
    eng.sem_inc(passed, 1)


class Chain:

    def __init__(self, eng, sem):
        self.eng, self.sem, self.base, self.n = eng, sem, 0, 0

    def step(self, ins):
        self.n += 1
        return ins.then_inc(self.sem, 1)

    def sync(self):
        self.eng.wait_ge(self.sem, self.base + self.n)

    def link(self, ins):
        self.step(ins)
        self.sync()

    def restart(self):
        self.sync()
        self.eng.drain()
        self.eng.sem_clear(self.sem)
        self.base = self.n = 0

    @contextmanager
    def loop(self, count, per):
        before = self.base + self.n
        with self.eng.Fori(0, count) as i:
            self.base, self.n = i * per + before, 0
            yield i
            assert self.n == per, f"{self.n} steps in a loop's body, {per} stated"
        self.base, self.n = before + count * per, 0


def view(ap, *dims):
    return bass.AP(tensor=ap.tensor, offset=ap.offset, ap=[list(ap.ap[0])] + [list(d) for d in dims])




def build(nc, x_in, wstream, consts, onehot, relb, par1, par2, rpb, experts, out):
    ctx = ExitStack()
    with ctx:
        def sb(name, shape, dt=F32):
            return ctx.enter_context(nc.sbuf_tensor(name, shape, dt))

        def sem(name):
            return ctx.enter_context(nc.semaphore(name))

        X = sb("x", [P, TT, D])
        HN = sb("h_norm", [P, TT, D])
        FH, FL = sb("feat_hi", [P, KC, S], F32R), sb("feat_lo", [P, KC, S], F32R)
        W = sb("weights", [P, SLOTS, HW])
        WH, WL = sb("weights_hi", [P, SLOTS, HW], F32R), sb("weights_lo", [P, SLOTS, HW], F32R)
        FGH, FGL = sb("ff_gated_hi", [P, 2, S], F32R), sb("ff_gated_lo", [P, 2, S], F32R)
        CONST = sb("consts", [P, C_END])
        PAR = sb("params", [P, max(P_END, Q_END)])
        SMALL = sb("small", [P, 512])
        ZERO = sb("zero", [P, 512], BF16)
        EIDX = sb("expert_idx", [P, 2, TOPK], U32)
        GWT = sb("expert_gate", [P, 2, TOPK])
        work = sb("work", [P, 16392])
        arena = sb("arena", [P, 12800])
        ps = ctx.enter_context(nc.psum_tensor("ps", [P, 8 * 512], F32))
        na_rows = nc.dram_tensor("na_rows", [LAYERS, P, NQ, NA_KK * GRID_W], F32).ap()
        scratch = nc.dram_tensor("bias_rows", [20, VAR * EW], F32).ap()

        def carve(region, at, *shape):
            n = int(np.prod(shape))
            v = region[:, at:at + n]
            if len(shape) > 1:
                names = "abcd"[:len(shape)]
                v = v.rearrange(f"p ({' '.join(names)}) -> p {' '.join(names)}",
                                **dict(zip(names, shape)))
            return v, at + n

        ident = CONST[:, C_ID:C_ID + P]
        turn = CONST[:, C_TURN:C_TURN + P]
        before = CONST[:, C_BM:C_BM + S]
        not_before = CONST[:, C_NB:C_NB + S]
        iota16 = CONST[:, C_IOTA:C_IOTA + TOPK]

        LG0, w0 = carve(work, 0, 2056)
        PT, w0 = carve(work, w0, 16, P)
        O, w0 = carve(work, w0, TT, D)
        LG = (LG0, work[:, w0:w0 + 2056])
        MT, w0 = carve(work, w0, KC, S)
        Y, w0 = carve(work, w0, TT, D)
        GT, w0 = carve(work, w0, 24, S)
        ring = work[:, 0:RING * 2 * D].rearrange("p (r n) -> p r n", r=RING)
        ffacc = work[:, 0:1024].rearrange("p (j g n) -> p j g n", j=2, g=2)
        ffp = work[:, 1024:1536].rearrange("p (j n) -> p j n", j=2)
        aqT, a0 = carve(arena, 0, 6, S)
        akT, a0 = carve(arena, a0, 6, S)
        av, a0 = carve(arena, a0, TT, 768)
        bqT, a0 = carve(arena, a0, 4, S)
        bkT, a0 = carve(arena, a0, S)
        bv, a0 = carve(arena, a0, TT, P)
        cqT, a0 = carve(arena, a0, 2, S)
        ckT, a0 = carve(arena, a0, 2, S)
        cv, a0 = carve(arena, a0, TT, S)
        bias_all = arena[:, a0:a0 + (A_H * A_G + B_H) * S]
        biasA, a0 = carve(arena, a0, A_H, A_G, S)
        biasB, a0 = carve(arena, a0, B_H, S)
        hankA, h0 = carve(work, 8200, A_H, A_G, S)
        hankB, h0 = carve(work, h0, B_H, S)
        hank = work[:, 8200:h0]
        BIAS_FILLS = (h0 - 8200) // 512
        erow, _ = carve(work, 0, VAR * EW)
        ohot, _ = carve(work, 2056, VAR * EW)
        relb_sb, _ = carve(work, 2056 + VAR * EW, 20)
        naB, b0 = carve(arena, 0, NQ, NA_KK * GRID_W)
        QK, b0 = carve(arena, b0, TT, QKW)
        qkT, b0 = carve(arena, b0, QK_HEADS // 2, S)
        va, b0 = carve(arena, b0, TT, NQ * HD)
        vb, b0 = carve(arena, b0, TT, P)
        rot, _ = carve(work, 0, 4, TT * 10 * 32)
        qksq, _ = carve(work, 2560, TT * QKW)
        pqT, c0 = carve(arena, 0, 16, S)
        SC, c0 = carve(arena, c0, ROUTES, 2, NKEY)
        keys, c0 = carve(arena, c0, 2, NKEY)
        cand, c0 = carve(arena, c0, TOPK * TOPK)
        eqA, c0 = carve(arena, c0, TOPK * TOPK)
        eqB, c0 = carve(arena, c0, TOPK * TOPK)
        sv, c0 = carve(arena, c0, 2, TOPK)
        siF, c0 = carve(arena, c0, 2, TOPK)
        topv, c0 = carve(arena, c0, TOPK)
        abF, c0 = carve(arena, c0, 2, TOPK)
        eF, c0 = carve(arena, c0, 2, TOPK)
        si = arena[:, c0:c0 + 2 * TOPK].bitcast(U32).rearrange("p (a k) -> p a k", k=TOPK)
        sel = arena[:, c0 + 2 * TOPK:c0 + 5 * TOPK].bitcast(U32).rearrange("p (a k) -> p a k", k=TOPK)
        ssq, std, rstd = SMALL[:, 0:2], SMALL[:, 2:4], SMALL[:, 4:6]
        negms, sums2, rsum = SMALL[:, 224:240], SMALL[:, 240:256], SMALL[:, 24:32]
        negm, sums = (negms[:, 0:8], negms[:, 8:16]), (sums2[:, 0:8], sums2[:, 8:16])
        hssq, hrstd = SMALL[:, 32:32 + 52], SMALL[:, 96:96 + 52]
        hd = SMALL[:, 160:160 + RING]
        ga = SMALL[:, 176:176 + RING]
        gw8 = SMALL[:, 192:192 + RING]
        lbase = SMALL[:, 208:209]
        esum, ersum, topneg = SMALL[:, 216:217], SMALL[:, 217:218], SMALL[:, 218:219]
        DIAG, _ = carve(arena, c0 + 5 * TOPK, RING, P)
        junk = HN

        def bank(b, n=1):
            return ps[:, b * 512:(b + n) * 512]

        def two(t, b):
            return t[:, 2 * b:2 * b + 2, :].rearrange("p c n -> p (c n)")

        x_loaded, const_loaded, par1_loaded, bias_in = sem("x_loaded"), sem("const_loaded"), sem("par1_loaded"), sem("bias_in")
        w_landed = [sem(f"w_landed{i}") for i in range(SLOTS)]
        half_done = sem("half_done")
        w_hi, w_lo = sem("w_hi"), sem("w_lo")
        heads_hi, mt_hi, mt_lo = sem("heads_hi"), sem("mt_hi"), sem("mt_lo")
        ff_prod, ff_hi = sem("ff_prod"), sem("ff_hi")
        proj_taken = sem("proj_taken")
        lproj_taken = sem("layer_proj_taken")
        merged = sem("merged")
        ff_taken = sem("ff_taken")
        wo_taken = sem("wo_taken")
        br_taken = sem("branch_taken")
        zeroed = sem("zeroed")
        erow_ready, erow_copied, erow_stored = sem("erow_ready"), sem("erow_copied"), sem("erow_stored")
        bias_loaded = sem("bias_loaded")
        bias_turned, bias_taken = sem("bias_turned"), sem("bias_taken")
        dve_step, route_step = sem("dve_step"), sem("route_step")
        x_ready = sem("x_ready")
        low_scores, llow_scores = sem("low_scores"), sem("layer_low_scores")
        scores_ready, logits_ready, probs_ready = sem("scores_ready"), sem("logits_ready"), sem("probs_ready")
        pT_ready, pT_taken = sem("pT_ready"), sem("pT_taken")
        lscores_ready, llogits_ready, lprobs_ready = sem("layer_scores_ready"), sem("layer_logits_ready"), sem("layer_probs_ready")
        lpT_ready, lpT_taken = sem("layer_pT_ready"), sem("layer_pT_taken")
        ff_init, ff_conv, ff_gelu, ff_gated = sem("ff_init"), sem("ff_conv"), sem("ff_gelu"), sem("ff_gated")
        out_stored = sem("out_stored")
        par2_loaded, na_loaded, na_stored = sem("par2_loaded"), sem("na_loaded"), sem("na_stored")
        qksq_ready, qkvar_ready, qkstd_ready, qk_ready = sem("qksq_ready"), sem("qkvar_ready"), sem("qkstd_ready"), sem("qk_ready")
        sc_done, sc_ready = sem("sc_done"), sem("sc_ready")
        topd_ready, texp_ready, routed, gates_ready = sem("topd_ready"), sem("texp_ready"), sem("routed"), sem("gates_ready")
        g_landed = [sem(f"g_landed{i}") for i in range(RING)]
        set_used = [sem(f"set_used{i}") for i in range(SETS)]
        dots_ready, gelu_ready, w_ready, diag_ready = sem("dots_ready"), sem("gelu_ready"), sem("w_ready"), sem("diag_ready")
        acc_ready = sem("acc_ready")
        pool_passed, dve_passed = sem("pool_waits_passed"), sem("dve_waits_passed")

        class Norm:

            def __init__(self, name):
                self.sq = sem(name + "_squares")
                self.var = sem(name + "_var")
                self.std = sem(name + "_std")
                self.hn = sem(name + "_normed")
                self.xp = sem(name + "_transposed")
                self.hi = sem(name + "_hi")
                self.hT = sem(name + "_hT")

        n_attn, n_post, n_ffn, n_fpost = Norm("n_attn"), Norm("n_post"), Norm("n_ffn"), Norm("n_fpost")
        n_mix, n_peer = Norm("n_mix"), Norm("n_peer")


        def norm_act(act, nm, src, l):
            for t in range(TT):
                ins = nc.scalar.activation(junk[:, t, :], src[:, t, :], ACT.Square, accum_out=ssq[:, t:t + 1])
            ins.then_inc(nm.sq, 1)
            act.wait_ge(nm.var, l + 1)
            nc.scalar.activation(std, ssq, ACT.Sqrt).then_inc(nm.std, 1)

        def norm_dve_rstd(dve, ch, nm, l):
            dve.wait_ge(nm.sq, l + 1)
            nc.vector.tensor_scalar(ssq, ssq, 1.0 / D, EPS, ALU.mult, ALU.add).then_inc(nm.var, 1)
            dve.wait_ge(nm.std, l + 1)
            ch.link(nc.vector.reciprocal(rstd, std))

        def norm_dve_pre(dve, ch, nm, l, gain_fm, gain_tok, first=None, at=0):
            norm_dve_rstd(dve, ch, nm, l)
            for t in range(TT):
                if gain_tok is None:
                    ins = nc.vector.tensor_scalar(HN[:, t, :], X[:, t, :], rstd[:, t:t + 1], None, ALU.mult)
                else:
                    ins = nc.vector.scalar_tensor_tensor(out=HN[:, t, :], in0=X[:, t, :], scalar=rstd[:, t:t + 1],
                                                         in1=gain_tok, op0=ALU.mult, op1=ALU.mult)
            ins.then_inc(nm.hn, 1)
            if first is not None:
                split_lo(dve, first, at)
            for b in range(4):
                dve.wait_ge(nm.hi, 4 * l + b + 1)
                if gain_fm is None:
                    ins = nc.vector.tensor_tensor(two(FL, b), bank(b), two(FH, b), ALU.subtract)
                else:
                    for c in (2 * b, 2 * b + 1):
                        ins = nc.vector.scalar_tensor_tensor(out=FL[:, c, :], in0=ps[:, c * S:(c + 1) * S], scalar=gain_fm[:, c:c + 1],
                                                             in1=FH[:, c, :], op0=ALU.mult, op1=ALU.subtract)
                ins.then_inc(nm.hT, 1)
            if first is not None:
                for n in range(first + 1, first + SLOTS):
                    split_lo(dve, n, at)

        def norm_act_hi(act, nm, l, gain_fm, first=None, at=0):
            if first is not None:
                split_hi(act, first, at)
            for b in range(4):
                act.wait_ge(nm.xp, 4 * l + b + 1)
                if gain_fm is None:
                    ins = nc.scalar.activation(two(FH, b), bank(b), ACT.Copy)
                else:
                    for c in (2 * b, 2 * b + 1):
                        ins = nc.scalar.activation(FH[:, c, :], ps[:, c * S:(c + 1) * S], ACT.Copy, scale=gain_fm[:, c:c + 1])
                ins.then_inc(nm.hi, 1)
            if first is not None:
                for n in range(first + 1, first + SLOTS):
                    split_hi(act, n, at)

        def norm_pe(pe, nm, l):
            pe.wait_ge(nm.hn, l + 1)
            for b in range(4):
                for c in (2 * b, 2 * b + 1):
                    for t in range(TT):
                        ins = nc.tensor.transpose(ps[:, c * S + t * P:c * S + (t + 1) * P],
                                                  HN[:, t, c * P:(c + 1) * P], ident)
                ins.then_inc(nm.xp, 1)

        def norm_dve_post(dve, ch, nm, gain):
            norm_dve_rstd(dve, ch, nm, 0)
            for t in range(TT):
                ch.step(nc.vector.scalar_tensor_tensor(out=Y[:, t, :], in0=Y[:, t, :], scalar=rstd[:, t:t + 1],
                                                       in1=gain, op0=ALU.mult, op1=ALU.mult))
            ch.sync()
            nc.vector.tensor_tensor(X[:, :, :], X[:, :, :], Y, ALU.add).then_inc(x_ready, 1)


        def split_hi(act, n, at=0):
            per = 0 if isinstance(at, int) else at.landed
            base = 0 if isinstance(at, int) else at.halves
            act.wait_ge(w_landed[n % SLOTS], per + 16 * (n // SLOTS + 1))
            if n >= SLOTS:
                act.wait_ge(half_done, base + n - SLOTS + 1)
            nc.scalar.activation(WH[:, n % SLOTS, :], W[:, n % SLOTS, :], ACT.Copy).then_inc(w_hi, 1)

        def split_lo(dve, n, at=0):
            base = 0 if isinstance(at, int) else at.halves
            dve.wait_ge(w_hi, base + n + 1)
            nc.vector.tensor_tensor(WL[:, n % SLOTS, :], W[:, n % SLOTS, :], WH[:, n % SLOTS, :], ALU.subtract).then_inc(w_lo, 1)

        def split_pe(pe, n, at=0):
            base = 0 if isinstance(at, int) else at.halves
            pe.wait_ge(w_lo, base + n + 1)
            return WH[:, n % SLOTS, :], WL[:, n % SLOTS, :]

        class At:

            def __init__(self, i, halves):
                self.halves, self.landed = i * halves, i * (16 * halves // SLOTS)

        def product(out, stat, mov, start, stop):
            nc.tensor.matmul(out, stat[0], mov[0], start=start, stop=False)
            nc.tensor.matmul(out, stat[0], mov[1], start=False, stop=False)
            return nc.tensor.matmul(out, stat[1], mov[0], start=False, stop=stop)

        def cols(pair, at, n):
            return tuple(x[:, at:at + n] for x in pair)

        def feat(c, at, n):
            return FH[:, c, at:at + n], FL[:, c, at:at + n]

        def group_fm(pe, g, b, at=0, parts=(range(KC),), also=None):
            for h in range(2):
                w = split_pe(pe, 2 * g + h, at)
                for j, chunks in enumerate(parts):
                    for c in chunks:
                        if also and h == 0:
                            also(c)
                        ins = product(ps[:, (b + j) * 512 + h * S:(b + j) * 512 + (h + 1) * S], cols(w, c * P, P), feat(c, 0, S),
                                      c == chunks[0], c == chunks[-1])
                ins.then_inc(half_done, 1)

        def group_tok(pe, g, b, at=0, also=None):
            nc.tensor.matmul(bank(b), ZERO[:, 0:P], ZERO[:, :], start=True, stop=False)
            for h in range(2):
                w = split_pe(pe, 2 * g + h, at)
                for t in range(TT):
                    for c in range(h * HC, (h + 1) * HC):
                        if also and t == 0:
                            also(c)
                        ins = product(ps[:, b * 512 + t * GC:b * 512 + (t + 1) * GC], feat(c, t * P, P), cols(w, c % HC * GC, GC),
                                      False, c == KC - 1 and t == TT - 1)
                ins.then_inc(half_done, 1)

        class Attn:

            def __init__(self, low, scores, logits, probs, pTr, pTt, batches, fills):
                self.low, self.scores, self.logits, self.probs = low, scores, logits, probs
                self.pTr, self.pTt = pTr, pTt
                self.batches, self.fills = batches, fills

        class Batch:

            def __init__(self, at, fill, rows, width, q, col, kind, bias=None, sink=None):
                self.at, self.fill, self.rows, self.width, self.q, self.col = at, fill, rows, width, q, col
                self.kind, self.bias, self.sink = kind, bias, sink
                self.n = len(rows)
                self.wide = width + (sink is not None)
                self.blocks = self.n * width // P
                self.copies = -(-self.blocks // 4)
                self.fills = self.copies + 1
                self.turn = at % 2
                self.L = LG[self.turn][:, 0:self.n * self.wide].rearrange("p (n w) -> p n w", n=self.n)
                self.ps = ps[:, 0:self.n * width].rearrange("p (n w) -> p n w", n=self.n)

        def scores_pe(pe, A, b, l=0):
            if b.at:
                pe.wait_ge(A.logits, l * A.batches + b.at)
            places = []
            for r, (pieces, _) in enumerate(b.rows):
                at = r * b.width
                for q, k in pieces:
                    places.append((q.base_partition(), at, q, k))
                    at += k.shape[-1]
            for part in (0, HD):
                for p, at, q, k in places:
                    if p == part:
                        ins = nc.tensor.matmul(ps[:, at:at + k.shape[-1]], q, k, start=True, stop=True)
                if part == 0:
                    ins.then_inc(A.low, 1)
                    pe.wait_ge(A.low, l * A.batches + b.at + 1)
            ins.then_inc(A.scores, 1)

        def transposes_pe(pe, A, fill, sources, l):
            for f in range(0, len(sources), 4):
                n = fill + f // 4
                if n >= 2:
                    pe.wait_ge(A.pTt, l * A.fills + n - 1)
                for j, src in enumerate(sources[f:f + 4]):
                    ins = nc.tensor.transpose(ps[:, (4 + n % 2) * 512 + j * P:(4 + n % 2) * 512 + (j + 1) * P], src, ident)
                ins.then_inc(A.pTr, 1)

        def transposed_dve(dve, A, fill, count, dst, l):
            for f in range(0, count, 4):
                n, m = fill + f // 4, min(4, count - f)
                dve.wait_ge(A.pTr, l * A.fills + n + 1)
                nc.vector.tensor_copy(dst[:, f * P:(f + m) * P], ps[:, (4 + n % 2) * 512:(4 + n % 2) * 512 + m * P]).then_inc(A.pTt, 1)

        def values_pe(pe, A, b, l=0):
            pe.wait_ge(A.probs, l * A.batches + b.at + 1)
            per = b.width // P
            transposes_pe(pe, A, b.fill, [b.L[:, r, k * P:(k + 1) * P] for r in range(b.n) for k in range(per)], l)
            pe.wait_ge(A.pTt, l * A.fills + b.fill + b.copies)
            out = bank(4 + (b.fill + b.copies) % 2)
            for r, (_, vals) in enumerate(b.rows):
                for k, v in enumerate(vals):
                    ins = nc.tensor.matmul(out[:, r * HD:(r + 1) * HD], PT[:, r * per + k, :], v,
                                           start=k == 0, stop=k == per - 1)
            ins.then_inc(A.pTr, 1)

        def logits_dve(dve, ch, A, b, l=0):
            if b.sink is not None:
                ch.step(nc.vector.tensor_copy(b.L[:, :, b.width:], b.sink.unsqueeze(2)))
            dve.wait_ge(A.scores, l * A.batches + b.at + 1)
            src, dst, bias = b.ps, b.L[:, :, 0:b.width], b.bias
            if len(bias.shape) == 3 and bias.shape[1] != b.n:
                src = ps[:, 0:b.n * b.width].rearrange("p (n w) -> p n w", n=bias.shape[1])
                dst = LG[b.turn][:, 0:b.n * b.width].rearrange("p (n w) -> p n w", n=bias.shape[1])
            ch.link(nc.vector.scalar_tensor_tensor(out=dst, in0=src, scalar=SCALE, in1=bias,
                                                   op0=ALU.mult, op1=ALU.add))
            nc.vector.tensor_reduce(negm[b.turn][:, 0:b.n], b.L, AX.X, ALU.max, negate=True).then_inc(A.logits, 1)

        def probs_act(act, A, b, l=0):
            act.wait_ge(A.logits, l * A.batches + b.at + 1)
            for r in range(b.n):
                ins = nc.scalar.activation(b.L[:, r, :], b.L[:, r, :], ACT.Exp, bias=negm[b.turn][:, r:r + 1],
                                           accum_out=sums[b.turn][:, r:r + 1])
            ins.then_inc(A.probs, 1)

        def heads_dve(dve, ch, A, b, l=0):
            transposed_dve(dve, A, b.fill, b.blocks, PT.rearrange("p k n -> p (k n)"), l)
            if b.kind == "softmax":
                ch.link(nc.vector.reciprocal(rsum[:, 0:b.n], sums[b.turn][:, 0:b.n]))
            n = b.fill + b.copies
            dve.wait_ge(A.pTr, l * A.fills + n + 1)
            dst, src = O[:, b.q, b.col:b.col + b.n * HD], bank(4 + n % 2)[:, 0:b.n * HD]
            if b.kind == "softmax":
                nc.vector.tensor_tensor(dst.rearrange("p (n d) -> p n d", n=b.n), src.rearrange("p (n d) -> p n d", n=b.n),
                                        view(rsum, [1, b.n], [0, HD]), ALU.mult).then_inc(A.pTt, 1)
            else:
                nc.vector.tensor_copy(dst, src).then_inc(A.pTt, 1)

        beta, keeps = LG, HN

        def stick_act(act, A, b):
            act.wait_ge(A.scores, b.at + 1)
            n = b.n * b.width
            nc.scalar.activation(beta[b.turn][:, 0:n], ps[:, 0:n], ACT.Sigmoid, scale=SCALE)
            nc.scalar.activation(keeps[:, b.turn, 0:n], ps[:, 0:n], ACT.Sigmoid, scale=-SCALE).then_inc(A.logits, 1)

        def stick_dve(dve, ch, A, b):
            n, w = b.n * b.width, b.width
            prod = Y.rearrange("p t d -> p (t d)")[:, 8:8 + b.n * (w + 1)].rearrange("p (n w) -> p n w", n=b.n)
            zeros = Y.rearrange("p t d -> p (t d)")[:, 1100:1100 + w]
            ch.step(nc.vector.memset(prod[:, :, w:], 1.0))
            ch.step(nc.vector.memset(zeros, 0.0))
            dve.wait_ge(A.logits, b.at + 1)
            k3 = keeps[:, b.turn, 0:n].rearrange("p (n w) -> p n w", n=b.n)
            mask = not_before[:, S - w:S]
            ch.link(nc.vector.tensor_tensor(k3, k3, view(mask, [0, b.n], [1, w]), ALU.max))
            for r in range(b.n):
                ch.step(nc.vector.tensor_tensor_scan(prod[:, r, 0:w][:, ::-1], k3[:, r, ::-1], zeros, 1.0,
                                                     ALU.mult, ALU.add))
            ch.sync()
            b3 = beta[b.turn][:, 0:n].rearrange("p (n w) -> p n w", n=b.n)
            ch.link(nc.vector.tensor_tensor(b3, b3, prod[:, :, 1:], ALU.mult))
            mask = before[:, S - w:S]
            nc.vector.tensor_tensor(b3, b3, view(mask, [0, b.n], [1, w]), ALU.mult).then_inc(A.probs, 1)

        def heads_parts(eng, A, fill, l):
            for f in range(4):
                n = fill + f
                src = bank(4 + n % 2)
                if eng is nc.scalar:
                    eng.wait_ge(A.pTr, l * A.fills + n + 1)
                    nc.scalar.activation(two(FH, f), src, ACT.Copy).then_inc(heads_hi, 1)
                else:
                    eng.wait_ge(heads_hi, l * 4 + (0 if isinstance(l, int) else 4) + f + 1)
                    nc.vector.tensor_tensor(two(FL, f), src, two(FH, f), ALU.subtract).then_inc(A.pTt, 1)

        def branches_pe(pe, A, fill, g0, parts, l=0, at=0):
            transposes_pe(pe, A, fill, [O[:, t, c * P:(c + 1) * P] for c in range(KC) for t in range(TT)], l)
            pe.wait_ge(A.pTt, l * A.fills + fill + 4)
            for g in range(BR):
                if g >= 2:
                    pe.wait_ge(br_taken, g - 1 if isinstance(l, int) else l * BR + BR + g - 1)
                group_fm(pe, g0 + g, 3 * (g % 2), at, parts=parts)

        def merge_act(act, A, fill, g0, l=0, at=0):
            heads_parts(nc.scalar, A, fill, l)
            for n in range(2 * g0, 2 * (g0 + BR)):
                split_hi(act, n + SLOTS, at)
            for g in range(BR):
                act.wait_ge(merged, g + 1 if isinstance(l, int) else l * BR + BR + g + 1)
                nc.scalar.activation(two(FH, g), two(MT, g), ACT.Copy).then_inc(mt_hi, 1)

        def merge_dve(dve, ch, A, fill, g0, n_br, gates, l=0, at=0):
            heads_parts(nc.vector, A, fill, l)
            dve.wait_ge(*gates)
            done = 0 if isinstance(l, int) else l * BR + BR

            def merge(g):
                base = 0 if isinstance(at, int) else at.halves
                dve.wait_ge(half_done, base + 2 * (g0 + g) + 2)
                b = 3 * (g % 2)
                dst = two(MT, g)
                tmp = PT.rearrange("p k n -> p (k n)")[:, (g % 2) * 1024:(g % 2) * 1024 + (n_br - 1) * 512]
                for j in range(n_br):
                    ins = nc.vector.tensor_tensor(dst if j == 0 else tmp[:, (j - 1) * 512:j * 512], bank(b + j),
                                                  two(GT[:, KC * j:KC * (j + 1), :], g), ALU.mult)
                    if j < n_br - 1:
                        ch.step(ins)
                ins.then_inc(br_taken, 1)
                dve.wait_ge(br_taken, done + g + 1)
                ch.sync()
                for j in range(1, n_br):
                    ins = nc.vector.tensor_tensor(dst, dst, tmp[:, (j - 1) * 512:j * 512], ALU.add)
                    if j < n_br - 1:
                        ch.link(ins)
                ins.then_inc(merged, 1)

            def lower(g):
                dve.wait_ge(mt_hi, done + g + 1)
                nc.vector.tensor_tensor(two(FL, g), two(MT, g), two(FH, g), ALU.subtract).then_inc(mt_lo, 1)

            for g in range(BR):
                for n in range(2 * (g0 + g), 2 * (g0 + g) + 2):
                    split_lo(dve, n + SLOTS, at)
                if g == BR - 1:
                    for e in range(BR - 1):
                        lower(e)
                merge(g)
            lower(BR - 1)

        def wo_pe(pe, gates, g0, l=0, at=0):
            done = 0 if isinstance(l, int) else l * BR + BR
            for g in range(WO):
                if g >= 2:
                    pe.wait_ge(wo_taken, g - 1 if isinstance(l, int) else l * (WO - 1) + WO + g - 1)
                else:
                    pe.wait_ge(*gates)
                group_tok(pe, g0 + g, 6 + g % 2, at,
                          also=(lambda c: c % 2 or pe.wait_ge(mt_lo, done + c // 2 + 1)) if g == 0 else None)

        AT1 = Attn(low_scores, scores_ready, logits_ready, probs_ready, pT_ready, pT_taken, 7, 0)
        batches1 = []

        def add1(**kw):
            batches1.append(Batch(len(batches1), sum(b.fills for b in batches1), **kw))

        def half(tile3, c, h, sl):
            return tile3[HD * h:HD * (h + 1), c, sl]

        def rows_a(heads, q):
            rows = []
            for h in heads:
                hs = [(g * A_H + h) for g in range(A_G)]
                rows.append(([(half(aqT, j // 2, j % 2, slice(q * P, (q + 1) * P)),
                               half(akT, j // 2, j % 2, slice(0, (q + 1) * P))) for j in hs],
                             [av[:, k, j * HD:(j + 1) * HD] for j in hs for k in range(q + 1)]))
            return rows

        a_blocks = biasA.rearrange("p h g w -> p (h g) w")
        add1(rows=rows_a(range(4), 0), width=3 * P, q=0, col=0, kind="softmax", bias=a_blocks[:, :, P:S])
        for h in (0, 2):
            add1(rows=rows_a((h, h + 1), 1), width=3 * S, q=1, col=h * HD, kind="softmax",
                 bias=a_blocks[:, 3 * h:3 * h + 6, :])
        for q in range(TT):
            rows = [([(half(bqT, h % 4, h // 4, slice(q * P, (q + 1) * P)),
                       bkT[HD * (h // 4):HD * (h // 4 + 1), 0:(q + 1) * P])],
                     [bv[:, k, HD * (h // 4):HD * (h // 4 + 1)] for k in range(q + 1)]) for h in range(B_H)]
            add1(rows=rows, width=(q + 1) * P, q=q, col=A_H * HD, kind="softmax",
                 bias=biasB[:, :, (1 - q) * P:S], sink=PAR[:, P_SK:P_SK + B_H])
        for q in range(TT):
            rows = [([(half(cqT, h // 2, h % 2, slice(q * P, (q + 1) * P)),
                       half(ckT, h // 2, h % 2, slice(0, (q + 1) * P)))],
                     [cv[:, k, h * HD:(h + 1) * HD] for k in range(q + 1)]) for h in range(C_H)]
            add1(rows=rows, width=(q + 1) * P, q=q, col=(A_H + B_H) * HD, kind="stick")
        fill_o1 = sum(b.fills for b in batches1)

        order1 = ["G"] * 9 + ["B"]
        for b in batches1:
            order1 += ["G", ("S", b), "G"] + ([("V", batches1[b.at - 1])] if b.at else [])
        order1 += ["G"] * (IN_QKV + IN_GATE - order1.count("G")) + [("V", batches1[-1])]

        FILL_QKT = 7
        batches2 = []
        for kind in range(2):
            for q in range(TT):
                rows = []
                for h in range(NQ):
                    if kind == 0:
                        c, k, part = h // 2, 4 + h // 2, h % 2
                        vals = [va[:, t, h * HD:(h + 1) * HD] for t in range(TT)]
                    else:
                        c, k, part = 8 + h % 4, 12, h // 4
                        vals = [vb[:, t, HD * part:HD * (part + 1)] for t in range(TT)]
                    rows.append(([(half(qkT, c, part, slice(q * P, (q + 1) * P)), half(qkT, k, part, slice(0, S)))], vals))
                if kind == 0:
                    bias, sink = naB[:, :, (2 - 2 * q) * GRID_W:(2 - 2 * q) * GRID_W + S], None
                else:
                    bias = view(CONST[:, C_SW + q * S:C_SW + q * S + S], [0, NQ], [1, S])
                    sink = PAR[:, Q_SK:Q_SK + NQ]
                batches2.append(Batch(len(batches2), FILL_QKT + sum(b.fills for b in batches2), rows=rows, width=S, q=q,
                                      col=kind * NQ * HD, kind="softmax", bias=bias, sink=sink))
        fill_o2 = FILL_QKT + sum(b.fills for b in batches2)
        L_FILLS = fill_o2 + 4
        AT2 = Attn(llow_scores, lscores_ready, llogits_ready, lprobs_ready, lpT_ready, lpT_taken, 4, L_FILLS)
        order2 = ["G"] * (L_PROJ + 2) + ["Q", ("S", batches2[0]), "G"]
        for b in batches2[1:]:
            order2 += ["G"] * (b.at == 1) + [("S", b), "G"] + [("V", batches2[b.at - 1])] + ["G"] * (b.at == 2)
        order2 += [("V", batches2[-1])]
        assert order2.count("G") == L_PROJ + L_GATE
        N2 = L_PROJ + L_GATE + L_PQ

        block = ctx.enter_context(nc.Block())

        @block.sync
        def _(sp):
            sp.dma_start(X[:, :, :], x_in.rearrange("(t p) d -> p t d", p=P)).then_inc(x_loaded, 16)
            sp.dma_start(CONST[:, :], consts).then_inc(const_loaded, 16)
            for n in range(SLOTS):
                sp.dma_start(W[:, n, :], wstream[n]).then_inc(w_landed[n], 16)
            whole = (HALVES - SLOTS) // SLOTS
            with sp.Fori(0, whole) as k:
                for s in range(SLOTS):
                    sp.wait_ge(w_lo, k * SLOTS + s + 1)
                    sp.dma_start(W[:, s, :], wstream[k * SLOTS + SLOTS + s]).then_inc(w_landed[s], 16)
            for n in range(SLOTS + whole * SLOTS, HALVES):
                sp.wait_ge(w_lo, n - SLOTS + 1)
                sp.dma_start(W[:, n % SLOTS, :], wstream[n]).then_inc(w_landed[n % SLOTS], 16)
            sp.wait_ge(x_ready, 2 + 3 * LAYERS)
            sp.dma_start(out.rearrange("(t p) d -> p t d", p=P), X[:, :, :]).then_inc(out_stored, 16)
            sp.wait_ge(out_stored, 16)

        @block.gpsimd
        def _(pool):
            nc.gpsimd.memset(ZERO[:, :], 0.0)
            nc.gpsimd.memset(lbase, 0.0).then_inc(zeroed, 1)
            for l in range(LAYERS):
                for r in range(2):
                    for h in range(NQ):
                        at = ((l * NQ + h) * RPB_R + 5 - r) * GRID_W * RPB_PAD + GRID_W - 1
                        pool.dma_start(na_rows[l, r * GRID_W:(r + 1) * GRID_W, h, :].rearrange("p (k n) -> p k n", k=NA_KK),
                                       bass.AP(tensor=rpb.tensor, offset=at, ap=[[RPB_PAD - 1, GRID_W], [GRID_W * RPB_PAD, NA_KK], [1, GRID_W]])).then_inc(na_stored, 16)
            with pool.Fori(0, LAYERS) as l:
                with pool.Fori(0, STEPS // 2) as i:
                    for b in range(2):
                        wait_alone(pool, routed, l * ROUTES + i * 2 + b + 1, pool_passed)
                        for c in range(PASSES):
                            use = l * USES + i * (2 * PASSES) + b * PASSES + c
                            for q in range(SETS):
                                wait_alone(pool, set_used[q], use + 1, pool_passed)
                                for r in range(q * SET, (q + 1) * SET):
                                    nc.gpsimd.indirect_dma_start(
                                        ring[:, r, :], None, experts,
                                        bass.IndirectOffsetOnAxis(ap=EIDX[:, b, c * RING + r:c * RING + r + 1], axis=0)).then_inc(g_landed[r], 16)

        @block.tensor
        def _(pe):
            for q in range(SETS):
                pe.sem_inc(set_used[q], 1)
            pe.wait_ge(bias_in, 32)
            for v in range(VAR):
                ins = nc.tensor.matmul(ps[0:20, v * 512:v * 512 + EW], relb_sb[0:NB_BUCKETS + 1, :],
                                       ohot[0:NB_BUCKETS + 1, v * EW:(v + 1) * EW], start=True, stop=True)
            ins.then_inc(erow_ready, 1)
            pe.wait_ge(const_loaded, 16)
            pe.wait_ge(zeroed, 1)
            pe.wait_ge(erow_copied, 1)
            norm_pe(pe, n_attn, 0)
            g = 0
            for what in order1:
                if what == "G":
                    if g >= 2:
                        pe.wait_ge(proj_taken, g - 1)
                    token_major = g in TOK_1
                    if g == 11:
                        b = (6 + g % 2) * 512
                        for h in range(2):
                            w = split_pe(pe, 2 * g + h)
                            for t in range(h * TT + 1 - h):
                                for c in range(KC):
                                    out = ps[:, b:b + S] if h == 0 else ps[:, b + S + t * P:b + S + (t + 1) * P]
                                    k = feat(c, 0, S) if h == 0 else feat(c, t * P, P)
                                    stat, mov = (cols(w, c * P, P), k) if h == 0 else (k, cols(w, c * P, P))
                                    ins = product(out, stat, mov, c == 0, c == KC - 1)
                            ins.then_inc(half_done, 1)
                    elif token_major:
                        group_tok(pe, g, 6 + g % 2)
                    else:
                        group_fm(pe, g, 6 + g % 2, also=(lambda c: c % 2 or pe.wait_ge(n_attn.hT, c // 2 + 1)) if g == 0 else None)
                    g += 1
                elif what == "B":
                    pe.wait_ge(bias_loaded, 64)
                    for n in range(BIAS_FILLS):
                        if n >= 4:
                            pe.wait_ge(bias_taken, n - 3)
                        nc.tensor.matmul(bank(n % 4), turn, hank[:, n * 512:(n + 1) * 512], start=True, stop=True).then_inc(bias_turned, 1)
                    pe.wait_ge(bias_taken, BIAS_FILLS)
                elif what[0] == "S":
                    b = what[1]
                    pe.wait_ge(proj_taken, 9 if b.at < 3 else 12 if b.at < 5 else 15)
                    scores_pe(pe, AT1, b)
                else:
                    values_pe(pe, AT1, what[1])
            pe.wait_ge(pT_taken, fill_o1)
            branches_pe(pe, AT1, fill_o1, G_BR, (range(0, 2), range(2, 6), range(6, 8)))
            wo_pe(pe, (proj_taken, IN_QKV + IN_GATE), G_WO)
            norm_pe(pe, n_ffn, 0)
            pe.wait_ge(n_ffn.hT, 4)
            for b in range(4):
                nc.tensor.matmul(bank(b), ZERO[:, 0:P], ZERO[:, :], start=True, stop=False)

            def down(n, at, last):
                for j in range(2):
                    w = split_pe(pe, n + j, at)
                    for t in range(TT):
                        for h in range(2):
                            ins = product(bank(2 * t + h), cols((FGH[:, j, :], FGL[:, j, :]), t * P, P), cols(w, h * 512, 512),
                                          False, last and j == 1)
                    ins.then_inc(half_done, 1)

            for j in range(2):
                group_fm(pe, G_FF + j, 6 + j)
            with pe.Fori(0, FF_BLOCKS // 2 - 1) as i:
                at = At(i, F_BODY)
                for j in range(2):
                    pe.wait_ge(ff_conv, i * 2 + j + 1)
                    group_fm(pe, G_FF + 2 + j, 6 + j, at)
                pe.wait_ge(ff_gated, i * 2 + 2)
                down(F_HALF + 8, at, False)
            pe.wait_ge(ff_gated, FF_BLOCKS)
            down(L_HALF - 2, 0, True)

            with pe.Fori(0, LAYERS) as l:
                at = At(l, L_HALVES)
                norm_pe(pe, n_mix, l)
                g = 0
                for what in order2:
                    if what == "G":
                        if g >= 2:
                            pe.wait_ge(lproj_taken, l * N2 + g - 1)
                        (group_tok if g < L_PROJ else group_fm)(pe, G_LAYER + g, 6 + g % 2, at, also=(
                            lambda c: c % 2 or pe.wait_ge(n_mix.hT, l * 4 + c // 2 + 1)) if g == 0 else None)
                        g += 1
                    elif what == "Q":
                        pe.wait_ge(qk_ready, l + 1)
                        transposes_pe(pe, AT2, 0, [QK[:, t, c * P:(c + 1) * P] for c in range(QK_HEADS // 2) for t in range(TT)], l)
                        pe.wait_ge(lpT_taken, l * L_FILLS + FILL_QKT)
                        pe.wait_ge(lproj_taken, l * N2 + L_PROJ)
                    elif what[0] == "S":
                        scores_pe(pe, AT2, what[1], l)
                    else:
                        values_pe(pe, AT2, what[1], l)
                pe.wait_ge(lpT_taken, l * L_FILLS + fill_o2)
                branches_pe(pe, AT2, fill_o2, G_LAYER + LG_BR, (range(0, 4), range(4, 8)), l, at)
                wo_pe(pe, (lproj_taken, l * N2 + L_PROJ + L_GATE), G_LAYER + LG_WO, l, at)
                norm_pe(pe, n_peer, l)

                def key_scores(h):
                    pe.wait_ge(lproj_taken, l * N2 + L_PROJ + L_GATE + h + 1)
                    if h >= 2:
                        pe.wait_ge(sc_ready, l * PH + h - 1)
                    for t in range(TT):
                        for s in range(2):
                            ins = nc.tensor.matmul(ps[:, (4 + h % 2) * 512 + (t * 2 + s) * NKEY:(4 + h % 2) * 512 + (t * 2 + s + 1) * NKEY],
                                                   pqT[:, 2 * h + s, t * P:(t + 1) * P],
                                                   PAR[:, Q_KEYS + s * NKEY:Q_KEYS + (s + 1) * NKEY], start=True, stop=True)
                    ins.then_inc(sc_done, 1)

                for j in range(L_PQ):
                    if j >= 2:
                        pe.wait_ge(lproj_taken, l * N2 + L_PROJ + L_GATE + j - 1)
                    group_fm(pe, G_LAYER + LG_PQ + j, 6 + j % 2, at, also=(
                        lambda c: c % 2 or pe.wait_ge(n_peer.hT, l * 4 + c // 2 + 1)) if j == 0 else None)
                    if j >= 1:
                        key_scores(j - 1)
                key_scores(PH - 1)
                for t in range(TT):
                    for h in range(2):
                        nc.tensor.matmul(bank(2 * t + h), ZERO[:, 0:P], ZERO[:, :], start=True, stop=False)
                    with pe.Fori(0, PH * PASSES) as i:
                        use = l * USES + i + t * PH * PASSES
                        for q in range(SETS):
                            pe.wait_ge(diag_ready, use * SETS + q + 1)
                            for r in range(q * SET, (q + 1) * SET):
                                for h in range(2):
                                    ins = nc.tensor.matmul(bank(2 * t + h), DIAG[:, r, :], ring[:, r, D + h * 512:D + (h + 1) * 512],
                                                           start=False, stop=False)
                            ins.then_inc(set_used[q], 1)
                    for h in range(2):
                        ins = nc.tensor.matmul(bank(2 * t + h), ZERO[:, 0:P], ZERO[:, :], start=False, stop=True)
                    ins.then_inc(acc_ready, 1)

        @block.scalar
        def _(act):
            act.dma_start(relb_sb[0:NB_BUCKETS + 1, :], relb).then_inc(bias_in, 16)
            act.dma_start(ohot[0:NB_BUCKETS + 1, :], onehot).then_inc(bias_in, 16)
            act.dma_start(PAR[:, 0:P_END], par1).then_inc(par1_loaded, 16)
            act.wait_ge(erow_ready, 1)
            for v in range(VAR):
                ins = nc.scalar.activation(erow[0:20, v * EW:(v + 1) * EW], ps[0:20, v * 512:v * 512 + EW], ACT.Copy)
            ins.then_inc(erow_copied, 1)
            act.wait_ge(erow_copied, 1)
            act.dma_start(scratch, erow[0:20, :]).then_inc(erow_stored, 16)
            act.wait_ge(x_loaded, 16)
            norm_act(act, n_attn, X, 0)
            act.wait_ge(erow_stored, 16)
            for gi in range(A_G):
                act.dma_start(hankA[:, :, gi, :], bass.AP(tensor=scratch.tensor, offset=gi * A_H * VAR * EW + gi * EW,
                                                          ap=[[1, P], [VAR * EW, A_H], [1, S]])).then_inc(bias_loaded, 16)
            act.dma_start(hankB, bass.AP(tensor=scratch.tensor, offset=A_G * A_H * VAR * EW + 3 * EW,
                                         ap=[[1, P], [VAR * EW, B_H], [1, S]])).then_inc(bias_loaded, 16)
            act.wait_ge(par1_loaded, 16)
            norm_act_hi(act, n_attn, 0, PAR[:, P_G1:P_G1 + KC], first=0)

            def take1(g):
                act.wait_ge(half_done, 2 * g + 2)
                src = bank(6 + g % 2)
                t2 = src.rearrange("p (t n) -> p t n", t=TT)
                if g < 3:
                    ins = nc.scalar.activation(aqT[:, 2 * g:2 * g + 2, :], t2, ACT.Copy)
                elif g < 6:
                    ins = nc.scalar.activation(akT[:, 2 * g - 6:2 * g - 4, :], t2, ACT.Copy)
                elif g < 9:
                    ins = nc.scalar.activation(av[:, :, (g - 6) * GC:(g - 5) * GC], t2, ACT.Copy)
                elif g < 11:
                    ins = nc.scalar.activation(bqT[:, 2 * (g - 9):2 * (g - 8), :], t2, ACT.Copy)
                elif g == 11:
                    nc.scalar.activation(bkT, src[:, 0:S], ACT.Copy)
                    ins = nc.scalar.activation(bv, src[:, S:2 * S].rearrange("p (t n) -> p t n", t=TT), ACT.Copy)
                elif g < 15:
                    ins = nc.scalar.activation((cqT, ckT, cv)[g - 12], t2, ACT.Copy)
                else:
                    for j in range(2):
                        f = 2 * (g - G_GATE) + j
                        ins = nc.scalar.activation(GT[:, f, :], t2[:, j, :], ACT.Sigmoid, bias=PAR[:, P_BG + f:P_BG + f + 1])
                ins.then_inc(proj_taken, 1)

            g = 0
            for k, what in enumerate(order1):
                if what == "G":
                    split_hi(act, 2 * g + SLOTS)
                    if k and order1[k - 1][0] == "S":
                        b = order1[k - 1][1]
                        if b.kind == "softmax":
                            probs_act(act, AT1, b)
                        else:
                            stick_act(act, AT1, b)
                    split_hi(act, 2 * g + 1 + SLOTS)
                    take1(g)
                    g += 1
            merge_act(act, AT1, fill_o1, G_BR)
            for n in range(2 * G_WO, 2 * (G_WO + WO)):
                split_hi(act, n + SLOTS)
            act.wait_ge(wo_taken, WO)
            norm_act(act, n_post, Y, 0)
            act.wait_ge(x_ready, 1)
            norm_act(act, n_ffn, X, 0)
            norm_act_hi(act, n_ffn, 0, PAR[:, P_G2:P_G2 + KC])

            def ff_init_act(j, cvw, done):
                act.wait_ge(half_done, done)
                for gv in range(2):
                    ins = nc.scalar.activation(ffacc[:, j, gv, :], bank(6 + j)[:, gv * S:(gv + 1) * S], ACT.Identity,
                                               scale=cvw(gv, 2), bias=cvw(gv, 3))
                ins.then_inc(ff_init, 1)

            def ff_gelu_act(blk, j):
                act.wait_ge(ff_conv, blk + 1)
                nc.scalar.activation(ffacc[:, j, 0, :], ffacc[:, j, 0, :], ACT.Gelu_apprx_tanh).then_inc(ff_gelu, 1)

            def static_taps(n):
                return lambda gv, k: PAR[:, P_CV + n * 8 + gv * 4 + k:P_CV + n * 8 + gv * 4 + k + 1]

            split_hi(act, F_HALF + 3)
            for j in range(2):
                ff_init_act(j, static_taps(j), F_HALF + 2 * j + 2)
                split_hi(act, F_HALF + 4 + j)
                ff_gelu_act(j, j)
            with act.Fori(0, FF_BLOCKS // 2 - 1) as i:
                at = At(i, F_BODY)
                split_hi(act, F_HALF + 6, at)
                for j in range(2):
                    def taps(gv, k):
                        return PAR[:, bass.ds(i * 16 + (P_CV + 16 + j * 8 + gv * 4 + k), 1)]
                    split_hi(act, F_HALF + 7 + 2 * j, at)
                    act.wait_ge(ff_prod, i * 2 + j + 1)
                    ff_init_act(j, taps, at.halves + F_HALF + 6 + 2 * j)
                    split_hi(act, F_HALF + 8 + 2 * j, at)
                    ff_gelu_act(i * 2 + 2 + j, j)
                split_hi(act, F_HALF + 11, at)
            act.wait_ge(ff_taken, 1)
            norm_act(act, n_fpost, Y, 0)

            act.wait_ge(na_stored, LAYERS * 2 * NQ * 16)
            with act.Fori(0, LAYERS) as l:
                act.wait_ge(x_ready, l * 3 + 2)
                act.dma_start(PAR[:, 0:Q_END], par2[l]).then_inc(par2_loaded, 16)
                act.dma_start(naB, na_rows[l]).then_inc(na_loaded, 16)
                at = At(l, L_HALVES)
                norm_act(act, n_mix, X, l)
                act.wait_ge(par2_loaded, l * 16 + 16)
                norm_act_hi(act, n_mix, l, PAR[:, Q_G:Q_G + KC], first=L_HALF, at=at)

                def take2(g):
                    act.wait_ge(half_done, at.halves + L_HALF + 2 * g + 2)
                    t2 = bank(6 + g % 2).rearrange("p (t n) -> p t n", t=TT)
                    if g < 6:
                        ins = nc.scalar.activation(QK[:, :, g * GC:(g + 1) * GC], t2, ACT.Copy)
                    elif g == 6:
                        nc.scalar.activation(QK[:, :, 6 * GC:6 * GC + P], t2[:, :, 0:P], ACT.Copy)
                        ins = nc.scalar.activation(vb, t2[:, :, P:2 * P], ACT.Copy)
                    elif g < 9:
                        ins = nc.scalar.activation(va[:, :, (g - 7) * GC:(g - 6) * GC], t2, ACT.Copy)
                    else:
                        for j in range(2):
                            f = 2 * (g - L_PROJ) + j
                            ins = nc.scalar.activation(GT[:, f, :], t2[:, j, :], ACT.Sigmoid, bias=PAR[:, Q_BG + f:Q_BG + f + 1])
                    ins.then_inc(lproj_taken, 1)
                    if g == 6:
                        act.wait_ge(lproj_taken, l * N2 + 7)
                        nc.scalar.activation(qksq, QK.rearrange("p t n -> p (t n)"), ACT.Square).then_inc(qksq_ready, 1)
                        act.wait_ge(qkvar_ready, l + 1)
                        nc.scalar.activation(hrstd, hssq, ACT.Sqrt).then_inc(qkstd_ready, 1)

                g = 0
                for k, what in enumerate(order2):
                    if what == "G":
                        split_hi(act, L_HALF + 2 * g + SLOTS, at)
                        if k and order2[k - 1][0] == "S":
                            probs_act(act, AT2, order2[k - 1][1], l)
                        split_hi(act, L_HALF + 2 * g + 1 + SLOTS, at)
                        take2(g)
                        g += 1
                merge_act(act, AT2, fill_o2, G_LAYER + LG_BR, l, at)
                for n in range(2 * LG_WO, 2 * LG_PQ):
                    split_hi(act, L_HALF + n + SLOTS, at)
                act.wait_ge(x_ready, l * 3 + 3)
                norm_act(act, n_peer, X, l)
                norm_act_hi(act, n_peer, l, None)

                def gate_exp(k):
                    act.wait_ge(topd_ready, l * ROUTES + k + 1)
                    nc.scalar.activation(topv, topv, ACT.Exp, bias=topneg, accum_out=esum).then_inc(texp_ready, 1)

                def take_scores(h):
                    act.wait_ge(sc_done, l * PH + h + 1)
                    nc.scalar.activation(SC[:, 0:STEPS, :, :].rearrange("p (t h) s n -> p t h (s n)", h=PH)[:, :, h, :],
                                         bank(4 + h % 2).rearrange("p (t n) -> p t n", t=TT), ACT.Copy).then_inc(sc_ready, 1)

                for j in range(L_PQ):
                    for n in range(2 * (LG_PQ + j) + SLOTS, min(2 * (LG_PQ + j) + SLOTS + 2, L_HALVES)):
                        split_hi(act, L_HALF + n, at)
                    act.wait_ge(half_done, at.halves + L_HALF + 2 * (LG_PQ + j) + 2)
                    nc.scalar.activation(pqT[:, 2 * j:2 * j + 2, :], bank(6 + j % 2).rearrange("p (t n) -> p t n", t=TT),
                                         ACT.Copy).then_inc(lproj_taken, 1)
                    if j >= 1:
                        take_scores(j - 1)
                    if j == 3:
                        gate_exp(0)
                take_scores(PH - 1)

                for t in range(TT):
                    with act.Fori(0, PH) as i:
                        for c in range(PASSES):
                            use = l * USES + i * PASSES + t * PH * PASSES + c

                            def gelu(q):
                                act.wait_ge(dots_ready, use * SETS + q + 1)
                                nc.scalar.activation(ga[:, q * SET:(q + 1) * SET], hd[:, q * SET:(q + 1) * SET], ACT.Gelu).then_inc(gelu_ready, 1)

                            def diagonals(q):
                                act.wait_ge(w_ready, use * SETS + q + 1)
                                for r in range(q * SET, (q + 1) * SET):
                                    ins = nc.scalar.activation(DIAG[:, r, :], ident, ACT.Copy, scale=gw8[:, r:r + 1])
                                ins.then_inc(diag_ready, 1)

                            gelu(0)
                            for q in range(1, SETS):
                                if c == 0 and q == SETS - 1:
                                    gate_exp(i + t * PH + 1)
                                gelu(q)
                                diagonals(q - 1)
                            diagonals(SETS - 1)

        @block.vector
        def _(dve):
            ch = Chain(dve, dve_step)
            dve.wait_ge(x_loaded, 16)
            dve.wait_ge(par1_loaded, 16)
            dve.wait_ge(const_loaded, 16)
            norm_dve_pre(dve, ch, n_attn, 0, PAR[:, P_G1:P_G1 + KC], None, first=0)

            def take_bias():
                for n in range(BIAS_FILLS):
                    dve.wait_ge(bias_turned, n + 1)
                    nc.vector.tensor_copy(bias_all[:, n * 512:(n + 1) * 512], bank(n % 4)).then_inc(bias_taken, 1)
                dve.wait_ge(bias_taken, BIAS_FILLS)

            g, later = 0, []
            for what in order1:
                if what[0] != "V":
                    for n in later:
                        split_lo(dve, n)
                    later = []
                if what == "G":
                    split_lo(dve, 2 * g + SLOTS)
                    later = [2 * g + SLOTS + 1]
                    g += 1
                elif what == "B":
                    take_bias()
                elif what[0] == "V":
                    heads_dve(dve, ch, AT1, what[1])
                elif what[1].kind == "softmax":
                    logits_dve(dve, ch, AT1, what[1])
                else:
                    stick_dve(dve, ch, AT1, what[1])
            for n in later:
                split_lo(dve, n)
            merge_dve(dve, ch, AT1, fill_o1, G_BR, 3, (proj_taken, IN_QKV + IN_GATE))
            for g in range(WO):
                for n in range(2 * (G_WO + g) + SLOTS, 2 * (G_WO + g) + SLOTS + 2):
                    split_lo(dve, n)
                dve.wait_ge(half_done, 2 * (G_WO + g) + 2)
                nc.vector.tensor_copy(Y[:, :, g * GC:(g + 1) * GC], bank(6 + g % 2).rearrange("p (t n) -> p t n", t=TT)).then_inc(wo_taken, 1)
            dve.wait_ge(wo_taken, WO)
            norm_dve_post(dve, ch, n_post, PAR[:, P_POST:P_POST + D])
            dve.wait_ge(x_ready, 1)
            norm_dve_pre(dve, ch, n_ffn, 0, PAR[:, P_G2:P_G2 + KC], None)

            def ff_conv_dve(blk, j, taps):
                dve.wait_ge(ff_init, blk + 1)
                for back, k in ((1, 1), (2, 0)):
                    for gv in range(2):
                        acc = ffacc[:, j, gv, back:S]
                        ins = nc.vector.scalar_tensor_tensor(out=acc, in0=bank(6 + j)[:, gv * S:(gv + 1) * S - back], scalar=taps(gv, k),
                                                             in1=acc, op0=ALU.mult, op1=ALU.add)
                        if back == 1:
                            ch.step(ins)
                    if back == 1:
                        ch.sync()
                ins.then_inc(ff_conv, 1)

            def ff_gate_dve(blk, j):
                dve.wait_ge(ff_gelu, blk + 1)
                nc.vector.tensor_tensor(ffp[:, j, :], ffacc[:, j, 0, :], ffacc[:, j, 1, :], ALU.mult).then_inc(ff_prod, 1)

            def ff_parts_dve(blk, j):
                dve.wait_ge(ff_prod, blk + 1)
                nc.vector.tensor_copy(FGH[:, j, :], ffp[:, j, :]).then_inc(ff_hi, 1)
                dve.wait_ge(ff_hi, blk + 1)
                nc.vector.tensor_tensor(FGL[:, j, :], ffp[:, j, :], FGH[:, j, :], ALU.subtract).then_inc(ff_gated, 1)

            def static_taps(n):
                return lambda gv, k: PAR[:, P_CV + n * 8 + gv * 4 + k:P_CV + n * 8 + gv * 4 + k + 1]

            split_lo(dve, F_HALF + 3)
            for j in range(2):
                ff_conv_dve(j, j, static_taps(j))
                split_lo(dve, F_HALF + 4 + j)
                ff_gate_dve(j, j)
                ff_parts_dve(j, j)
            with ch.loop(FF_BLOCKS // 2 - 1, 4) as i:
                at = At(i, F_BODY)
                split_lo(dve, F_HALF + 6, at)
                for j in range(2):
                    def taps(gv, k):
                        return PAR[:, bass.ds(i * 16 + (P_CV + 16 + j * 8 + gv * 4 + k), 1)]
                    split_lo(dve, F_HALF + 7 + 2 * j, at)
                    ff_conv_dve(i * 2 + 2 + j, j, taps)
                    split_lo(dve, F_HALF + 8 + 2 * j, at)
                    ff_gate_dve(i * 2 + 2 + j, j)
                split_lo(dve, F_HALF + 11, at)
                dve.wait_ge(half_done, at.halves + F_HALF + 10)
                for j in range(2):
                    ff_parts_dve(i * 2 + 2 + j, j)
            dve.wait_ge(half_done, L_HALF)
            nc.vector.tensor_copy(Y, ps[:, 0:2048].rearrange("p (t n) -> p t n", t=TT)).then_inc(ff_taken, 1)
            dve.wait_ge(ff_taken, 1)
            norm_dve_post(dve, ch, n_fpost, PAR[:, P_FPOST:P_FPOST + D])

            dve.wait_ge(zeroed, 1)
            ch.restart()
            with dve.Fori(0, LAYERS) as l:
                dve.wait_ge(x_ready, l * 3 + 2)
                dve.wait_ge(par2_loaded, l * 16 + 16)
                at = At(l, L_HALVES)
                norm_dve_pre(dve, ch, n_mix, l, PAR[:, Q_G:Q_G + KC], None, first=L_HALF, at=at)
                dve.wait_ge(na_loaded, l * 16 + 16)
                na4 = naB.rearrange("p h (k n) -> p (h k) n", k=NA_KK)
                ch.step(nc.vector.tensor_tensor(na4, na4, view(CONST[:, C_NA:C_NA + GRID_W], [0, NQ * NA_KK], [1, GRID_W]), ALU.add))
                def los(g):
                    for n in range(2 * g + SLOTS, min(2 * g + SLOTS + 2, L_HALVES)):
                        split_lo(dve, L_HALF + n, at)

                for g in range(7):
                    los(g)
                dve.wait_ge(qksq_ready, l + 1)
                ch.link(nc.vector.tensor_reduce(hssq, qksq.rearrange("p (h d) -> p h d", d=HD), AX.X, ALU.add))
                nc.vector.tensor_scalar(hssq, hssq, 1.0 / HD, EPS, ALU.mult, ALU.add).then_inc(qkvar_ready, 1)
                los(7)
                dve.wait_ge(qkstd_ready, l + 1)
                ch.link(nc.vector.reciprocal(hrstd, hrstd))
                qk3 = QK.rearrange("p t (h d) -> p (t h) d", d=HD)
                ch.link(nc.vector.tensor_tensor(qk3, qk3, view(hrstd, [1, TT * QK_HEADS], [0, HD]), ALU.mult))
                los(8)
                ch.link(nc.vector.tensor_tensor(QK, QK, view(PAR[:, Q_QKN:Q_QKN + QKW], [0, TT], [1, QKW]), ALU.mult))
                los(9)
                q4 = QK[:, :, 2 * NQ * HD:].rearrange("p t (h s d) -> p t h s d", s=2, d=32)
                x1, x2 = q4[:, :, :, 0, :], q4[:, :, :, 1, :]
                cos = view(CONST[:, C_COS:C_COS + 1], [32, TT], [0, 10], [1, 32])
                sin = view(CONST[:, C_SIN:C_SIN + 1], [32, TT], [0, 10], [1, 32])
                r4 = [rot[:, j, :].rearrange("p (t h d) -> p t h d", t=TT, h=10) for j in range(4)]
                for j, (a, c) in enumerate(((x1, cos), (x2, sin), (x1, sin), (x2, cos))):
                    ch.step(nc.vector.tensor_tensor(r4[j], a, c, ALU.mult))
                ch.sync()
                ch.step(nc.vector.tensor_tensor(x1, r4[0], r4[1], ALU.subtract))
                nc.vector.tensor_tensor(x2, r4[2], r4[3], ALU.add).then_inc(qk_ready, 1)
                transposed_dve(dve, AT2, 0, QK_HEADS, qkT.rearrange("p c n -> p (c n)"), l)
                los(L_PROJ + 1)
                g, later = L_PROJ + 2, []
                for what in order2[order2.index("Q") + 1:]:
                    if what[0] != "V":
                        for n in later:
                            split_lo(dve, n, at)
                        later = []
                    if what == "G":
                        split_lo(dve, L_HALF + 2 * g + SLOTS, at)
                        later = [L_HALF + 2 * g + SLOTS + 1]
                        g += 1
                    elif what[0] == "S":
                        logits_dve(dve, ch, AT2, what[1], l)
                    else:
                        heads_dve(dve, ch, AT2, what[1], l)
                for n in later:
                    split_lo(dve, n, at)
                merge_dve(dve, ch, AT2, fill_o2, G_LAYER + LG_BR, 2, (lproj_taken, l * N2 + L_PROJ + L_GATE), l, at)
                for g in range(WO):
                    los(LG_WO + g)
                    dve.wait_ge(half_done, at.halves + L_HALF + 2 * (LG_WO + g) + 2)
                    dst = X[:, :, g * GC:(g + 1) * GC]
                    ins = nc.vector.tensor_tensor(dst, dst, bank(6 + g % 2).rearrange("p (t n) -> p t n", t=TT), ALU.add)
                    ins.then_inc(wo_taken if g < WO - 1 else x_ready, 1)
                dve.wait_ge(x_ready, l * 3 + 3)
                norm_dve_pre(dve, ch, n_peer, l, None, PAR[:, Q_GF:Q_GF + D])

                def route(k, b):
                    rc = Chain(dve, route_step)

                    def top16(vals, best, where):
                        rc.link(nc.vector.max(best[:, 0:8], vals))
                        rc.link(nc.vector.max_index(where[:, 0:8], best[:, 0:8], vals))
                        rc.link(nc.vector.match_replace(vals, best[:, 0:8], vals, LOWEST))
                        rc.link(nc.vector.max(best[:, 8:16], vals))
                        rc.step(nc.vector.max_index(where[:, 8:16], best[:, 8:16], vals))

                    def first_keys():
                        rc.link(nc.vector.tensor_copy(keys, SC[:, bass.ds(k, 1), :, :].rearrange("p a s n -> p (a s) n")))
                        top16(keys[:, 0, :], sv[:, 0, :], si[:, 0, :])

                    def second_keys():
                        top16(keys[:, 1, :], sv[:, 1, :], si[:, 1, :])

                    def pairs():
                        rc.sync()
                        rc.step(nc.vector.tensor_copy(siF, si))
                        rc.link(nc.vector.tensor_tensor(cand.rearrange("p (a b) -> p a b", a=TOPK), view(sv[:, 0, :], [1, TOPK], [0, TOPK]),
                                                        view(sv[:, 1, :], [0, TOPK], [1, TOPK]), ALU.add))
                        top16(cand, topv, sel[:, 0, :])
                        nc.vector.tensor_scalar(topneg, topv[:, 0:1], -1.0, None, ALU.mult).then_inc(topd_ready, 1)

                    def indices():
                        rc.sync()
                        rc.step(nc.vector.tensor_scalar(sel[:, 1, :], sel[:, 0, :], 4, None, ALU.logical_shift_right))
                        rc.link(nc.vector.tensor_scalar(sel[:, 2, :], sel[:, 0, :], TOPK - 1, None, ALU.bitwise_and))
                        rc.link(nc.vector.tensor_copy(abF, sel[:, 1:3, :]))
                        both = tuple((j, eq, eq.rearrange("p (k a) -> p k a", a=TOPK)) for j, eq in enumerate((eqA, eqB)))
                        for j, eq, eq3 in both:
                            rc.step(nc.vector.tensor_tensor(eq3, view(abF[:, j, :], [1, TOPK], [0, TOPK]), view(iota16, [0, TOPK], [1, TOPK]), ALU.is_equal))
                        rc.sync()
                        for j, eq, eq3 in both:
                            rc.step(nc.vector.tensor_tensor(eq3, eq3, view(siF[:, j, :], [0, TOPK], [1, TOPK]), ALU.mult))
                        rc.sync()
                        for j, eq, eq3 in both:
                            rc.step(nc.vector.tensor_reduce(eF[:, j, :], eq3, AX.X, ALU.add))
                        rc.sync()
                        rc.link(nc.vector.scalar_tensor_tensor(out=eF[:, 0, :], in0=eF[:, 0, :], scalar=float(NKEY), in1=eF[:, 1, :],
                                                               op0=ALU.mult, op1=ALU.add))
                        nc.vector.tensor_scalar(EIDX[:, b, :], eF[:, 0, :], lbase, None, ALU.add).then_inc(routed, 1)
                        dve.wait_ge(texp_ready, l * ROUTES + k + 1)
                        rc.link(nc.vector.reciprocal(ersum, esum))
                        nc.vector.tensor_scalar(GWT[:, b, :], topv, ersum, None, ALU.mult).then_inc(gates_ready, 1)
                        rc.restart()

                    return first_keys, second_keys, pairs, indices

                ch.step(nc.vector.memset(SC[:, STEPS, :, :], 0.0))
                los(LG_PQ)
                los(LG_PQ + 1)
                wait_alone(dve, sc_ready, l * PH + 1, dve_passed)
                for j, part in enumerate(route(0, 0)):
                    part()
                    los(LG_PQ + 2 + j)
                for j in range(LG_PQ + 6, L_GROUPS):
                    los(j)
                for t in range(TT):
                    with dve.Fori(0, PH // 2) as i:
                        for b in range(2):
                            k = i * 2 + (t * PH + b)
                            for c in range(PASSES):
                                use = l * USES + i * (2 * PASSES) + (t * PH * PASSES + b * PASSES + c)

                                def dots(q):
                                    for r in range(q * SET, (q + 1) * SET):
                                        dve.wait_ge(g_landed[r], use * 16 + 16)
                                        ins = nc.vector.tensor_tensor_reduce(ring[:, r, 0:D], HN[:, t, :], ring[:, r, 0:D], 1.0, 0.0,
                                                                             ALU.mult, ALU.add, hd[:, r:r + 1])
                                    ins.then_inc(dots_ready, 1)

                                def weights(q):
                                    dve.wait_ge(gelu_ready, use * SETS + q + 1)
                                    nc.vector.tensor_tensor(gw8[:, q * SET:(q + 1) * SET], ga[:, q * SET:(q + 1) * SET],
                                                            GWT[:, b, c * RING + q * SET:c * RING + (q + 1) * SET], ALU.mult).then_inc(w_ready, 1)

                                if c == 0:
                                    dve.wait_ge(gates_ready, l * ROUTES + k + 1)
                                    if t == 0:
                                        wait_alone(dve, sc_ready, l * PH + i * 2 + 2 if b == 0 else l * PH + i + 5, dve_passed)
                                    parts = route(k + 1, 1 - b)
                                for q in range(SETS):
                                    dots(q)
                                    if q:
                                        weights(q - 1)
                                    if c == 0:
                                        parts[q]()
                                weights(SETS - 1)
                    dve.wait_ge(acc_ready, l * TT + t + 1)
                    nc.vector.tensor_tensor(X[:, t, :], X[:, t, :], ps[:, 2 * t * 512:(2 * t + 2) * 512], ALU.add).then_inc(x_ready, 1)
                ch.sync()
                nc.vector.tensor_scalar(lbase, lbase, float(EXPERTS), None, ALU.add).then_inc(dve_step, 1)
                ch.n += 1
                ch.restart()


def t5_bucket(dist):
    exact = NB_BUCKETS // 2
    nf = np.maximum(dist, 1).astype(np.float32)
    large = exact + (np.log(nf / np.float32(exact)) / np.float32(np.log(2048 / exact)) * np.float32(NB_BUCKETS - exact)).astype(np.int32)
    return np.where(dist < exact, dist, np.minimum(large, NB_BUCKETS - 1))


def shape_constants():
    f = np.float32
    c = np.zeros((P, C_END), f)
    c[:, C_ID:C_ID + P] = np.eye(P, dtype=f)
    c[:, C_TURN:C_TURN + P] = np.eye(P, dtype=f)[::-1]
    q = np.arange(P)
    b = np.ones((P, S), f)
    b[:, P:] = q[None, :] < q[:, None]
    c[:, C_BM:C_BM + S] = b
    c[:, C_NB:C_NB + S] = 1 - b
    col = q % GRID_W
    cs = np.clip(col - 8, 0, GRID_W - 16)
    kc = np.arange(GRID_W)
    c[:, C_NA:C_NA + GRID_W] = np.where((kc[None] >= cs[:, None]) & (kc[None] < cs[:, None] + 16), 0, NEG)
    inv = f(10000.0) ** (-np.arange(32, dtype=f) / f(32))
    for t in range(TT):
        pos = q + t * P
        c[:, C_SW + t * S:C_SW + (t + 1) * S] = np.where(np.abs(pos[:, None] - np.arange(S)[None]) <= 128, 0, NEG)
        ang = pos.astype(f)[:, None] * inv[None]
        c[:, C_COS + t * 32:C_COS + (t + 1) * 32] = np.cos(ang)
        c[:, C_SIN + t * 32:C_SIN + (t + 1) * 32] = np.sin(ang)
    c[:, C_IOTA:C_IOTA + TOPK] = np.arange(TOPK, dtype=f)
    oh = np.zeros((NB_BUCKETS + 1, VAR, EW), f)
    for v, (step, limit) in enumerate(((1, 128), (4, 512), (16, 2048), (1, 127))):
        for x in range(EW):
            dist = S - 1 - x
            ok = 0 <= dist <= limit and dist % step == 0
            oh[int(t5_bucket(np.array(dist))) if ok else NB_BUCKETS, v, x] = 1
    return c, oh.reshape(NB_BUCKETS + 1, VAR * EW)


def pack(w, tok=()):
    n = w.shape[1] // GC
    w = w.reshape(KC, P, n, GC)
    by_features = w.reshape(KC, P, n, 2, P).transpose(2, 3, 1, 0, 4).reshape(n, 2, P, HW)
    by_chunks = w.reshape(2, HC, P, n, GC).transpose(3, 0, 2, 1, 4).reshape(n, 2, P, HW)
    return np.stack([(by_chunks if g in tok else by_features)[g] for g in range(n)]).reshape(2 * n, P, HW)


def by_feature(v):
    return v.reshape(-1, P).T


def rows_on_all(v):
    return np.broadcast_to(v.reshape(1, -1), (P, v.size))


def lay_out(i):
    cat = np.concatenate
    pairs = [0, 4, 1, 5, 2, 6, 3, 7]
    w = i["w_in"][0]
    bq = w[:, 2304:2816].reshape(D, 8, HD)[:, pairs].reshape(D, 512)
    w = cat([w[:, :2304], bq, w[:, 2816:]], 1)
    groups = [pack(w, TOK_1), pack(cat([i["w_br_a"][0], i["w_br_b"][0], i["w_br_c"][0]], 0)), pack(i["w_out"][0], range(WO))]
    up = pack(i["w_up"][0].reshape(D, 2, FF_BLOCKS, P).transpose(0, 2, 1, 3).reshape(D, 2 * FF_BLOCKS * P))
    dn = i["w_down"][0].reshape(FF_BLOCKS, P, D)
    ff = [up[0:4]]
    for k in range(1, FF_BLOCKS // 2):
        ff += [up[4 * k:4 * k + 4], dn[2 * k - 2:2 * k]]
    groups += ff + [dn[-2:]]
    par2, rpb = [], []
    for l in range(LAYERS):
        w = i["w_in_2"][l]
        qb = w[:, 1536:2048].reshape(D, 8, HD)[:, pairs].reshape(D, 512)
        w = cat([w[:, 0:1024], qb, w[:, 2048:2304], w[:, 1024:1536], w[:, 2304:]], 1)
        groups += [pack(w, range(L_PROJ)), pack(cat([i["w_branch_na_2"][l], i["w_branch_swa_2"][l]], 0)), pack(i["w_out_2"][l], range(WO)),
                   pack(i["peer_query_2"][l])]
        n = i["qk_norm_2"][l]
        qkn = cat([np.broadcast_to(n[j], (c, HD)).reshape(-1) for j, c in ((0, 8), (1, 8), (2, 8), (3, 2))])
        par2.append(cat([by_feature(i["norm_mix_2"][l]), by_feature(i["gate_bias_2"][l].reshape(-1)), rows_on_all(i["swa_sink_2"][l]),
                         rows_on_all(qkn), rows_on_all(i["norm_ffn_2"][l]),
                         i["peer_sub_keys_2"][l].transpose(2, 0, 1).reshape(P, 2 * NKEY)], 1))
        padded = np.pad(i["na_rpb_2"][l], ((0, 0), (0, 0), (GRID_W - 16, GRID_W - 16)))
        rpb.append(np.broadcast_to(padded[:, :, None, :], (NQ, RPB_R, GRID_W, RPB_PAD)))
    cw = i["conv_w"][0].reshape(3, 2, FF_BLOCKS, P)
    cb = i["conv_b"][0].reshape(1, 2, FF_BLOCKS, P)
    taps = cat([cw, cb], 0).transpose(3, 2, 1, 0).reshape(P, FF_BLOCKS * 8)
    par1 = cat([by_feature(i["attn_pre_norm"][0]), by_feature(i["ffn_pre_norm"][0]), by_feature(i["b_gate"][0].reshape(-1)), taps,
                rows_on_all(i["sinks"][0]), rows_on_all(i["attn_post_norm"][0]), rows_on_all(i["ffn_post_norm"][0])], 1)
    consts, onehot = shape_constants()
    return {
        "x": i["x"][0], "wstream": cat(groups, 0), "consts": consts, "onehot": onehot,
        "relb": np.pad(i["rel_bias"], ((0, 1), (0, 0)), constant_values=NEG),
        "par1": par1, "par2": np.stack(par2), "rpb": np.stack(rpb),
        "experts": cat([i["peer_down_2"].reshape(-1, D), i["peer_up_2"].reshape(-1, D)], 1),
    }


def kernel(**inputs):
    import concourse.bacc as bacc
    from concourse.bass_utils import run_bass_kernel_spmd as run

    nc = bacc.Bacc("TRN2", target_bir_lowering=False, num_devices=1)
    laid = lay_out({k: np.asarray(v) for k, v in inputs.items()})
    arrays, args = {}, []
    for name, a in laid.items():
        arrays["in_" + name] = np.ascontiguousarray(a, dtype=np.float32)
        args.append(nc.dram_tensor("in_" + name, a.shape, F32, kind="ExternalInput").ap())
    result = nc.dram_tensor("result", (S, D), F32, kind="ExternalOutput").ap()
    build(nc, *args, result)
    return run(nc, [arrays], core_ids=[0]).results[0]["result"].reshape(1, S, D)
```

```python
from contextlib import ExitStack, contextmanager

import numpy as np

import concourse.bass as bass
from concourse import mybir

F32 = mybir.dt.float32
F32R = mybir.dt.float32r
BF16 = mybir.dt.bfloat16
U32 = mybir.dt.uint32
ACT = mybir.ActivationFunctionType
ALU = mybir.AluOpType
AX = mybir.AxisListType

P = 128
D = 1024
S = 256
TT = S // P
KC = D // P
HD = 64
SCALE = HD ** -0.5
EPS = 1e-6
NEG = -1e30
LOWEST = -3.0e38

GC = 256
GW = KC * GC
HW = GW // 2
HC = KC // 2
SLOTS = 3
IN_QKV, IN_GATE, BR, WO = 15, 12, 4, 4
FF_BLOCKS = 32
TOK_1 = (6, 7, 8, 14)
G_GATE = IN_QKV
G_BR = IN_QKV + IN_GATE
G_WO = G_BR + BR
G_FF = G_WO + WO
G_LAYER = G_FF + FF_BLOCKS + FF_BLOCKS // 2
L_PROJ, L_GATE, L_PQ = 9, 8, 8
LG_GATE = L_PROJ
LG_BR = LG_GATE + L_GATE
LG_WO = LG_BR + BR
LG_PQ = LG_WO + WO
L_GROUPS = LG_PQ + L_PQ
LAYERS = 2
GROUPS = G_LAYER + LAYERS * L_GROUPS
HALVES, L_HALVES = 2 * GROUPS, 2 * L_GROUPS
F_HALF, L_HALF = 2 * G_FF, 2 * G_LAYER
F_BODY = 6
assert L_HALVES % SLOTS == 0 and F_BODY % SLOTS == 0

A_H, A_G, B_H, C_H = 4, 3, 8, 4
VAR = 4
EW = 384
NB_BUCKETS = 32

WO_ORDER = [(0, 0), (1, 0), (0, 1), (1, 1)] + [(g, h) for g in range(2, WO) for h in range(2)]
WO_HALVES = [2 * g + h for g, h in WO_ORDER]
NQ = 8
QK_HEADS = 3 * NQ + 2
QKW = QK_HEADS * HD
EARLY = 2
ROWS = 4
GRID_W = 64
RPB_R, RPB_C = 15, 31
RPB_PAD = 2 * GRID_W - 1
NA_KK = 6
PH = 8
NKEY = 128
TOPK = 16
EXPERTS = NKEY * NKEY
PICKS = PH * TOPK
SETS, SET = 4, 2
RING = SETS * SET
PASSES = TOPK // RING
STEPS = TT * PH
USES = STEPS * PASSES
ROUTES = STEPS + 1

C_ID, C_TURN, C_BM, C_NB, C_NA, C_SW, C_COS, C_SIN, C_IOTA, C_END = np.cumsum(
    [0, P, P, S, S, GRID_W, TT * S, TT * 32, TT * 32, TOPK]).tolist()
P_G1, P_G2, P_BG, P_CV, P_SK, P_POST, P_FPOST, P_END = np.cumsum(
    [0, KC, KC, 24, FF_BLOCKS * 8, B_H, D, D]).tolist()
Q_G, Q_BG, Q_SK, Q_QKN, Q_GF, Q_KEYS, Q_END = np.cumsum(
    [0, KC, 16, NQ, QKW, D, 2 * NKEY]).tolist()


def wait_alone(eng, sem, value, passed):
    eng.wait_ge(sem, value)
    eng.sem_inc(passed, 1)


class Chain:

    def __init__(self, eng, sem):
        self.eng, self.sem, self.base, self.n = eng, sem, 0, 0

    def step(self, ins):
        self.n += 1
        return ins.then_inc(self.sem, 1)

    def sync(self):
        self.eng.wait_ge(self.sem, self.base + self.n)

    def link(self, ins):
        self.step(ins)
        self.sync()

    def restart(self):
        self.sync()
        self.eng.drain()
        self.eng.sem_clear(self.sem)
        self.base = self.n = 0

    @contextmanager
    def loop(self, count, per):
        before = self.base + self.n
        with self.eng.Fori(0, count) as i:
            self.base, self.n = i * per + before, 0
            yield i
            assert self.n == per, f"{self.n} steps in a loop's body, {per} stated"
        self.base, self.n = before + count * per, 0


def view(ap, *dims):
    return bass.AP(tensor=ap.tensor, offset=ap.offset, ap=[list(ap.ap[0])] + [list(d) for d in dims])




def build(nc, x_in, wstream, consts, onehot, relb, par1, par2, rpb, experts, out):
    ctx = ExitStack()
    with ctx:
        def sb(name, shape, dt=F32):
            return ctx.enter_context(nc.sbuf_tensor(name, shape, dt))

        def sem(name):
            return ctx.enter_context(nc.semaphore(name))

        X = sb("x", [P, TT, D])
        HN = sb("h_norm", [P, TT, D])
        FH, FL = sb("feat_hi", [P, KC, S], F32R), sb("feat_lo", [P, KC, S], F32R)
        W = sb("weights", [P, SLOTS, HW])
        WH, WL = sb("weights_hi", [P, SLOTS, HW], F32R), sb("weights_lo", [P, SLOTS, HW], F32R)
        FGH, FGL = sb("ff_gated_hi", [P, 2, S], F32R), sb("ff_gated_lo", [P, 2, S], F32R)
        CONST = sb("consts", [P, C_END])
        PAR = sb("params", [P, max(P_END, Q_END)])
        SMALL = sb("small", [P, 512])
        ZERO = sb("zero", [P, 512], BF16)
        EIDX = sb("expert_idx", [P, 2, TOPK], U32)
        GWT = sb("expert_gate", [P, 2, TOPK])
        work = sb("work", [P, 16392])
        arena = sb("arena", [P, 12800])
        ps = ctx.enter_context(nc.psum_tensor("ps", [P, 8 * 512], F32))
        na_rows = nc.dram_tensor("na_rows", [LAYERS, P, NQ, NA_KK * GRID_W], F32).ap()
        scratch = nc.dram_tensor("bias_rows", [20, VAR * EW], F32).ap()

        def carve(region, at, *shape):
            n = int(np.prod(shape))
            v = region[:, at:at + n]
            if len(shape) > 1:
                names = "abcd"[:len(shape)]
                v = v.rearrange(f"p ({' '.join(names)}) -> p {' '.join(names)}",
                                **dict(zip(names, shape)))
            return v, at + n

        ident = CONST[:, C_ID:C_ID + P]
        turn = CONST[:, C_TURN:C_TURN + P]
        before = CONST[:, C_BM:C_BM + S]
        not_before = CONST[:, C_NB:C_NB + S]
        iota16 = CONST[:, C_IOTA:C_IOTA + TOPK]

        LG0, w0 = carve(work, 0, 2056)
        PT, w0 = carve(work, w0, 16, P)
        O, w0 = carve(work, w0, TT, D)
        LG = (LG0, work[:, w0:w0 + 2056])
        MT, w0 = carve(work, w0, KC, S)
        Y, w0 = carve(work, w0, TT, D)
        GT, w0 = carve(work, w0, 24, S)
        ring = work[:, 0:RING * 2 * D].rearrange("p (r n) -> p r n", r=RING)
        ffacc = work[:, 0:1024].rearrange("p (j g n) -> p j g n", j=2, g=2)
        ffp = work[:, 1024:1536].rearrange("p (j n) -> p j n", j=2)
        aqT, a0 = carve(arena, 0, 6, S)
        akT, a0 = carve(arena, a0, 6, S)
        av, a0 = carve(arena, a0, TT, 768)
        bqT, a0 = carve(arena, a0, 4, S)
        bkT, a0 = carve(arena, a0, S)
        bv, a0 = carve(arena, a0, TT, P)
        cqT, a0 = carve(arena, a0, 2, S)
        ckT, a0 = carve(arena, a0, 2, S)
        cv, a0 = carve(arena, a0, TT, S)
        bias_all = arena[:, a0:a0 + (A_H * A_G + B_H) * S]
        biasA, a0 = carve(arena, a0, A_H, A_G, S)
        biasB, a0 = carve(arena, a0, B_H, S)
        hankA, h0 = carve(work, 8200, A_H, A_G, S)
        hankB, h0 = carve(work, h0, B_H, S)
        hank = work[:, 8200:h0]
        BIAS_FILLS = (h0 - 8200) // 512
        erow, _ = carve(work, 0, VAR * EW)
        ohot, _ = carve(work, 2056, VAR * EW)
        relb_sb, _ = carve(work, 2056 + VAR * EW, 20)
        naB, b0 = carve(arena, 0, NQ, NA_KK * GRID_W)
        QK, b0 = carve(arena, b0, TT, QKW)
        qkT, b0 = carve(arena, b0, QK_HEADS // 2, S)
        va, b0 = carve(arena, b0, TT, NQ * HD)
        vb, b0 = carve(arena, b0, TT, P)
        QK_PARTS = ((0, 2 * NQ), (2 * NQ, QK_HEADS))
        rots = [carve(work, at, 2, TT * 10 * 32)[0] for at in (8208, 14344)]
        qksq = [carve(work, at, TT, (h1 - h0) * HD)[0] for at, (h0, h1) in zip((2560, 8208), QK_PARTS)]
        pqT, c0 = carve(arena, 0, 16, S)
        SC, c0 = carve(arena, c0, ROUTES, 2, NKEY)
        keys, c0 = carve(arena, c0, 2, NKEY)
        cand, c0 = carve(arena, c0, TOPK * TOPK)
        eqA, c0 = carve(arena, c0, TOPK * TOPK)
        eqB, c0 = carve(arena, c0, TOPK * TOPK)
        sv, c0 = carve(arena, c0, 2, TOPK)
        siF, c0 = carve(arena, c0, 2, TOPK)
        topv, c0 = carve(arena, c0, TOPK)
        abF, c0 = carve(arena, c0, 2, TOPK)
        eF, c0 = carve(arena, c0, 2, TOPK)
        si = arena[:, c0:c0 + 2 * TOPK].bitcast(U32).rearrange("p (a k) -> p a k", k=TOPK)
        sel = arena[:, c0 + 2 * TOPK:c0 + 5 * TOPK].bitcast(U32).rearrange("p (a k) -> p a k", k=TOPK)
        ssq, std, rstd, ssq_early = SMALL[:, 0:2], SMALL[:, 2:4], SMALL[:, 4:6], SMALL[:, 6:8]
        negm, sums, rsum = ([SMALL[:, at + 8 * turn:at + 8 * turn + 8] for turn in range(2)] for at in (224, 240, 256))
        hssq, hrstd = ([SMALL[:, at + TT * h0:at + TT * h1] for h0, h1 in QK_PARTS] for at in (32, 96))
        hd = SMALL[:, 160:160 + RING]
        ga = SMALL[:, 176:176 + RING]
        gw8 = SMALL[:, 192:192 + RING]
        lbase = SMALL[:, 208:209]
        esum, ersum, topneg = SMALL[:, 216:217], SMALL[:, 217:218], SMALL[:, 218:219]
        DIAG, _ = carve(arena, c0 + 5 * TOPK, RING, P)
        junk = HN

        def bank(b, n=1):
            return ps[:, b * 512:(b + n) * 512]

        def two(t, b):
            return t[:, 2 * b:2 * b + 2, :].rearrange("p c n -> p (c n)")

        x_loaded, const_loaded, par1_loaded, bias_in = sem("x_loaded"), sem("const_loaded"), sem("par1_loaded"), sem("bias_in")
        w_landed = [sem(f"w_landed{i}") for i in range(SLOTS)]
        half_done = sem("half_done")
        w_hi, w_lo = sem("w_hi"), sem("w_lo")
        gates_on = sem("gates_on")
        heads_hi, mt_hi, mt_lo = sem("heads_hi"), sem("mt_hi"), sem("mt_lo")
        ff_prod, ff_hi = sem("ff_prod"), sem("ff_hi")
        proj_taken = sem("proj_taken")
        lproj_taken = sem("layer_proj_taken")
        merged = sem("merged")
        wo_taken = sem("wo_taken")
        br_taken = sem("branch_taken")
        zeroed = sem("zeroed")
        erow_ready, erow_copied, erow_stored = sem("erow_ready"), sem("erow_copied"), sem("erow_stored")
        bias_loaded = sem("bias_loaded")
        bias_turned, bias_taken = sem("bias_turned"), sem("bias_taken")
        dve_step, route_step = sem("dve_step"), sem("route_step")
        x_ready = sem("x_ready")
        low_scores, llow_scores = sem("low_scores"), sem("layer_low_scores")
        scores_ready, logits_ready, probs_ready = sem("scores_ready"), sem("logits_ready"), sem("probs_ready")
        pT_ready, pT_taken = sem("pT_ready"), sem("pT_taken")
        lscores_ready, llogits_ready, lprobs_ready = sem("layer_scores_ready"), sem("layer_logits_ready"), sem("layer_probs_ready")
        lpT_ready, lpT_taken = sem("layer_pT_ready"), sem("layer_pT_taken")
        ff_squared, ff_gained = sem("ff_squared"), sem("ff_gained")
        ff_init, ff_conv, ff_gelu, ff_gated = sem("ff_init"), sem("ff_conv"), sem("ff_gelu"), sem("ff_gated")
        out_stored = sem("out_stored")
        gains1_loaded, gains2_loaded, par2_loaded, na_loaded, na_stored = sem("gains1_loaded"), sem("gains2_loaded"), sem("par2_loaded"), sem("na_loaded"), sem("na_stored")
        qk_normed, turned_parts = sem("qk_normed"), sem("turned_parts")
        qksq_ready, qkvar_ready, qkstd_ready, qk_ready = sem("qksq_ready"), sem("qkvar_ready"), sem("qkstd_ready"), sem("qk_ready")
        sq_early, var_early = sem("squares_early"), sem("variance_early")
        sc_done, sc_ready = sem("sc_done"), sem("sc_ready")
        topd_ready, texp_ready, routed, gates_ready = sem("topd_ready"), sem("texp_ready"), sem("routed"), sem("gates_ready")
        g_landed = [sem(f"g_landed{i}") for i in range(RING)]
        set_used = [sem(f"set_used{i}") for i in range(SETS)]
        dots_ready, gelu_ready, w_ready, diag_ready = sem("dots_ready"), sem("gelu_ready"), sem("w_ready"), sem("diag_ready")
        acc_ready = sem("acc_ready")
        pool_passed, dve_passed = sem("pool_waits_passed"), sem("dve_waits_passed")

        class Norm:

            def __init__(self, name):
                self.sq = sem(name + "_squares")
                self.var = sem(name + "_var")
                self.std = sem(name + "_std")
                self.rstd = sem(name + "_rstd")
                self.hn = sem(name + "_normed")
                self.xp = sem(name + "_transposed")
                self.hi = sem(name + "_hi")
                self.hT = sem(name + "_hT")

        n_attn, n_post, n_ffn, n_fpost = Norm("n_attn"), Norm("n_post"), Norm("n_ffn"), Norm("n_fpost")
        n_mix, n_peer = Norm("n_mix"), Norm("n_peer")


        def root_table(col):
            nc.scalar.activation(SMALL[:, col:col + 1], ident[:, 0:1], ACT.Sqrt)

        EARLY_D = (WO - 1) * GC

        def squares_act(act, src, taken):
            act.wait_ge(*taken)
            for t in range(TT):
                nc.scalar.activation(junk[:, t, 0:EARLY_D], src(t)[:, 0:EARLY_D], ACT.Square,
                                     accum_out=ssq_early[:, t:t + 1]).then_inc(sq_early, 1)

        def norm_act(act, nm, src, l, ready=None, between=None, rows=False, first=0, one=None):
            for t in range(TT):
                if t and between:
                    between()
                if ready is not None:
                    act.wait_ge(x_ready, ready + t + 1)
                ins = nc.scalar.activation(junk[:, t, first:], src(t)[:, first:], ACT.Square, accum_out=ssq[:, t:t + 1])
                if one and t == 0:
                    ins.then_inc(one, 1)
            ins.then_inc(nm.sq, 1)
            act.wait_ge(nm.var, l + 1)
            nc.scalar.activation(std, ssq, ACT.Sqrt).then_inc(nm.std, 1)
            if rows:
                act.wait_ge(nm.rstd, l + 1)
                nc.scalar.activation(HN[:, 1, :], X[:, 1, :], ACT.Copy, scale=rstd[:, 1:2]).then_inc(nm.hn, 1)

        def norm_dve_rstd(dve, nm, l, split=None):
            if split is not None:
                dve.wait_ge(sq_early, split)
                nc.vector.tensor_scalar(ssq_early, ssq_early, 1.0 / D, EPS, ALU.mult, ALU.add).then_inc(var_early, TT)
                dve.wait_ge(var_early, split)
            dve.wait_ge(nm.sq, l + 1)
            if split is not None:
                nc.vector.scalar_tensor_tensor(out=ssq, in0=ssq, scalar=1.0 / D, in1=ssq_early, op0=ALU.mult, op1=ALU.add).then_inc(nm.var, 1)
            else:
                nc.vector.tensor_scalar(ssq, ssq, 1.0 / D, EPS, ALU.mult, ALU.add).then_inc(nm.var, 1)
            dve.wait_ge(nm.std, l + 1)
            nc.vector.reciprocal(rstd, std).then_inc(nm.rstd, 1)
            dve.wait_ge(nm.rstd, l + 1)

        def norm_dve_pre(dve, nm, l, gain_fm, gain_tok, first=None, at=0, split=None):
            norm_dve_rstd(dve, nm, l, split)
            if gain_tok is None:
                nc.vector.tensor_scalar(HN[:, 0, :], X[:, 0, :], rstd[:, 0:1], None, ALU.mult).then_inc(nm.hn, 1)
            else:
                for t in range(TT):
                    nc.vector.scalar_tensor_tensor(out=HN[:, t, :], in0=X[:, t, :], scalar=rstd[:, t:t + 1],
                                                   in1=gain_tok, op0=ALU.mult, op1=ALU.mult).then_inc(nm.hn, 1)
            if first is not None:
                split_lo(dve, first, at)
            for b in range(4):
                dve.wait_ge(nm.hi, 4 * l + b + 1)
                if gain_fm is None:
                    ins = nc.vector.tensor_tensor(two(FL, b), bank(b), two(FH, b), ALU.subtract)
                else:
                    for c in (2 * b, 2 * b + 1):
                        ins = nc.vector.scalar_tensor_tensor(out=FL[:, c, :], in0=ps[:, c * S:(c + 1) * S], scalar=gain_fm[:, c:c + 1],
                                                             in1=FH[:, c, :], op0=ALU.mult, op1=ALU.subtract)
                ins.then_inc(nm.hT, 1)
            if first is not None:
                for n in range(first + 1, first + SLOTS):
                    split_lo(dve, n, at)

        def norm_act_hi(act, nm, l, gain_fm, first=None, at=0):
            if first is not None:
                split_hi(act, first, at)
            for b in range(4):
                act.wait_ge(nm.xp, 4 * l + b + 1)
                if gain_fm is None:
                    ins = nc.scalar.activation(two(FH, b), bank(b), ACT.Copy)
                else:
                    for c in (2 * b, 2 * b + 1):
                        ins = nc.scalar.activation(FH[:, c, :], ps[:, c * S:(c + 1) * S], ACT.Copy, scale=gain_fm[:, c:c + 1])
                ins.then_inc(nm.hi, 1)
            if first is not None:
                for n in range(first + 1, first + SLOTS):
                    split_hi(act, n, at)

        def keep_warm(pe, turns, b=4):
            with pe.Fori(0, turns):
                for _ in range(4):
                    nc.tensor.matmul(bank(b), ZERO[:, 0:P], ZERO[:, :], start=True, stop=True)

        def norm_pe(pe, nm, l):
            pe.wait_ge(nm.hn, l * TT + TT)
            for b in range(4):
                for c in (2 * b, 2 * b + 1):
                    for t in range(TT):
                        ins = nc.tensor.transpose(ps[:, c * S + t * P:c * S + (t + 1) * P],
                                                  HN[:, t, c * P:(c + 1) * P], ident)
                ins.then_inc(nm.xp, 1)

        def norm_dve_post(dve, ch, nm, gained, split=None):
            norm_dve_rstd(dve, nm, 0, split)
            ch.sync()
            for t in range(TT):
                nc.vector.scalar_tensor_tensor(out=X[:, t, :], in0=gained[:, t, :], scalar=rstd[:, t:t + 1], in1=X[:, t, :],
                                               op0=ALU.mult, op1=ALU.add).then_inc(x_ready, 1)

        def stream(t):
            return X[:, t, :]

        YG = PT.rearrange("p k n -> p (k n)")[:, 0:TT * D].rearrange("p (t d) -> p t d", t=TT)

        def unnormed(t):
            return Y[:, t, :]

        def ff_result(t):
            return ps[:, t * D:(t + 1) * D]


        def split_hi(act, n, at=0):
            per = 0 if isinstance(at, int) else at.landed
            base = 0 if isinstance(at, int) else at.halves
            act.wait_ge(w_landed[n % SLOTS], per + 16 * (n // SLOTS + 1))
            if n >= SLOTS:
                act.wait_ge(half_done, base + n - SLOTS + 1)
            nc.scalar.activation(WH[:, n % SLOTS, :], W[:, n % SLOTS, :], ACT.Copy).then_inc(w_hi, 1)

        def split_lo(dve, n, at=0):
            base = 0 if isinstance(at, int) else at.halves
            dve.wait_ge(w_hi, base + n + 1)
            nc.vector.tensor_tensor(WL[:, n % SLOTS, :], W[:, n % SLOTS, :], WH[:, n % SLOTS, :], ALU.subtract).then_inc(w_lo, 1)

        def split_pe(pe, n, at=0):
            base = 0 if isinstance(at, int) else at.halves
            pe.wait_ge(w_lo, base + n + 1)
            return WH[:, n % SLOTS, :], WL[:, n % SLOTS, :]

        class At:

            def __init__(self, i, halves):
                self.halves, self.landed = i * halves, i * (16 * halves // SLOTS)

        def product(out, stat, mov, start, stop):
            nc.tensor.matmul(out, stat[0], mov[0], start=start, stop=False)
            nc.tensor.matmul(out, stat[0], mov[1], start=False, stop=False)
            return nc.tensor.matmul(out, stat[1], mov[0], start=False, stop=stop)

        def cols(pair, at, n):
            return tuple(x[:, at:at + n] for x in pair)

        def feat(c, at, n):
            return FH[:, c, at:at + n], FL[:, c, at:at + n]

        def group_fm(pe, g, b, at=0, parts=(range(KC),), also=None, done=0):
            for h in range(2):
                w = split_pe(pe, 2 * g + h, at)
                for j, chunks in enumerate(parts):
                    if j == 0 and h < done:
                        continue
                    for c in chunks:
                        if also and h == 0:
                            also(c)
                        ins = product(ps[:, (b + j) * 512 + h * S:(b + j) * 512 + (h + 1) * S], cols(w, c * P, P), feat(c, 0, S),
                                      c == chunks[0], c == chunks[-1])
                ins.then_inc(half_done, 1)

        def half_tok(pe, n, b, h, at=0, also=None):
            if h == 0:
                nc.tensor.matmul(bank(b), ZERO[:, 0:P], ZERO[:, :], start=True, stop=False)
            w = split_pe(pe, n, at)
            for t in range(TT):
                for c in range(h * HC, (h + 1) * HC):
                    if also and t == 0:
                        also(c)
                    ins = product(ps[:, b * 512 + t * GC:b * 512 + (t + 1) * GC], feat(c, t * P, P), cols(w, c % HC * GC, GC),
                                  False, c == KC - 1 and t == TT - 1)
            ins.then_inc(half_done, 1)

        def group_tok(pe, g, b, at=0, also=None):
            for h in range(2):
                half_tok(pe, 2 * g + h, b, h, at, also)

        class Attn:

            def __init__(self, low, scores, logits, probs, pTr, pTt, batches, fills):
                self.low, self.scores, self.logits, self.probs = low, scores, logits, probs
                self.pTr, self.pTt = pTr, pTt
                self.batches, self.fills = batches, fills

        class Batch:

            def __init__(self, at, fill, rows, width, q, col, kind, bias=None, sink=None):
                self.at, self.fill, self.rows, self.width, self.q, self.col = at, fill, rows, width, q, col
                self.kind, self.bias, self.sink = kind, bias, sink
                self.n = len(rows)
                self.wide = width + (sink is not None)
                self.blocks = self.n * width // P
                self.copies = -(-self.blocks // 4)
                self.fills = self.copies + 1
                self.values = fill + self.copies
                self.turn = at % 2
                self.L = LG[self.turn][:, 0:self.n * self.wide].rearrange("p (n w) -> p n w", n=self.n)
                self.ps = ps[:, 0:self.n * width].rearrange("p (n w) -> p n w", n=self.n)

        def scores_pe(pe, A, b, l=0):
            if b.at:
                pe.wait_ge(A.logits, l * A.batches + b.at)
            places = []
            for r, (pieces, _) in enumerate(b.rows):
                at = r * b.width
                for q, k in pieces:
                    places.append((q.base_partition(), at, q, k))
                    at += k.shape[-1]
            for part in (0, HD):
                for p, at, q, k in places:
                    if p == part:
                        ins = nc.tensor.matmul(ps[:, at:at + k.shape[-1]], q, k, start=True, stop=True)
                if part == 0:
                    ins.then_inc(A.low, 1)
                    pe.wait_ge(A.low, l * A.batches + b.at + 1)
            ins.then_inc(A.scores, 1)

        def transposes_pe(pe, A, fill, sources, l, fills=None):
            for f in fills or range(-(-len(sources) // 4)):
                n = fill + f
                if n >= 2:
                    pe.wait_ge(A.pTt, l * A.fills + n - 1)
                for j, src in enumerate(sources[4 * f:4 * f + 4]):
                    ins = nc.tensor.transpose(ps[:, (4 + n % 2) * 512 + j * P:(4 + n % 2) * 512 + (j + 1) * P], src, ident)
                ins.then_inc(A.pTr, 1)

        def transposed_dve(dve, A, fill, count, dst, l, fills=None):
            for f in fills or range(-(-count // 4)):
                n, m = fill + f, min(4, count - 4 * f)
                dve.wait_ge(A.pTr, l * A.fills + n + 1)
                nc.vector.tensor_copy(dst[:, 4 * f * P:(4 * f + m) * P], ps[:, (4 + n % 2) * 512:(4 + n % 2) * 512 + m * P]).then_inc(A.pTt, 1)

        def probs_pe(pe, A, b, fills, l=0):
            per = b.width // P
            pe.wait_ge(A.probs, l * A.batches + b.at + 1)
            transposes_pe(pe, A, b.fill, [b.L[:, r, k * P:(k + 1) * P] for r in range(b.n) for k in range(per)], l, fills)

        def values_pe(pe, A, b, l=0):
            per = b.width // P
            pe.wait_ge(A.pTt, l * A.fills + b.fill + b.copies)
            out = bank(4 + b.values % 2)
            for r, (_, vals) in enumerate(b.rows):
                for k, v in enumerate(vals):
                    ins = nc.tensor.matmul(out[:, r * HD:(r + 1) * HD], PT[:, r * per + k, :], v,
                                           start=k == 0, stop=k == per - 1)
            ins.then_inc(A.pTr, 1)

        def logits_dve(dve, ch, A, b, l=0):
            if b.sink is not None:
                ch.step(nc.vector.tensor_copy(b.L[:, :, b.width:], b.sink.unsqueeze(2)))
            dve.wait_ge(A.scores, l * A.batches + b.at + 1)
            src, dst, bias = b.ps, b.L[:, :, 0:b.width], b.bias
            if len(bias.shape) == 3 and bias.shape[1] != b.n:
                src = ps[:, 0:b.n * b.width].rearrange("p (n w) -> p n w", n=bias.shape[1])
                dst = LG[b.turn][:, 0:b.n * b.width].rearrange("p (n w) -> p n w", n=bias.shape[1])
            ch.link(nc.vector.scalar_tensor_tensor(out=dst, in0=src, scalar=SCALE, in1=bias,
                                                   op0=ALU.mult, op1=ALU.add))
            nc.vector.tensor_reduce(negm[b.turn][:, 0:b.n], b.L, AX.X, ALU.max, negate=True).then_inc(A.logits, 1)

        def probs_act(act, A, b, half, l=0):
            if half == 0:
                act.wait_ge(A.logits, l * A.batches + b.at + 1)
            for r in range(half * b.n // 2, (half + 1) * b.n // 2):
                ins = nc.scalar.activation(b.L[:, r, :], b.L[:, r, :], ACT.Exp, bias=negm[b.turn][:, r:r + 1],
                                           accum_out=sums[b.turn][:, r:r + 1])
            if half:
                ins.then_inc(A.probs, 1)

        def probs_dve(dve, ch, A, b, fills, l=0):
            transposed_dve(dve, A, b.fill, b.blocks, PT.rearrange("p k n -> p (k n)"), l, fills)
            if b.kind == "softmax" and fills[0] == 0:
                ch.step(nc.vector.reciprocal(rsum[b.turn][:, 0:b.n], sums[b.turn][:, 0:b.n]))

        def heads_dve(dve, ch, A, b, l=0):
            n = b.values
            dve.wait_ge(A.pTr, l * A.fills + n + 1)
            dst, src = O[:, b.q, b.col:b.col + b.n * HD], bank(4 + n % 2)[:, 0:b.n * HD]
            if b.kind == "softmax":
                ch.sync()
                nc.vector.tensor_tensor(dst.rearrange("p (n d) -> p n d", n=b.n), src.rearrange("p (n d) -> p n d", n=b.n),
                                        view(rsum[b.turn], [1, b.n], [0, HD]), ALU.mult).then_inc(A.pTt, 1)
            else:
                nc.vector.tensor_copy(dst, src).then_inc(A.pTt, 1)

        beta, keeps = LG, HN

        def stick_act(act, A, b):
            act.wait_ge(A.scores, b.at + 1)
            n = b.n * b.width
            nc.scalar.activation(beta[b.turn][:, 0:n], ps[:, 0:n], ACT.Sigmoid, scale=SCALE)
            nc.scalar.activation(keeps[:, b.turn, 0:n], ps[:, 0:n], ACT.Sigmoid, scale=-SCALE).then_inc(A.logits, 1)

        def stick_dve(dve, ch, A, b):
            n, w = b.n * b.width, b.width
            prod = Y.rearrange("p t d -> p (t d)")[:, 8:8 + b.n * (w + 1)].rearrange("p (n w) -> p n w", n=b.n)
            zeros = Y.rearrange("p t d -> p (t d)")[:, 1100:1100 + w]
            ch.step(nc.vector.memset(prod[:, :, w:], 1.0))
            ch.step(nc.vector.memset(zeros, 0.0))
            dve.wait_ge(A.logits, b.at + 1)
            k3 = keeps[:, b.turn, 0:n].rearrange("p (n w) -> p n w", n=b.n)
            mask = not_before[:, S - w:S]
            ch.link(nc.vector.tensor_tensor(k3, k3, view(mask, [0, b.n], [1, w]), ALU.max))
            for r in range(b.n):
                ch.step(nc.vector.tensor_tensor_scan(prod[:, r, 0:w][:, ::-1], k3[:, r, ::-1], zeros, 1.0,
                                                     ALU.mult, ALU.add))
            ch.sync()
            b3 = beta[b.turn][:, 0:n].rearrange("p (n w) -> p n w", n=b.n)
            ch.link(nc.vector.tensor_tensor(b3, b3, prod[:, :, 1:], ALU.mult))
            mask = before[:, S - w:S]
            nc.vector.tensor_tensor(b3, b3, view(mask, [0, b.n], [1, w]), ALU.mult).then_inc(A.probs, 1)

        def heads_first(batches):
            batches[-2].values += EARLY
            batches[-1].fill += EARLY
            batches[-1].values += EARLY

        def heads_parts(eng, A, fill, l, fills):
            for f in fills:
                n = fill + f
                src = bank(6 + f if f < EARLY else 4 + n % 2)
                if eng is nc.scalar:
                    eng.wait_ge(A.pTr, l * A.fills + n + 1)
                    nc.scalar.activation(two(FH, f), src, ACT.Copy).then_inc(heads_hi, 1)
                else:
                    eng.wait_ge(heads_hi, l * 4 + (0 if isinstance(l, int) else 4) + f + 1)
                    nc.vector.tensor_tensor(two(FL, f), src, two(FH, f), ALU.subtract).then_inc(A.pTt, 1)

        def turn_heads(pe, A, fill, l, fills):
            tiles = [O[:, t, c * P:(c + 1) * P] for c in range(KC) for t in range(TT)]
            if fills[0] >= EARLY:
                transposes_pe(pe, A, fill, tiles, l, fills)
                return
            for f in fills:
                for j, src in enumerate(tiles[4 * f:4 * f + 4]):
                    ins = nc.tensor.transpose(ps[:, (6 + f) * 512 + j * P:(6 + f) * 512 + (j + 1) * P], src, ident)
                ins.then_inc(A.pTr, 1)

        def early_heads_pe(pe, A, b, taken, l=0):
            pe.wait_ge(*taken)
            pe.wait_ge(A.pTt, l * A.fills + b.fill)
            turn_heads(pe, A, b.fill + b.copies, l, range(EARLY))

        def early_branch_pe(pe, A, b, g0, chunks, l=0, at=0):
            pe.wait_ge(A.pTt, l * A.fills + b.fill + b.copies + EARLY)
            for h in range(2):
                first_branch(pe, 2 * g0 + h, 0, h, chunks, at)

        def first_branch(pe, n, b, h, chunks, at):
            w = split_pe(pe, n, at)
            for c in chunks:
                product(ps[:, b * 512 + h * S:b * 512 + (h + 1) * S], cols(w, c * P, P), feat(c, 0, S), c == chunks[0], c == chunks[-1])

        def branches_pe(pe, A, fill, g0, parts, l=0, at=0):
            pe.wait_ge(A.pTt, l * A.fills + fill + EARLY)
            turn_heads(pe, A, fill, l, range(EARLY, 4))
            first_branch(pe, 2 * g0 + 2, 3, 0, parts[0], at)
            pe.wait_ge(A.pTt, l * A.fills + fill + 4)
            for g in range(BR):
                if g >= 2:
                    pe.wait_ge(br_taken, g - 1 if isinstance(l, int) else l * BR + BR + g - 1)
                group_fm(pe, g0 + g, 3 * (g % 2), at, parts=parts, done=(2, 1, 0, 0)[g])

        def merge_act(act, A, fill, g0, l=0, at=0):
            heads_parts(nc.scalar, A, fill, l, range(EARLY, 4))
            last = 2 * (g0 + BR) - 1
            for n in range(2 * g0, last):
                split_hi(act, n + SLOTS, at)
            act.wait_ge(half_done, (0 if isinstance(at, int) else at.halves) + last + 1)
            for g in range(BR):
                if g == BR - 1:
                    split_hi(act, last + SLOTS, at)
                act.wait_ge(merged, g + 1 if isinstance(l, int) else l * BR + BR + g + 1)
                nc.scalar.activation(two(FH, g), two(MT, g), ACT.Copy).then_inc(mt_hi, 1)

        def merge_dve(dve, ch, A, fill, g0, n_br, gates, l=0, at=0):
            heads_parts(nc.vector, A, fill, l, range(EARLY, 4))
            dve.wait_ge(*gates)
            done = 0 if isinstance(l, int) else l * BR + BR

            def merge(g):
                base = 0 if isinstance(at, int) else at.halves
                dve.wait_ge(half_done, base + 2 * (g0 + g) + 2)
                b = 3 * (g % 2)
                dst = two(MT, g)
                tmp = PT.rearrange("p k n -> p (k n)")[:, (g % 2) * 1024:(g % 2) * 1024 + (n_br - 1) * 512]
                for j in range(n_br):
                    ins = nc.vector.tensor_tensor(dst if j == 0 else tmp[:, (j - 1) * 512:j * 512], bank(b + j),
                                                  two(GT[:, KC * j:KC * (j + 1), :], g), ALU.mult)
                    if j < n_br - 1:
                        ch.step(ins)
                ins.then_inc(br_taken, 1)
                dve.wait_ge(br_taken, done + g + 1)
                ch.sync()
                for j in range(1, n_br):
                    ins = nc.vector.tensor_tensor(dst, dst, tmp[:, (j - 1) * 512:j * 512], ALU.add)
                    if j < n_br - 1:
                        ch.link(ins)
                ins.then_inc(merged, 1)

            def lower(g):
                dve.wait_ge(mt_hi, done + g + 1)
                nc.vector.tensor_tensor(two(FL, g), two(MT, g), two(FH, g), ALU.subtract).then_inc(mt_lo, 1)

            for g in range(BR):
                split_lo(dve, 2 * (g0 + g) + SLOTS, at)
                if g < BR - 1:
                    split_lo(dve, 2 * (g0 + g) + 1 + SLOTS, at)
                else:
                    for e in range(BR - 1):
                        lower(e)
                merge(g)
            split_lo(dve, 2 * (g0 + BR) - 1 + SLOTS, at)
            lower(BR - 1)

        def wo_pe(pe, gates, g0, l=0, at=0):
            done = 0 if isinstance(l, int) else l * BR + BR
            for n, (g, h) in enumerate(WO_ORDER):
                if g < 2:
                    pe.wait_ge(*gates)
                elif h == 0:
                    pe.wait_ge(wo_taken, g - 1 if isinstance(l, int) else l * (WO - 1) + WO + g - 1)
                half_tok(pe, 2 * g0 + n, 6 + g % 2, h, at,
                         also=(lambda c: c % 2 or pe.wait_ge(mt_lo, done + c // 2 + 1)) if g == 0 else None)

        def wo_done(g):
            return WO_ORDER.index((g, 1)) + 1

        AT1 = Attn(low_scores, scores_ready, logits_ready, probs_ready, pT_ready, pT_taken, 7, 0)
        PARTS1 = range(0, 2), range(2, 6), range(6, 8)
        PARTS2 = range(0, 4), range(4, 8)
        batches1 = []

        def add1(**kw):
            batches1.append(Batch(len(batches1), sum(b.fills for b in batches1), **kw))

        def half(tile3, c, h, sl):
            return tile3[HD * h:HD * (h + 1), c, sl]

        def rows_a(heads, q):
            rows = []
            for h in heads:
                hs = [(g * A_H + h) for g in range(A_G)]
                rows.append(([(half(aqT, j // 2, j % 2, slice(q * P, (q + 1) * P)),
                               half(akT, j // 2, j % 2, slice(0, (q + 1) * P))) for j in hs],
                             [av[:, k, j * HD:(j + 1) * HD] for j in hs for k in range(q + 1)]))
            return rows

        a_blocks = biasA.rearrange("p h g w -> p (h g) w")
        add1(rows=rows_a(range(4), 0), width=3 * P, q=0, col=0, kind="softmax", bias=a_blocks[:, :, P:S])
        for h in (0, 2):
            add1(rows=rows_a((h, h + 1), 1), width=3 * S, q=1, col=h * HD, kind="softmax",
                 bias=a_blocks[:, 3 * h:3 * h + 6, :])
        for q in range(TT):
            rows = [([(half(bqT, h % 4, h // 4, slice(q * P, (q + 1) * P)),
                       bkT[HD * (h // 4):HD * (h // 4 + 1), 0:(q + 1) * P])],
                     [bv[:, k, HD * (h // 4):HD * (h // 4 + 1)] for k in range(q + 1)]) for h in range(B_H)]
            add1(rows=rows, width=(q + 1) * P, q=q, col=A_H * HD, kind="softmax",
                 bias=biasB[:, :, (1 - q) * P:S], sink=PAR[:, P_SK:P_SK + B_H])
        for q in range(TT):
            rows = [([(half(cqT, h // 2, h % 2, slice(q * P, (q + 1) * P)),
                       half(ckT, h // 2, h % 2, slice(0, (q + 1) * P)))],
                     [cv[:, k, h * HD:(h + 1) * HD] for k in range(q + 1)]) for h in range(C_H)]
            add1(rows=rows, width=(q + 1) * P, q=q, col=(A_H + B_H) * HD, kind="stick")
        fill_o1 = sum(b.fills for b in batches1)
        heads_first(batches1)

        def turned(b):
            return ["G", ("T", b, range(0, min(2, b.copies)))] + (["G", ("T", b, range(2, b.copies))] if b.copies > 2 else ["G"])

        def attention(batches):
            order = []
            for b in batches[1:]:
                order += [("S", b)] + ([("V", batches[b.at - 2])] if b.at > 1 else []) + turned(batches[b.at - 1])
            return order

        def last_steps(batches):
            b, last = batches[-2:]
            return [("O", b), ("V", b), ("T", last, range(last.copies)), ("P", b), ("V", last)]

        order1 = ["G"] * 9 + ["B", "G", ("S", batches1[0]), "G", "G"] + attention(batches1)
        order1 += ["G"] * (IN_QKV + IN_GATE - order1.count("G")) + last_steps(batches1)
        assert order1.count("G") == IN_QKV + IN_GATE

        QK_FILLS = (4, 3)
        qk_fill = (0, QK_FILLS[0])
        batches2 = []
        for kind in range(2):
            for q in range(TT):
                rows = []
                for h in range(NQ):
                    if kind == 0:
                        c, k, part = h // 2, 4 + h // 2, h % 2
                        vals = [va[:, t, h * HD:(h + 1) * HD] for t in range(TT)]
                    else:
                        c, k, part = 8 + h % 4, 12, h // 4
                        vals = [vb[:, t, HD * part:HD * (part + 1)] for t in range(TT)]
                    rows.append(([(half(qkT, c, part, slice(q * P, (q + 1) * P)), half(qkT, k, part, slice(0, S)))], vals))
                if kind == 0:
                    bias, sink = naB[:, :, (2 - 2 * q) * GRID_W:(2 - 2 * q) * GRID_W + S], None
                else:
                    bias = view(CONST[:, C_SW + q * S:C_SW + q * S + S], [0, NQ], [1, S])
                    sink = PAR[:, Q_SK:Q_SK + NQ]
                batches2.append(Batch(len(batches2), sum(QK_FILLS) + sum(b.fills for b in batches2), rows=rows, width=S, q=q,
                                      col=kind * NQ * HD, kind="softmax", bias=bias, sink=sink))
        fill_o2 = sum(QK_FILLS) + sum(b.fills for b in batches2)
        heads_first(batches2)
        L_FILLS = fill_o2 + 4
        AT2 = Attn(llow_scores, lscores_ready, llogits_ready, lprobs_ready, lpT_ready, lpT_taken, 4, L_FILLS)
        order2 = ["G"] * (L_PROJ - 2) + [("Q", 0, range(0, 2)), "G", ("Q", 0, range(2, 4)), "G",
                                         ("S", batches2[0]), "G", "G", ("Q", 1, range(0, 2)), ("Q", 1, range(2, 3))]
        order2 += attention(batches2) + last_steps(batches2)
        assert order2.count("G") == L_PROJ + L_GATE
        N2 = L_PROJ + L_GATE + L_PQ

        block = ctx.enter_context(nc.Block())

        @block.sync
        def _(sp):
            sp.dma_start(X[:, :, :], x_in.rearrange("(t p) d -> p t d", p=P)).then_inc(x_loaded, 16)
            sp.dma_start(CONST[:, :], consts).then_inc(const_loaded, 16)
            for n in range(SLOTS):
                sp.dma_start(W[:, n, :], wstream[n]).then_inc(w_landed[n], 16)
            whole = (HALVES - SLOTS) // SLOTS
            with sp.Fori(0, whole) as k:
                for s in range(SLOTS):
                    sp.wait_ge(w_lo, k * SLOTS + s + 1)
                    sp.dma_start(W[:, s, :], wstream[k * SLOTS + SLOTS + s]).then_inc(w_landed[s], 16)
            for n in range(SLOTS + whole * SLOTS, HALVES):
                sp.wait_ge(w_lo, n - SLOTS + 1)
                sp.dma_start(W[:, n % SLOTS, :], wstream[n]).then_inc(w_landed[n % SLOTS], 16)
            sp.wait_ge(x_ready, 2 * TT + 3 * LAYERS)
            sp.dma_start(out.rearrange("(t p) d -> p t d", p=P), X[:, :, :]).then_inc(out_stored, 16)
            sp.wait_ge(out_stored, 16)

        @block.gpsimd
        def _(pool):
            nc.gpsimd.memset(ZERO[:, :], 0.0)
            nc.gpsimd.memset(lbase, 0.0).then_inc(zeroed, 1)
            for l in range(LAYERS):
                for r in range(2):
                    for h in range(NQ):
                        pool.wait_ge(half_done, F_HALF + 2 + 2 * ((l * 2 + r) * NQ + h))
                        at = ((l * NQ + h) * RPB_R + 5 - r) * GRID_W * RPB_PAD + GRID_W - 1
                        pool.dma_start(na_rows[l, r * GRID_W:(r + 1) * GRID_W, h, :].rearrange("p (k n) -> p k n", k=NA_KK),
                                       bass.AP(tensor=rpb.tensor, offset=at, ap=[[RPB_PAD - 1, GRID_W], [GRID_W * RPB_PAD, NA_KK], [1, GRID_W]])).then_inc(na_stored, 16)
            pool.wait_ge(const_loaded, 16)
            with pool.Fori(0, LAYERS) as l:
                wait_alone(pool, qk_normed, l + 1, pool_passed)
                q4 = QK[:, :, 2 * NQ * HD:].rearrange("p t (h s d) -> p t h s d", s=2, d=32)
                x1, x2 = q4[:, :, :, 0, :], q4[:, :, :, 1, :]
                cos = view(CONST[:, C_COS:C_COS + 1], [32, TT], [0, 10], [1, 32])
                sin = view(CONST[:, C_SIN:C_SIN + 1], [32, TT], [0, 10], [1, 32])
                r4 = [rots[j // 2][:, j % 2, :].rearrange("p (t h d) -> p t h d", t=TT, h=10) for j in range(4)]
                for j, (a, c) in enumerate(((x1, cos), (x2, sin), (x1, sin), (x2, cos))):
                    nc.gpsimd.tensor_tensor(r4[j], a, c, ALU.mult).then_inc(turned_parts, 1)
                wait_alone(pool, turned_parts, l * 4 + 4, pool_passed)
                nc.gpsimd.tensor_tensor(x1, r4[0], r4[1], ALU.subtract).then_inc(qk_ready, 1)
                nc.gpsimd.tensor_tensor(x2, r4[2], r4[3], ALU.add).then_inc(qk_ready, 1)
                with pool.Fori(0, STEPS // 2) as i:
                    for b in range(2):
                        wait_alone(pool, routed, l * ROUTES + i * 2 + b + 1, pool_passed)
                        for c in range(PASSES):
                            use = l * USES + i * (2 * PASSES) + b * PASSES + c
                            for q in range(SETS):
                                if (b, c, q) == (0, 0, 1):
                                    for n in range(L_HALF + L_HALVES - SLOTS, L_HALF + L_HALVES):
                                        wait_alone(pool, w_landed[n % SLOTS], At(l, L_HALVES).landed + 16 * (n // SLOTS + 1), pool_passed)
                                wait_alone(pool, set_used[q], use + 1, pool_passed)
                                for r in range(q * SET, (q + 1) * SET):
                                    nc.gpsimd.indirect_dma_start(
                                        ring[:, r, :], None, experts,
                                        bass.IndirectOffsetOnAxis(ap=EIDX[:, b, c * RING + r:c * RING + r + 1], axis=0)).then_inc(g_landed[r], 16)

        @block.tensor
        def _(pe):
            for q in range(SETS):
                pe.sem_inc(set_used[q], 1)
            pe.wait_ge(zeroed, 1)
            keep_warm(pe, 4, 0)
            pe.wait_ge(bias_in, 32)
            for v in range(VAR):
                ins = nc.tensor.matmul(bank(4 + v)[0:20, 0:EW], relb_sb[0:NB_BUCKETS + 1, :],
                                       ohot[0:NB_BUCKETS + 1, v * EW:(v + 1) * EW], start=True, stop=True)
            ins.then_inc(erow_ready, 1)
            pe.wait_ge(const_loaded, 16)
            norm_pe(pe, n_attn, 0)
            pe.wait_ge(erow_copied, 1)
            g = 0
            for what in order1:
                if what == "G":
                    if g >= 2:
                        pe.wait_ge(proj_taken, g - 1)
                    token_major = g in TOK_1
                    if g == 11:
                        b = (6 + g % 2) * 512
                        for h in range(2):
                            w = split_pe(pe, 2 * g + h)
                            for t in range(h * TT + 1 - h):
                                for c in range(KC):
                                    out = ps[:, b:b + S] if h == 0 else ps[:, b + S + t * P:b + S + (t + 1) * P]
                                    k = feat(c, 0, S) if h == 0 else feat(c, t * P, P)
                                    stat, mov = (cols(w, c * P, P), k) if h == 0 else (k, cols(w, c * P, P))
                                    ins = product(out, stat, mov, c == 0, c == KC - 1)
                            ins.then_inc(half_done, 1)
                    elif token_major:
                        group_tok(pe, g, 6 + g % 2)
                    else:
                        group_fm(pe, g, 6 + g % 2, also=(lambda c: c % 2 or pe.wait_ge(n_attn.hT, c // 2 + 1)) if g == 0 else None)
                    g += 1
                elif what == "B":
                    pe.wait_ge(bias_loaded, 64)
                    for n in range(BIAS_FILLS):
                        if n >= 4:
                            pe.wait_ge(bias_taken, n - 3)
                        nc.tensor.matmul(bank(n % 4), turn, hank[:, n * 512:(n + 1) * 512], start=True, stop=True).then_inc(bias_turned, 1)
                    pe.wait_ge(bias_taken, BIAS_FILLS)
                elif what[0] == "S":
                    b = what[1]
                    pe.wait_ge(proj_taken, 9 if b.at < 3 else 12 if b.at < 5 else 15)
                    scores_pe(pe, AT1, b)
                elif what[0] == "T":
                    probs_pe(pe, AT1, what[1], what[2])
                elif what[0] == "O":
                    early_heads_pe(pe, AT1, what[1], (proj_taken, IN_QKV + IN_GATE))
                elif what[0] == "P":
                    early_branch_pe(pe, AT1, what[1], G_BR, PARTS1[0])
                else:
                    values_pe(pe, AT1, what[1])
            branches_pe(pe, AT1, fill_o1, G_BR, PARTS1)
            wo_pe(pe, (proj_taken, IN_QKV + IN_GATE), G_WO)
            keep_warm(pe, 10)
            norm_pe(pe, n_ffn, 0)
            def down(n, at, gated, last):
                for j in range(2):
                    pe.wait_ge(ff_gated, gated + j + 1)
                    w = split_pe(pe, n + j, at)
                    for t in range(TT):
                        for h in range(2):
                            ins = product(bank(2 * t + h), cols((FGH[:, j, :], FGL[:, j, :]), t * P, P), cols(w, h * 512, 512),
                                          False, last and j == 1)
                    ins.then_inc(half_done, 1)

            for j in range(2):
                group_fm(pe, G_FF + j, 6 + j, also=(lambda c: c % 2 or pe.wait_ge(n_ffn.hT, c // 2 + 1)) if j == 0 else None)
            for b in range(4):
                nc.tensor.matmul(bank(b), ZERO[:, 0:P], ZERO[:, :], start=True, stop=False)
            with pe.Fori(0, FF_BLOCKS // 2 - 1) as i:
                at = At(i, F_BODY)
                for j in range(2):
                    pe.wait_ge(ff_conv, i * 2 + j + 1)
                    group_fm(pe, G_FF + 2 + j, 6 + j, at)
                down(F_HALF + 8, at, i * 2, False)
            down(L_HALF - 2, 0, FF_BLOCKS - 2, True)

            keep_warm(pe, 6)
            with pe.Fori(0, LAYERS) as l:
                at = At(l, L_HALVES)
                keep_warm(pe, 5)
                norm_pe(pe, n_mix, l)
                g = 0
                for what in order2:
                    if what == "G":
                        if g >= 2:
                            pe.wait_ge(lproj_taken, l * N2 + g - 1)
                        (group_tok if g < L_PROJ else group_fm)(pe, G_LAYER + g, 6 + g % 2, at, also=(
                            lambda c: c % 2 or pe.wait_ge(n_mix.hT, l * 4 + c // 2 + 1)) if g == 0 else None)
                        g += 1
                    elif what[0] == "Q":
                        part = what[1]
                        h0, h1 = QK_PARTS[part]
                        pe.wait_ge(qk_ready, l * 3 + 2 * part + 1)
                        transposes_pe(pe, AT2, qk_fill[part], [QK[:, t, c * P:(c + 1) * P] for c in range(h0 // 2, h1 // 2) for t in range(TT)],
                                      l, what[2])
                    elif what[0] == "S":
                        part = what[1].at // TT
                        pe.wait_ge(lpT_taken, l * L_FILLS + qk_fill[part] + QK_FILLS[part])
                        scores_pe(pe, AT2, what[1], l)
                    elif what[0] == "T":
                        pe.wait_ge(lproj_taken, l * N2 + L_PROJ)
                        probs_pe(pe, AT2, what[1], what[2], l)
                    elif what[0] == "O":
                        early_heads_pe(pe, AT2, what[1], (lproj_taken, l * N2 + L_PROJ + L_GATE), l)
                    elif what[0] == "P":
                        early_branch_pe(pe, AT2, what[1], G_LAYER + LG_BR, PARTS2[0], l, at)
                    else:
                        values_pe(pe, AT2, what[1], l)
                branches_pe(pe, AT2, fill_o2, G_LAYER + LG_BR, PARTS2, l, at)
                wo_pe(pe, (lproj_taken, l * N2 + L_PROJ + L_GATE), G_LAYER + LG_WO, l, at)
                keep_warm(pe, 7)
                norm_pe(pe, n_peer, l)

                def key_scores(h):
                    pe.wait_ge(lproj_taken, l * N2 + L_PROJ + L_GATE + h + 1)
                    if h >= 2:
                        pe.wait_ge(sc_ready, l * PH + h - 1)
                    for t in range(TT):
                        for s in range(2):
                            ins = nc.tensor.matmul(ps[:, (4 + h % 2) * 512 + (t * 2 + s) * NKEY:(4 + h % 2) * 512 + (t * 2 + s + 1) * NKEY],
                                                   pqT[:, 2 * h + s, t * P:(t + 1) * P],
                                                   PAR[:, Q_KEYS + s * NKEY:Q_KEYS + (s + 1) * NKEY], start=True, stop=True)
                    ins.then_inc(sc_done, 1)

                for j in range(L_PQ):
                    if j >= 2:
                        pe.wait_ge(lproj_taken, l * N2 + L_PROJ + L_GATE + j - 1)
                    group_fm(pe, G_LAYER + LG_PQ + j, 6 + j % 2, at, also=(
                        lambda c: c % 2 or pe.wait_ge(n_peer.hT, l * 4 + c // 2 + 1)) if j == 0 else None)
                    if j != 1:
                        key_scores(max(j - 1, 0))
                key_scores(PH - 1)
                for t in range(TT):
                    for h in range(2):
                        nc.tensor.matmul(bank(2 * t + h), ZERO[:, 0:P], ZERO[:, :], start=True, stop=False)
                    with pe.Fori(0, PH * PASSES) as i:
                        use = l * USES + i + t * PH * PASSES
                        for q in range(SETS):
                            pe.wait_ge(diag_ready, use * SETS + q + 1)
                            for r in range(q * SET, (q + 1) * SET):
                                for h in range(2):
                                    ins = nc.tensor.matmul(bank(2 * t + h), DIAG[:, r, :], ring[:, r, D + h * 512:D + (h + 1) * 512],
                                                           start=False, stop=False)
                            ins.then_inc(set_used[q], 1)
                    for h in range(2):
                        ins = nc.tensor.matmul(bank(2 * t + h), ZERO[:, 0:P], ZERO[:, :], start=False, stop=True)
                    ins.then_inc(acc_ready, 1)

        @block.scalar
        def _(act):
            act.dma_start(relb_sb[0:NB_BUCKETS + 1, :], relb).then_inc(bias_in, 16)
            act.dma_start(ohot[0:NB_BUCKETS + 1, :], onehot).then_inc(bias_in, 16)
            act.dma_start(PAR[:, 0:P_CV], par1[:, 0:P_CV]).then_inc(gains1_loaded, 16)
            act.dma_start(PAR[:, P_CV:P_END], par1[:, P_CV:P_END]).then_inc(par1_loaded, 16)
            act.wait_ge(x_loaded, 16)
            norm_act(act, n_attn, stream, 0, rows=True)
            act.wait_ge(erow_ready, 1)
            for v in range(VAR):
                ins = nc.scalar.activation(erow[0:20, v * EW:(v + 1) * EW], bank(4 + v)[0:20, 0:EW], ACT.Copy)
            ins.then_inc(erow_copied, 1)
            act.wait_ge(erow_copied, 1)
            act.dma_start(scratch, erow[0:20, :]).then_inc(erow_stored, 16)
            act.wait_ge(gains1_loaded, 16)
            norm_act_hi(act, n_attn, 0, PAR[:, P_G1:P_G1 + KC], first=0)
            act.wait_ge(erow_stored, 16)
            for gi in range(A_G):
                act.dma_start(hankA[:, :, gi, :], bass.AP(tensor=scratch.tensor, offset=gi * A_H * VAR * EW + gi * EW,
                                                          ap=[[1, P], [VAR * EW, A_H], [1, S]])).then_inc(bias_loaded, 16)
            act.dma_start(hankB, bass.AP(tensor=scratch.tensor, offset=A_G * A_H * VAR * EW + 3 * EW,
                                         ap=[[1, P], [VAR * EW, B_H], [1, S]])).then_inc(bias_loaded, 16)
            act.wait_ge(par1_loaded, 16)

            def take1(g):
                act.wait_ge(half_done, 2 * g + 2)
                src = bank(6 + g % 2)
                t2 = src.rearrange("p (t n) -> p t n", t=TT)
                if g < 3:
                    ins = nc.scalar.activation(aqT[:, 2 * g:2 * g + 2, :], t2, ACT.Copy)
                elif g < 6:
                    ins = nc.scalar.activation(akT[:, 2 * g - 6:2 * g - 4, :], t2, ACT.Copy)
                elif g < 9:
                    ins = nc.scalar.activation(av[:, :, (g - 6) * GC:(g - 5) * GC], t2, ACT.Copy)
                elif g < 11:
                    ins = nc.scalar.activation(bqT[:, 2 * (g - 9):2 * (g - 8), :], t2, ACT.Copy)
                elif g == 11:
                    nc.scalar.activation(bkT, src[:, 0:S], ACT.Copy)
                    ins = nc.scalar.activation(bv, src[:, S:2 * S].rearrange("p (t n) -> p t n", t=TT), ACT.Copy)
                elif g < 15:
                    ins = nc.scalar.activation((cqT, ckT, cv)[g - 12], t2, ACT.Copy)
                else:
                    for j in range(2):
                        f = 2 * (g - G_GATE) + j
                        ins = nc.scalar.activation(GT[:, f, :], t2[:, j, :], ACT.Identity, bias=PAR[:, P_BG + f:P_BG + f + 1])
                ins.then_inc(proj_taken, 1)

            def gates_act(count, taken):
                act.wait_ge(*taken)
                gt = GT[:, 0:count, :].rearrange("p f n -> p (f n)")
                nc.scalar.activation(gt, gt, ACT.Sigmoid).then_inc(gates_on, 1)

            g, due = 0, []
            for what in order1:
                if what == "G":
                    split_hi(act, 2 * g + SLOTS)
                    if due:
                        probs_act(act, AT1, *due.pop(0))
                    split_hi(act, 2 * g + 1 + SLOTS)
                    take1(g)
                    g += 1
                elif what[0] == "S" and what[1].kind == "softmax":
                    due += [(what[1], 0), (what[1], 1)]
                elif what[0] == "S":
                    for b, half in due:
                        probs_act(act, AT1, b, half)
                    due = []
                    stick_act(act, AT1, what[1])
                elif what[0] == "O":
                    heads_parts(nc.scalar, AT1, what[1].fill + what[1].copies, 0, range(EARLY))
            gates_act(3 * KC, (proj_taken, IN_QKV + IN_GATE))
            merge_act(act, AT1, fill_o1, G_BR)
            for n in range(2 * G_WO, 2 * (G_WO + WO)):
                split_hi(act, n + SLOTS)
            root_table(300)
            squares_act(act, unnormed, (wo_taken, WO - 1))
            act.wait_ge(wo_taken, WO)
            norm_act(act, n_post, unnormed, 0, first=EARLY_D)
            norm_act(act, n_ffn, stream, 0, ready=0, rows=True)
            norm_act_hi(act, n_ffn, 0, PAR[:, P_G2:P_G2 + KC])

            def ff_init_act(j, cvw, done):
                act.wait_ge(half_done, done)
                for gv in range(2):
                    ins = nc.scalar.activation(ffacc[:, j, gv, :], bank(6 + j)[:, gv * S:(gv + 1) * S], ACT.Identity,
                                               scale=cvw(gv, 2), bias=cvw(gv, 3))
                ins.then_inc(ff_init, 1)

            def ff_gelu_act(blk, j):
                act.wait_ge(ff_conv, blk + 1)
                nc.scalar.activation(ffacc[:, j, 0, :], ffacc[:, j, 0, :], ACT.Gelu_apprx_tanh).then_inc(ff_gelu, 1)

            def static_taps(n):
                return lambda gv, k: PAR[:, P_CV + n * 8 + gv * 4 + k:P_CV + n * 8 + gv * 4 + k + 1]

            split_hi(act, F_HALF + 3)
            for j in range(2):
                ff_init_act(j, static_taps(j), F_HALF + 2 * j + 2)
                if j == 0:
                    split_hi(act, F_HALF + 4)
                ff_gelu_act(j, j)
                if j == 0:
                    split_hi(act, F_HALF + 5)
            with act.Fori(0, FF_BLOCKS // 2 - 1) as i:
                at = At(i, F_BODY)
                split_hi(act, F_HALF + 6, at)
                for j in range(2):
                    def taps(gv, k):
                        return PAR[:, bass.ds(i * 16 + (P_CV + 16 + j * 8 + gv * 4 + k), 1)]
                    split_hi(act, F_HALF + 7 + 2 * j, at)
                    act.wait_ge(ff_prod, i * 2 + j + 1)
                    ff_init_act(j, taps, at.halves + F_HALF + 6 + 2 * j)
                    split_hi(act, F_HALF + 8 + 2 * j, at)
                    ff_gelu_act(i * 2 + 2 + j, j)
                split_hi(act, F_HALF + 11, at)
            root_table(301)
            act.wait_ge(half_done, L_HALF)
            norm_act(act, n_fpost, ff_result, 0, between=lambda: act.wait_ge(ff_gained, 1), one=ff_squared)

            act.wait_ge(na_stored, LAYERS * 2 * NQ * 16)
            with act.Fori(0, LAYERS) as l:
                at = At(l, L_HALVES)

                def load():
                    act.dma_start(PAR[:, 0:Q_SK], par2[l, :, 0:Q_SK]).then_inc(gains2_loaded, 16)
                    act.dma_start(PAR[:, Q_SK:Q_END], par2[l, :, Q_SK:Q_END]).then_inc(par2_loaded, 16)
                    act.dma_start(naB, na_rows[l]).then_inc(na_loaded, 16)

                root_table(302)
                norm_act(act, n_mix, stream, l, ready=l * 3 + TT, between=load, rows=True)
                act.wait_ge(gains2_loaded, l * 16 + 16)
                norm_act_hi(act, n_mix, l, PAR[:, Q_G:Q_G + KC], first=L_HALF, at=at)

                def take2(g):
                    act.wait_ge(half_done, at.halves + L_HALF + 2 * g + 2)
                    t2 = bank(6 + g % 2).rearrange("p (t n) -> p t n", t=TT)
                    if g < 6:
                        ins = nc.scalar.activation(QK[:, :, g * GC:(g + 1) * GC], t2, ACT.Copy)
                    elif g == 6:
                        nc.scalar.activation(QK[:, :, 6 * GC:6 * GC + P], t2[:, :, 0:P], ACT.Copy)
                        ins = nc.scalar.activation(vb, t2[:, :, P:2 * P], ACT.Copy)
                    elif g < 9:
                        ins = nc.scalar.activation(va[:, :, (g - 7) * GC:(g - 6) * GC], t2, ACT.Copy)
                    else:
                        for j in range(2):
                            f = 2 * (g - L_PROJ) + j
                            ins = nc.scalar.activation(GT[:, f, :], t2[:, j, :], ACT.Identity, bias=PAR[:, Q_BG + f:Q_BG + f + 1])
                    ins.then_inc(lproj_taken, 1)
                    for part, last in enumerate((3, 6)):
                        h0, h1 = QK_PARTS[part]
                        if g == last:
                            act.wait_ge(lproj_taken, l * N2 + last + 1)
                            nc.scalar.activation(qksq[part], QK[:, :, h0 * HD:h1 * HD], ACT.Square).then_inc(qksq_ready, 1)
                        elif g == last + 1:
                            act.wait_ge(qkvar_ready, l * 2 + part + 1)
                            nc.scalar.activation(hrstd[part], hssq[part], ACT.Sqrt).then_inc(qkstd_ready, 1)

                g, due = 0, []
                for what in order2:
                    if what == "G":
                        split_hi(act, L_HALF + 2 * g + SLOTS, at)
                        if due:
                            probs_act(act, AT2, *due.pop(0), l)
                        split_hi(act, L_HALF + 2 * g + 1 + SLOTS, at)
                        take2(g)
                        g += 1
                    elif what[0] == "S":
                        due += [(what[1], 0), (what[1], 1)]
                    elif what[0] == "O":
                        heads_parts(nc.scalar, AT2, what[1].fill + what[1].copies, l, range(EARLY))
                gates_act(2 * KC, (lproj_taken, l * N2 + L_PROJ + L_GATE))
                merge_act(act, AT2, fill_o2, G_LAYER + LG_BR, l, at)
                for n in range(2 * LG_WO, 2 * LG_PQ):
                    split_hi(act, L_HALF + n + SLOTS, at)
                root_table(303)
                squares_act(act, stream, (wo_taken, l * (WO - 1) + WO + WO - 1))
                act.wait_ge(x_ready, l * 3 + 2 * TT + 1)
                norm_act(act, n_peer, stream, l, first=EARLY_D)
                norm_act_hi(act, n_peer, l, None)

                def gate_exp(k):
                    act.wait_ge(topd_ready, l * ROUTES + k + 1)
                    nc.scalar.activation(topv, topv, ACT.Exp, bias=topneg, accum_out=esum).then_inc(texp_ready, 1)

                def take_scores(h):
                    act.wait_ge(sc_done, l * PH + h + 1)
                    nc.scalar.activation(SC[:, 0:STEPS, :, :].rearrange("p (t h) s n -> p t h (s n)", h=PH)[:, :, h, :],
                                         bank(4 + h % 2).rearrange("p (t n) -> p t n", t=TT), ACT.Copy).then_inc(sc_ready, 1)

                for j in range(L_PQ):
                    n = 2 * (LG_PQ + j) + SLOTS
                    if n < L_HALVES:
                        split_hi(act, L_HALF + n, at)
                    act.wait_ge(half_done, at.halves + L_HALF + 2 * (LG_PQ + j) + 2)
                    nc.scalar.activation(pqT[:, 2 * j:2 * j + 2, :], bank(6 + j % 2).rearrange("p (t n) -> p t n", t=TT),
                                         ACT.Copy).then_inc(lproj_taken, 1)
                    if n + 1 < L_HALVES:
                        split_hi(act, L_HALF + n + 1, at)
                    if j != 1:
                        take_scores(max(j - 1, 0))
                    if j == 4:
                        gate_exp(0)
                take_scores(PH - 1)

                for t in range(TT):
                    with act.Fori(0, PH) as i:
                        for c in range(PASSES):
                            use = l * USES + i * PASSES + t * PH * PASSES + c

                            def gelu(q):
                                act.wait_ge(dots_ready, use * SETS + q + 1)
                                nc.scalar.activation(ga[:, q * SET:(q + 1) * SET], hd[:, q * SET:(q + 1) * SET], ACT.Gelu).then_inc(gelu_ready, 1)

                            def diagonals(q):
                                act.wait_ge(w_ready, use * SETS + q + 1)
                                for r in range(q * SET, (q + 1) * SET):
                                    ins = nc.scalar.activation(DIAG[:, r, :], ident, ACT.Copy, scale=gw8[:, r:r + 1])
                                ins.then_inc(diag_ready, 1)

                            gelu(0)
                            for q in range(1, SETS):
                                if c == 0 and q == SETS - 1:
                                    gate_exp(i + t * PH + 1)
                                gelu(q)
                                diagonals(q - 1)
                            diagonals(SETS - 1)

        @block.vector
        def _(dve):
            ch = Chain(dve, dve_step)
            dve.wait_ge(x_loaded, 16)
            norm_dve_pre(dve, n_attn, 0, PAR[:, P_G1:P_G1 + KC], None, first=0)
            dve.wait_ge(par1_loaded, 16)
            dve.wait_ge(const_loaded, 16)

            def take_bias():
                for n in range(BIAS_FILLS):
                    dve.wait_ge(bias_turned, n + 1)
                    nc.vector.tensor_copy(bias_all[:, n * 512:(n + 1) * 512], bank(n % 4)).then_inc(bias_taken, 1)
                dve.wait_ge(bias_taken, BIAS_FILLS)

            stick = None
            g, later = 0, []
            for what in order1:
                if what[0] in "GSP":
                    for n in later:
                        split_lo(dve, n)
                    later = []
                if what == "G":
                    split_lo(dve, 2 * g + SLOTS)
                    later = [2 * g + SLOTS + 1]
                    g += 1
                    if stick:
                        stick_dve(dve, ch, AT1, stick)
                        stick = None
                elif what == "B":
                    take_bias()
                elif what[0] == "T":
                    probs_dve(dve, ch, AT1, what[1], what[2])
                elif what[0] == "V":
                    heads_dve(dve, ch, AT1, what[1])
                elif what[0] == "O":
                    heads_parts(nc.vector, AT1, what[1].fill + what[1].copies, 0, range(EARLY))
                elif what[0] == "P":
                    pass
                elif what[1].kind == "softmax":
                    logits_dve(dve, ch, AT1, what[1])
                else:
                    stick = what[1]
            merge_dve(dve, ch, AT1, fill_o1, G_BR, 3, (gates_on, 1))
            for g in range(WO):
                for n in range(2 * (G_WO + g) + SLOTS, 2 * (G_WO + g) + SLOTS + 2):
                    split_lo(dve, n)
                dve.wait_ge(half_done, 2 * G_WO + wo_done(g))
                nc.vector.tensor_copy(Y[:, :, g * GC:(g + 1) * GC], bank(6 + g % 2).rearrange("p (t n) -> p t n", t=TT)).then_inc(wo_taken, 1)
                dve.wait_ge(wo_taken, g + 1)
                ch.step(nc.vector.tensor_tensor(YG[:, :, g * GC:(g + 1) * GC], Y[:, :, g * GC:(g + 1) * GC],
                                                view(PAR[:, P_POST + g * GC:P_POST + (g + 1) * GC], [0, TT], [1, GC]), ALU.mult))
            norm_dve_post(dve, ch, n_post, YG, split=TT)
            dve.wait_ge(x_ready, TT)
            norm_dve_pre(dve, n_ffn, 0, PAR[:, P_G2:P_G2 + KC], None)

            def ff_conv_dve(blk, j, taps):
                dve.wait_ge(ff_init, blk + 1)
                for back, k in ((1, 1), (2, 0)):
                    for gv in range(2):
                        acc = ffacc[:, j, gv, back:S]
                        ins = nc.vector.scalar_tensor_tensor(out=acc, in0=bank(6 + j)[:, gv * S:(gv + 1) * S - back], scalar=taps(gv, k),
                                                             in1=acc, op0=ALU.mult, op1=ALU.add)
                        if back == 1:
                            ch.step(ins)
                    if back == 1:
                        ch.sync()
                ins.then_inc(ff_conv, 1)

            def ff_gate_dve(blk, j):
                dve.wait_ge(ff_gelu, blk + 1)
                nc.vector.tensor_tensor(ffp[:, j, :], ffacc[:, j, 0, :], ffacc[:, j, 1, :], ALU.mult).then_inc(ff_prod, 1)

            def ff_parts_dve(blk, j):
                dve.wait_ge(ff_prod, blk + 1)
                nc.vector.tensor_copy(FGH[:, j, :], ffp[:, j, :]).then_inc(ff_hi, 1)
                dve.wait_ge(ff_hi, blk + 1)
                nc.vector.tensor_tensor(FGL[:, j, :], ffp[:, j, :], FGH[:, j, :], ALU.subtract).then_inc(ff_gated, 1)

            def static_taps(n):
                return lambda gv, k: PAR[:, P_CV + n * 8 + gv * 4 + k:P_CV + n * 8 + gv * 4 + k + 1]

            split_lo(dve, F_HALF + 3)
            for j in range(2):
                ff_conv_dve(j, j, static_taps(j))
                if j == 0:
                    split_lo(dve, F_HALF + 4)
                ff_gate_dve(j, j)
                ff_parts_dve(j, j)
                if j == 0:
                    split_lo(dve, F_HALF + 5)
            with ch.loop(FF_BLOCKS // 2 - 1, 4) as i:
                at = At(i, F_BODY)
                split_lo(dve, F_HALF + 6, at)
                for j in range(2):
                    def taps(gv, k):
                        return PAR[:, bass.ds(i * 16 + (P_CV + 16 + j * 8 + gv * 4 + k), 1)]
                    split_lo(dve, F_HALF + 7 + 2 * j, at)
                    ff_conv_dve(i * 2 + 2 + j, j, taps)
                    split_lo(dve, F_HALF + 8 + 2 * j, at)
                    ff_gate_dve(i * 2 + 2 + j, j)
                split_lo(dve, F_HALF + 11, at)
                for j in range(2):
                    dve.wait_ge(half_done, at.halves + F_HALF + 9 + j)
                    ff_parts_dve(i * 2 + 2 + j, j)
            dve.wait_ge(half_done, L_HALF)
            nc.vector.tensor_tensor(Y[:, 1, :], ff_result(1), PAR[:, P_FPOST:P_FPOST + D], ALU.mult).then_inc(ff_gained, 1)
            dve.wait_ge(ff_squared, 1)
            ch.step(nc.vector.tensor_tensor(Y[:, 0, :], ff_result(0), PAR[:, P_FPOST:P_FPOST + D], ALU.mult))
            dve.wait_ge(ff_gained, 1)
            norm_dve_post(dve, ch, n_fpost, Y)

            dve.wait_ge(zeroed, 1)
            ch.restart()
            with dve.Fori(0, LAYERS) as l:
                dve.wait_ge(x_ready, l * 3 + 2 * TT)
                at = At(l, L_HALVES)
                norm_dve_pre(dve, n_mix, l, PAR[:, Q_G:Q_G + KC], None, first=L_HALF, at=at)
                dve.wait_ge(par2_loaded, l * 16 + 16)
                dve.wait_ge(na_loaded, l * 16 + 16)
                na4 = naB.rearrange("p h (k n) -> p (h k) n", k=NA_KK)
                ch.step(nc.vector.tensor_tensor(na4, na4, view(CONST[:, C_NA:C_NA + GRID_W], [0, NQ * NA_KK], [1, GRID_W]), ALU.add))
                def los(g):
                    for n in range(2 * g + SLOTS, min(2 * g + SLOTS + 2, L_HALVES)):
                        split_lo(dve, L_HALF + n, at)

                def heads_var(part):
                    dve.wait_ge(qksq_ready, l * 2 + part + 1)
                    ch.link(nc.vector.tensor_reduce(hssq[part], qksq[part].rearrange("p t (h d) -> p (t h) d", d=HD), AX.X, ALU.add))
                    nc.vector.tensor_scalar(hssq[part], hssq[part], 1.0 / HD, EPS, ALU.mult, ALU.add).then_inc(qkvar_ready, 1)

                def heads_normed(part):
                    h0, h1 = QK_PARTS[part]
                    n = h1 - h0
                    dve.wait_ge(qkstd_ready, l * 2 + part + 1)
                    ch.link(nc.vector.reciprocal(hrstd[part], hrstd[part]))
                    qk = QK[:, :, h0 * HD:h1 * HD]
                    qk4 = qk.rearrange("p t (h d) -> p t h d", d=HD)
                    ch.link(nc.vector.tensor_tensor(qk4, qk4, view(hrstd[part], [n, TT], [1, n], [0, HD]), ALU.mult))
                    return nc.vector.tensor_tensor(qk, qk, view(PAR[:, Q_QKN + h0 * HD:Q_QKN + h1 * HD], [0, TT], [1, n * HD]), ALU.mult)

                g, later = 0, []
                for what in order2:
                    if what[0] in "GSP":
                        for n in later:
                            split_lo(dve, n, at)
                        later = []
                    if what == "G":
                        split_lo(dve, L_HALF + 2 * g + SLOTS, at)
                        later = [L_HALF + 2 * g + SLOTS + 1]
                        if g in (3, 6):
                            split_lo(dve, later.pop(), at)
                            heads_var(0 if g == 3 else 1)
                        elif g == 4:
                            split_lo(dve, later.pop(), at)
                            heads_normed(0).then_inc(qk_ready, 1)
                        elif g == 8:
                            heads_normed(1).then_inc(qk_normed, 1)
                        g += 1
                    elif what[0] == "S":
                        logits_dve(dve, ch, AT2, what[1], l)
                    elif what[0] == "Q":
                        h0, h1 = QK_PARTS[what[1]]
                        transposed_dve(dve, AT2, qk_fill[what[1]], h1 - h0, qkT[:, h0 // 2:h1 // 2, :].rearrange("p c n -> p (c n)"), l, what[2])
                    elif what[0] == "T":
                        probs_dve(dve, ch, AT2, what[1], what[2], l)
                    elif what[0] == "O":
                        heads_parts(nc.vector, AT2, what[1].fill + what[1].copies, l, range(EARLY))
                    elif what[0] == "V":
                        heads_dve(dve, ch, AT2, what[1], l)
                merge_dve(dve, ch, AT2, fill_o2, G_LAYER + LG_BR, 2, (gates_on, l + 2), l, at)
                for g in range(WO):
                    los(LG_WO + g)
                    dve.wait_ge(half_done, at.halves + L_HALF + 2 * LG_WO + wo_done(g))
                    dst = X[:, :, g * GC:(g + 1) * GC]
                    ins = nc.vector.tensor_tensor(dst, dst, bank(6 + g % 2).rearrange("p (t n) -> p t n", t=TT), ALU.add)
                    ins.then_inc(wo_taken if g < WO - 1 else x_ready, 1)
                dve.wait_ge(x_ready, l * 3 + 2 * TT + 1)
                norm_dve_pre(dve, n_peer, l, None, PAR[:, Q_GF:Q_GF + D], split=l * TT + 2 * TT)

                def route(k, b):
                    rc = Chain(dve, route_step)

                    def top16(vals, best, where):
                        rc.link(nc.vector.max(best[:, 0:8], vals))
                        rc.link(nc.vector.max_index(where[:, 0:8], best[:, 0:8], vals))
                        rc.link(nc.vector.match_replace(vals, best[:, 0:8], vals, LOWEST))
                        rc.link(nc.vector.max(best[:, 8:16], vals))
                        rc.step(nc.vector.max_index(where[:, 8:16], best[:, 8:16], vals))

                    def first_keys():
                        rc.link(nc.vector.tensor_copy(keys, SC[:, bass.ds(k, 1), :, :].rearrange("p a s n -> p (a s) n")))
                        top16(keys[:, 0, :], sv[:, 0, :], si[:, 0, :])

                    def second_keys():
                        top16(keys[:, 1, :], sv[:, 1, :], si[:, 1, :])

                    def pairs():
                        rc.sync()
                        rc.step(nc.vector.tensor_copy(siF, si))
                        rc.link(nc.vector.tensor_tensor(cand.rearrange("p (a b) -> p a b", a=TOPK), view(sv[:, 0, :], [1, TOPK], [0, TOPK]),
                                                        view(sv[:, 1, :], [0, TOPK], [1, TOPK]), ALU.add))
                        top16(cand, topv, sel[:, 0, :])
                        nc.vector.tensor_scalar(topneg, topv[:, 0:1], -1.0, None, ALU.mult).then_inc(topd_ready, 1)

                    def indices():
                        rc.sync()
                        rc.step(nc.vector.tensor_scalar(sel[:, 1, :], sel[:, 0, :], 4, None, ALU.logical_shift_right))
                        rc.link(nc.vector.tensor_scalar(sel[:, 2, :], sel[:, 0, :], TOPK - 1, None, ALU.bitwise_and))
                        rc.link(nc.vector.tensor_copy(abF, sel[:, 1:3, :]))
                        both = tuple((j, eq, eq.rearrange("p (k a) -> p k a", a=TOPK)) for j, eq in enumerate((eqA, eqB)))
                        for j, eq, eq3 in both:
                            rc.step(nc.vector.tensor_tensor(eq3, view(abF[:, j, :], [1, TOPK], [0, TOPK]), view(iota16, [0, TOPK], [1, TOPK]), ALU.is_equal))
                        rc.sync()
                        for j, eq, eq3 in both:
                            rc.step(nc.vector.tensor_tensor(eq3, eq3, view(siF[:, j, :], [0, TOPK], [1, TOPK]), ALU.mult))
                        rc.sync()
                        for j, eq, eq3 in both:
                            rc.step(nc.vector.tensor_reduce(eF[:, j, :], eq3, AX.X, ALU.add))
                        rc.sync()
                        rc.link(nc.vector.scalar_tensor_tensor(out=eF[:, 0, :], in0=eF[:, 0, :], scalar=float(NKEY), in1=eF[:, 1, :],
                                                               op0=ALU.mult, op1=ALU.add))
                        nc.vector.tensor_scalar(EIDX[:, b, :], eF[:, 0, :], lbase, None, ALU.add).then_inc(routed, 1)

                    def gates():
                        dve.wait_ge(texp_ready, l * ROUTES + k + 1)
                        rc.link(nc.vector.reciprocal(ersum, esum))
                        nc.vector.tensor_scalar(GWT[:, b, :], topv, ersum, None, ALU.mult).then_inc(gates_ready, 1)
                        rc.restart()

                    return first_keys, second_keys, pairs, indices, gates

                ch.step(nc.vector.memset(SC[:, STEPS, :, :], 0.0))
                split_lo(dve, L_HALF + 2 * LG_PQ + SLOTS, at)
                wait_alone(dve, sc_ready, l * PH + 1, dve_passed)
                nxt = 2 * LG_PQ + SLOTS + 1
                for part, halves in zip(route(0, 0), (1, 2, 2, 3, L_HALVES)):
                    part()
                    for n in range(nxt, min(nxt + halves, L_HALVES)):
                        split_lo(dve, L_HALF + n, at)
                    nxt += halves
                for t in range(TT):
                    with dve.Fori(0, PH // 2) as i:
                        for b in range(2):
                            k = i * 2 + (t * PH + b)
                            for c in range(PASSES):
                                use = l * USES + i * (2 * PASSES) + (t * PH * PASSES + b * PASSES + c)

                                def dots(q):
                                    for r in range(q * SET, (q + 1) * SET):
                                        dve.wait_ge(g_landed[r], use * 16 + 16)
                                        ins = nc.vector.tensor_tensor_reduce(ring[:, r, 0:D], HN[:, t, :], ring[:, r, 0:D], 1.0, 0.0,
                                                                             ALU.mult, ALU.add, hd[:, r:r + 1])
                                    ins.then_inc(dots_ready, 1)

                                def weights(q):
                                    dve.wait_ge(gelu_ready, use * SETS + q + 1)
                                    nc.vector.tensor_tensor(gw8[:, q * SET:(q + 1) * SET], ga[:, q * SET:(q + 1) * SET],
                                                            GWT[:, b, c * RING + q * SET:c * RING + (q + 1) * SET], ALU.mult).then_inc(w_ready, 1)

                                if c == 0:
                                    dve.wait_ge(gates_ready, l * ROUTES + k + 1)
                                    if t == 0:
                                        wait_alone(dve, sc_ready, l * PH + i * 2 + 2 if b == 0 else l * PH + i + 5, dve_passed)
                                    parts = route(k + 1, 1 - b)
                                for q in range(SETS):
                                    dots(q)
                                    if q:
                                        weights(q - 1)
                                    if c == 0:
                                        parts[q]()
                                        if q == SETS - 1:
                                            parts[SETS]()
                                weights(SETS - 1)
                for t in range(TT):
                    dve.wait_ge(acc_ready, l * TT + t + 1)
                    nc.vector.tensor_tensor(X[:, t, :], X[:, t, :], ps[:, 2 * t * 512:(2 * t + 2) * 512], ALU.add).then_inc(x_ready, 1)
                ch.sync()
                nc.vector.tensor_scalar(lbase, lbase, float(EXPERTS), None, ALU.add).then_inc(dve_step, 1)
                ch.n += 1
                ch.restart()


def t5_bucket(dist):
    exact = NB_BUCKETS // 2
    nf = np.maximum(dist, 1).astype(np.float32)
    large = exact + (np.log(nf / np.float32(exact)) / np.float32(np.log(2048 / exact)) * np.float32(NB_BUCKETS - exact)).astype(np.int32)
    return np.where(dist < exact, dist, np.minimum(large, NB_BUCKETS - 1))


def shape_constants():
    f = np.float32
    c = np.zeros((P, C_END), f)
    c[:, C_ID:C_ID + P] = np.eye(P, dtype=f)
    c[:, C_TURN:C_TURN + P] = np.eye(P, dtype=f)[::-1]
    q = np.arange(P)
    b = np.ones((P, S), f)
    b[:, P:] = q[None, :] < q[:, None]
    c[:, C_BM:C_BM + S] = b
    c[:, C_NB:C_NB + S] = 1 - b
    col = q % GRID_W
    cs = np.clip(col - 8, 0, GRID_W - 16)
    kc = np.arange(GRID_W)
    c[:, C_NA:C_NA + GRID_W] = np.where((kc[None] >= cs[:, None]) & (kc[None] < cs[:, None] + 16), 0, NEG)
    inv = f(10000.0) ** (-np.arange(32, dtype=f) / f(32))
    for t in range(TT):
        pos = q + t * P
        c[:, C_SW + t * S:C_SW + (t + 1) * S] = np.where(np.abs(pos[:, None] - np.arange(S)[None]) <= 128, 0, NEG)
        ang = pos.astype(f)[:, None] * inv[None]
        c[:, C_COS + t * 32:C_COS + (t + 1) * 32] = np.cos(ang)
        c[:, C_SIN + t * 32:C_SIN + (t + 1) * 32] = np.sin(ang)
    c[:, C_IOTA:C_IOTA + TOPK] = np.arange(TOPK, dtype=f)
    oh = np.zeros((NB_BUCKETS + 1, VAR, EW), f)
    for v, (step, limit) in enumerate(((1, 128), (4, 512), (16, 2048), (1, 127))):
        for x in range(EW):
            dist = S - 1 - x
            ok = 0 <= dist <= limit and dist % step == 0
            oh[int(t5_bucket(np.array(dist))) if ok else NB_BUCKETS, v, x] = 1
    return c, oh.reshape(NB_BUCKETS + 1, VAR * EW)


def pack(w, tok=()):
    n = w.shape[1] // GC
    w = w.reshape(KC, P, n, GC)
    by_features = w.reshape(KC, P, n, 2, P).transpose(2, 3, 1, 0, 4).reshape(n, 2, P, HW)
    by_chunks = w.reshape(2, HC, P, n, GC).transpose(3, 0, 2, 1, 4).reshape(n, 2, P, HW)
    return np.stack([(by_chunks if g in tok else by_features)[g] for g in range(n)]).reshape(2 * n, P, HW)


def by_feature(v):
    return v.reshape(-1, P).T


def rows_on_all(v):
    return np.broadcast_to(v.reshape(1, -1), (P, v.size))


def lay_out(i):
    cat = np.concatenate
    pairs = [0, 4, 1, 5, 2, 6, 3, 7]
    w = i["w_in"][0]
    bq = w[:, 2304:2816].reshape(D, 8, HD)[:, pairs].reshape(D, 512)
    w = cat([w[:, :2304], bq, w[:, 2816:]], 1)
    groups = [pack(w, TOK_1), pack(cat([i["w_br_a"][0], i["w_br_b"][0], i["w_br_c"][0]], 0)), pack(i["w_out"][0], range(WO))[WO_HALVES]]
    up = pack(i["w_up"][0].reshape(D, 2, FF_BLOCKS, P).transpose(0, 2, 1, 3).reshape(D, 2 * FF_BLOCKS * P))
    dn = i["w_down"][0].reshape(FF_BLOCKS, P, D)
    ff = [up[0:4]]
    for k in range(1, FF_BLOCKS // 2):
        ff += [up[4 * k:4 * k + 4], dn[2 * k - 2:2 * k]]
    groups += ff + [dn[-2:]]
    par2, rpb = [], []
    for l in range(LAYERS):
        w = i["w_in_2"][l]
        qb = w[:, 1536:2048].reshape(D, 8, HD)[:, pairs].reshape(D, 512)
        w = cat([w[:, 0:1024], qb, w[:, 2048:2304], w[:, 1024:1536], w[:, 2304:]], 1)
        groups += [pack(w, range(L_PROJ)), pack(cat([i["w_branch_na_2"][l], i["w_branch_swa_2"][l]], 0)), pack(i["w_out_2"][l], range(WO))[WO_HALVES],
                   pack(i["peer_query_2"][l])]
        n = i["qk_norm_2"][l]
        qkn = cat([np.broadcast_to(n[j], (c, HD)).reshape(-1) for j, c in ((0, 8), (1, 8), (2, 8), (3, 2))])
        par2.append(cat([by_feature(i["norm_mix_2"][l]), by_feature(i["gate_bias_2"][l].reshape(-1)), rows_on_all(i["swa_sink_2"][l]),
                         rows_on_all(qkn), rows_on_all(i["norm_ffn_2"][l]),
                         i["peer_sub_keys_2"][l].transpose(2, 0, 1).reshape(P, 2 * NKEY)], 1))
        padded = np.pad(i["na_rpb_2"][l], ((0, 0), (0, 0), (GRID_W - 16, GRID_W - 16)))
        rpb.append(np.broadcast_to(padded[:, :, None, :], (NQ, RPB_R, GRID_W, RPB_PAD)))
    cw = i["conv_w"][0].reshape(3, 2, FF_BLOCKS, P)
    cb = i["conv_b"][0].reshape(1, 2, FF_BLOCKS, P)
    taps = cat([cw, cb], 0).transpose(3, 2, 1, 0).reshape(P, FF_BLOCKS * 8)
    par1 = cat([by_feature(i["attn_pre_norm"][0]), by_feature(i["ffn_pre_norm"][0]), by_feature(i["b_gate"][0].reshape(-1)), taps,
                rows_on_all(i["sinks"][0]), rows_on_all(i["attn_post_norm"][0]), rows_on_all(i["ffn_post_norm"][0])], 1)
    consts, onehot = shape_constants()
    return {
        "x": i["x"][0], "wstream": cat(groups, 0), "consts": consts, "onehot": onehot,
        "relb": np.pad(i["rel_bias"], ((0, 1), (0, 0)), constant_values=NEG),
        "par1": par1, "par2": np.stack(par2), "rpb": np.stack(rpb),
        "experts": cat([i["peer_down_2"].reshape(-1, D), i["peer_up_2"].reshape(-1, D)], 1),
    }


def kernel(**inputs):
    import concourse.bacc as bacc
    from concourse.bass_utils import run_bass_kernel_spmd as run

    nc = bacc.Bacc("TRN2", target_bir_lowering=False, num_devices=1)
    laid = lay_out({k: np.asarray(v) for k, v in inputs.items()})
    arrays, args = {}, []
    for name, a in laid.items():
        arrays["in_" + name] = np.ascontiguousarray(a, dtype=np.float32)
        args.append(nc.dram_tensor("in_" + name, a.shape, F32, kind="ExternalInput").ap())
    result = nc.dram_tensor("result", (S, D), F32, kind="ExternalOutput").ap()
    build(nc, *args, result)
    return run(nc, [arrays], core_ids=[0]).results[0]["result"].reshape(1, S, D)
```
